# Optimizing a Trainium2 kernel written in Bass

```python
import jax, jax.numpy as jnp
from jax import lax
import numpy as np

D_MODEL = 1024
BATCH = 1
SEQ = 512
DEPTH = 2
DEC_BATCH = 1
DEC_SEQ = 64
PAST_LEN = 1024

CHUNK = 64
N_PREV_CHUNKS = 8
N_BAND = N_PREV_CHUNKS + 1
BAND_ROWS = N_PREV_CHUNKS * CHUNK
D_MIX = D_MODEL
HEADS_A = 8
HEAD_DIM_A = 64
WIDTH_A = HEADS_A * HEAD_DIM_A
HEADS_R = 4
HEAD_DIM_R = 128
WIDTH_R = HEADS_R * HEAD_DIM_R
N_PROJ = 3 * WIDTH_A + 4 * WIDTH_R
REL_CLIP = 2 * CHUNK
D_FF = -(-8 * D_MODEL // (3 * 256)) * 256
ROPE_BASE = 10000.0
RMS_EPS = 1e-6
GN_EPS = 1e-5
NEG_INF = -1e30

kernel_name = "hybrid_band_attn_retention_stream_step"

def rms_norm(x, g):
    xf = x.astype(jnp.float32)
    y = xf * lax.rsqrt(jnp.mean(xf * xf, axis=-1, keepdims=True) + RMS_EPS)
    return (y * g.astype(jnp.float32)).astype(x.dtype)

def rope(x, pos):
    half = x.shape[-1] // 2
    inv = ROPE_BASE ** (-jnp.arange(half, dtype=jnp.float32) / half)
    ang = pos[..., None] * inv
    cos, sin = jnp.cos(ang), jnp.sin(ang)
    xf = x.astype(jnp.float32)
    x1, x2 = xf[..., :half], xf[..., half:]
    return jnp.concatenate([x1 * cos - x2 * sin, x1 * sin + x2 * cos], axis=-1).astype(x.dtype)

def rebase_state(S, shift):
    St = jnp.swapaxes(S, -1, -2)
    return jnp.swapaxes(rope(St, jnp.asarray(shift, dtype=jnp.float32)), -1, -2)

def rel_bias(rel_table, q_rel, k_rel):
    dist = q_rel[:, None] - k_rel[None, :]
    idx = jnp.clip(dist, -REL_CLIP, REL_CLIP) + REL_CLIP
    return rel_table[:, idx].astype(jnp.float32)

def retention_log_gamma():
    return jnp.log(1.0 - 2.0 ** (-5.0 - jnp.arange(HEADS_R, dtype=jnp.float32)))

def retention_block(q, k, v, S, log_gamma):
    L = q.shape[1]
    idx = jnp.arange(L, dtype=jnp.float32)
    diff = idx[:, None] - idx[None, :]
    decay = jnp.where(diff[None] >= 0,
                      jnp.exp(jnp.maximum(diff, 0.0)[None] * log_gamma[:, None, None]), 0.0)
    scores = jnp.einsum("blhd,bmhd->bhlm", q, k) * decay[None]
    intra = jnp.einsum("bhlm,bmhe->blhe", scores, v)
    q_decay = jnp.exp((idx + 1.0)[:, None] * log_gamma[None, :])
    cross = jnp.einsum("blhd,bhde->blhe", q, S) * q_decay[None, :, :, None]
    k_decay = jnp.exp((L - 1.0 - idx)[:, None] * log_gamma[None, :])
    S_new = (jnp.exp(L * log_gamma)[None, :, None, None] * S
             + jnp.einsum("blhd,blhe->bhde", k * k_decay[None, :, :, None], v))
    return intra + cross, S_new

def project(x, g_mix, w_in, q_norm, k_norm):
    B, L, _ = x.shape
    z = rms_norm(x, g_mix) @ w_in
    cuts = [WIDTH_A, 2 * WIDTH_A, 3 * WIDTH_A, 3 * WIDTH_A + WIDTH_R,
            3 * WIDTH_A + 2 * WIDTH_R, 3 * WIDTH_A + 3 * WIDTH_R]
    qa, ka, va, qr, kr, vr, gr = jnp.split(z, cuts, axis=-1)
    qa = rms_norm(qa.reshape(B, L, HEADS_A, HEAD_DIM_A), q_norm)
    ka = rms_norm(ka.reshape(B, L, HEADS_A, HEAD_DIM_A), k_norm)
    va = va.reshape(B, L, HEADS_A, HEAD_DIM_A)
    qr = qr.reshape(B, L, HEADS_R, HEAD_DIM_R)
    kr = kr.reshape(B, L, HEADS_R, HEAD_DIM_R)
    vr = vr.reshape(B, L, HEADS_R, HEAD_DIM_R)
    return qa, ka, va, qr, kr, vr, gr

def band_attention_prompt(q, k, v, rel_table):
    B, S = q.shape[0], q.shape[1]
    NC = S // CHUNK
    qc = q.reshape(B, NC, CHUNK, HEADS_A, HEAD_DIM_A)
    pad = ((0, 0), (N_PREV_CHUNKS, 0), (0, 0), (0, 0), (0, 0))
    band = jnp.arange(NC)[:, None] + jnp.arange(N_BAND)[None, :]
    kb = jnp.pad(k.reshape(B, NC, CHUNK, HEADS_A, HEAD_DIM_A), pad)[:, band]
    vb = jnp.pad(v.reshape(B, NC, CHUNK, HEADS_A, HEAD_DIM_A), pad)[:, band]
    kb = kb.reshape(B, NC, N_BAND * CHUNK, HEADS_A, HEAD_DIM_A)
    vb = vb.reshape(B, NC, N_BAND * CHUNK, HEADS_A, HEAD_DIM_A)
    k_rel = jnp.arange(N_BAND * CHUNK) - BAND_ROWS
    bias = rel_bias(rel_table, jnp.arange(CHUNK), k_rel)
    valid = jnp.repeat(band >= N_PREV_CHUNKS, CHUNK, axis=1)
    logits = jnp.einsum("bnqhd,bnkhd->bnhqk", qc, kb).astype(jnp.float32) * (HEAD_DIM_A ** -0.5) + bias
    logits = jnp.where(valid[None, :, None, None, :], logits, NEG_INF)
    p = jax.nn.softmax(logits, axis=-1).astype(v.dtype)
    o = jnp.einsum("bnhqk,bnkhd->bnqhd", p, vb)
    return o.reshape(B, S, WIDTH_A)

def band_attention_sample(q, k, v, cache_k, cache_v, rel_table):
    B, L = q.shape[0], q.shape[1]
    R = cache_k.shape[1]
    kk = jnp.concatenate([cache_k.astype(k.dtype), k], axis=1)
    vv = jnp.concatenate([cache_v.astype(v.dtype), v], axis=1)
    k_rel = jnp.concatenate([jnp.arange(R) - R, jnp.arange(L)])
    bias = rel_bias(rel_table, jnp.arange(L), k_rel)
    logits = jnp.einsum("bqhd,bkhd->bhqk", q, kk).astype(jnp.float32) * (HEAD_DIM_A ** -0.5) + bias
    p = jax.nn.softmax(logits, axis=-1).astype(v.dtype)
    return jnp.einsum("bhqk,bkhd->bqhd", p, vv).reshape(B, L, WIDTH_A)

def retention_prompt(q, k, v):
    B, S = q.shape[0], q.shape[1]
    NC = S // CHUNK
    pos = jnp.arange(S, dtype=jnp.float32)[:, None]
    q = rope(q, pos).astype(jnp.float32)
    k = rope(k, pos).astype(jnp.float32) * (HEAD_DIM_R ** -0.5)
    v = v.astype(jnp.float32)
    to_chunks = lambda t: t.reshape(B, NC, CHUNK, HEADS_R, HEAD_DIM_R).transpose(1, 0, 2, 3, 4)
    log_gamma = retention_log_gamma()

    def step(S_c, inp):
        qc, kc, vc = inp
        o_c, S_n = retention_block(qc, kc, vc, S_c, log_gamma)
        return S_n, o_c

    S0 = jnp.zeros((B, HEADS_R, HEAD_DIM_R, HEAD_DIM_R), jnp.float32)
    S_fin, o = lax.scan(step, S0, (to_chunks(q), to_chunks(k), to_chunks(v)))
    o = o.transpose(1, 0, 2, 3, 4).reshape(B, S, HEADS_R, HEAD_DIM_R)
    return o, rebase_state(S_fin, -S)

def retention_sample(q, k, v, state):
    L = q.shape[1]
    pos = jnp.arange(L, dtype=jnp.float32)[:, None]
    q = rope(q, pos).astype(jnp.float32)
    k = rope(k, pos).astype(jnp.float32) * (HEAD_DIM_R ** -0.5)
    o, S_new = retention_block(q, k, v.astype(jnp.float32), state.astype(jnp.float32), retention_log_gamma())
    return o, rebase_state(S_new, -L)

def merge_and_ffn(x, o_a, o_r, g_r, ret_norm, w_out, g_ffn, w_gate, w_up, w_down):
    B, L, _ = x.shape
    mu = jnp.mean(o_r, axis=-1, keepdims=True)
    var = jnp.mean(jnp.square(o_r - mu), axis=-1, keepdims=True)
    o_r = ((o_r - mu) * lax.rsqrt(var + GN_EPS)).reshape(B, L, WIDTH_R) * ret_norm.astype(jnp.float32)
    o_r = jax.nn.silu(g_r) * o_r.astype(x.dtype)
    x = x + jnp.concatenate([o_a, o_r], axis=-1) @ w_out
    h = rms_norm(x, g_ffn)
    return x + (jax.nn.silu(h @ w_gate) * (h @ w_up)) @ w_down

def setup_inputs(seed: int = 0) -> dict:
    key = jax.random.key(seed)
    ks = jax.random.split(key, 16)
    a_rows = min(BAND_ROWS, PAST_LEN)
    nrm = lambda k, shape, s: jax.random.normal(k, shape, jnp.float32) * s
    return {
        "x_prompt": nrm(ks[0], (BATCH, SEQ, D_MODEL), 1.0),
        "x_sample": nrm(ks[1], (DEC_BATCH, DEC_SEQ, D_MODEL), 1.0),
        "cache_a_k": nrm(ks[2], (DEPTH, DEC_BATCH, a_rows, HEADS_A, HEAD_DIM_A), 1.0),
        "cache_a_v": nrm(ks[3], (DEPTH, DEC_BATCH, a_rows, HEADS_A, HEAD_DIM_A), 1.0),
        "state_ret": nrm(ks[4], (DEPTH, DEC_BATCH, HEADS_R, HEAD_DIM_R, HEAD_DIM_R), 0.5),
        "norm_mix": 1.0 + nrm(ks[5], (DEPTH, D_MODEL), 0.02),
        "w_in": nrm(ks[6], (DEPTH, D_MODEL, N_PROJ), D_MODEL ** -0.5),
        "q_norm": 1.0 + nrm(ks[7], (DEPTH, HEAD_DIM_A), 0.02),
        "k_norm": 1.0 + nrm(ks[8], (DEPTH, HEAD_DIM_A), 0.02),
        "rel_table": nrm(ks[9], (DEPTH, HEADS_A, 2 * REL_CLIP + 1), 0.1),
        "ret_norm": 1.0 + nrm(ks[10], (DEPTH, WIDTH_R), 0.02),
        "w_out": nrm(ks[11], (DEPTH, D_MIX, D_MODEL), D_MIX ** -0.5),
        "norm_ffn": 1.0 + nrm(ks[12], (DEPTH, D_MODEL), 0.02),
        "w_gate": nrm(ks[13], (DEPTH, D_MODEL, D_FF), D_MODEL ** -0.5),
        "w_up": nrm(ks[14], (DEPTH, D_MODEL, D_FF), D_MODEL ** -0.5),
        "w_down": nrm(ks[15], (DEPTH, D_FF, D_MODEL), D_FF ** -0.5),
    }

def reference(x_prompt, x_sample, cache_a_k, cache_a_v, state_ret, norm_mix, w_in, q_norm, k_norm,
              rel_table, ret_norm, w_out, norm_ffn, w_gate, w_up, w_down):
    xp, xs = x_prompt, x_sample
    rows_p = min(BAND_ROWS, x_prompt.shape[1])
    kp_rows, vp_rows, sp_list, ks_rows, vs_rows, ss_list = [], [], [], [], [], []
    for l in range(DEPTH):
        qa, ka, va, qr, kr, vr, gr = project(xp, norm_mix[l], w_in[l], q_norm[l], k_norm[l])
        o_a = band_attention_prompt(qa, ka, va, rel_table[l])
        o_r, S_p = retention_prompt(qr, kr, vr)
        xp = merge_and_ffn(xp, o_a, o_r, gr, ret_norm[l], w_out[l], norm_ffn[l], w_gate[l], w_up[l], w_down[l])
        kp_rows.append(ka[:, -rows_p:])
        vp_rows.append(va[:, -rows_p:])
        sp_list.append(S_p)
        qa, ka, va, qr, kr, vr, gr = project(xs, norm_mix[l], w_in[l], q_norm[l], k_norm[l])
        o_a = band_attention_sample(qa, ka, va, cache_a_k[l], cache_a_v[l], rel_table[l])
        o_r, S_s = retention_sample(qr, kr, vr, state_ret[l])
        xs = merge_and_ffn(xs, o_a, o_r, gr, ret_norm[l], w_out[l], norm_ffn[l], w_gate[l], w_up[l], w_down[l])
        ks_rows.append(ka)
        vs_rows.append(va)
        ss_list.append(S_s)
    return (xp, xs,
            jnp.stack(kp_rows), jnp.stack(vp_rows), jnp.stack(sp_list),
            jnp.stack(ks_rows), jnp.stack(vs_rows), jnp.stack(ss_list))


_drawn_inputs = setup_inputs


def setup_inputs(seed=0):
    import zlib

    import numpy as np

    out = dict(_drawn_inputs(seed))
    spreads = {}
    factors = {'q_norm': 8.0,
     'k_norm': 2.693,
     'rel_table': 4.834,
     'ret_norm': 4.476,
     'norm_ffn': 2.759,
     'cache_a_k': 8.0,
     'cache_a_v': 8.0}
    for name, (base, spread) in spreads.items():
        noise = np.random.default_rng([zlib.crc32(name.encode()), seed]).standard_normal(out[name].shape)
        drawn = base * np.exp(spread * noise) if base else spread * noise
        out[name] = __import__('jax').numpy.asarray(drawn.astype(out[name].dtype))
    for name, factor in factors.items():
        out[name] = (out[name] * factor).astype(out[name].dtype)
    return out
```

```python
import concourse.bass as bass
from concourse import mybir
from contextlib import ExitStack

F32 = mybir.dt.float32
F32R = mybir.dt.float32r
ALU = mybir.AluOpType
ACT = mybir.ActivationFunctionType

P = 128
DEPTH = 2
D = 1024
KD = D // P
SEQ, DEC, PAST = 512, 64, 1024
TOK = SEQ + DEC
HALF = TOK // 2
QT = SEQ // P
TT = QT + 1
HA, DA = 8, 64
HR, DR = 4, 128
WA, WR = HA * DA, HR * DR
CHUNK = 64
REL = 128
DFF = 2816
GROUPS = 2
FT = DFF // P // GROUPS
U_IN = (3 * WA + 4 * WR) // P
U_OUT = D // P
U_GROUP = 2 * FT + U_OUT
U_LAYER = U_IN + U_OUT + GROUPS * U_GROUP
RING = 2
STRIP = 5 * P
LINE = STRIP + P - 1
GAINS = 2 * KD + 2 + WR // P
EV = RING + KD
RMS_EPS, GN_EPS = 1e-6, 1e-5
MASKED = 1e30

C_ID = 0
C_COS = C_ID + P
C_SIN = C_COS + SEQ
C_QDEC = C_SIN + SEQ
C_KDEC = C_QDEC + HR * DEC
C_ROT = C_KDEC + TT * HR
C_SEL = C_ROT + 4
C_ONE = C_SEL + 2
C_EPS = C_ONE + 1
C_ALL = C_EPS + 2


def gamma(h):
    return 1.0 - 2.0 ** (-5.0 - h)


def tok(t):
    return slice(t * P, t * P + rows(t))


def rows(t):
    return P if t < QT else DEC


def backwards(ap, n):
    dims = [list(d) for d in ap.ap]
    step, count = dims[-1]
    assert count == n
    dims[-1] = [-step, n]
    return bass.AP(tensor=ap.tensor, offset=ap.offset + step * (n - 1), ap=dims)


def build(nc, x_prompt, x_sample, cache_k, cache_v, state_in, norm_mix, w_in, q_norm, k_norm, rel_table,
          ret_norm, w_out, norm_ffn, w_gate, w_up, w_down, const, spread_in, decay,
          y_prompt, y_sample, nk_prompt, nv_prompt, ns_prompt, nk_sample, nv_sample, ns_sample, lines):
    ctx = ExitStack()
    with ctx:
        ROW = TOK * 4
        base = (nc.sbuf_base + 31) // 32 * 32
        A_X = base
        A_MIX = A_X + KD * ROW
        A_SH = A_MIX + 2 * KD * ROW
        A_W = A_SH + 2 * KD * ROW + 2 * FT * ROW
        UNIT = FT * P * 4
        A_MISC = A_W + 3 * RING * UNIT

        def place(name, shape, dt, at):
            return nc.alloc_sbuf_tensor_at(name, shape, dt, offset=at)

        nc.alloc_sbuf_tensor("arena", [P, (A_MISC - base) // 4], F32)
        x = place("x", [P, KD, TOK], F32, A_X)
        mix = place("mix", [P, KD, 2, TOK], F32R, A_MIX)
        A_KV = A_MIX + KD * ROW
        kc_tok = place("kc_tok", [P, RING, QT, P], F32, A_KV)
        vc_tok = place("vc_tok", [P, RING, QT, P], F32, A_KV + RING * 2048)
        kc_t = place("kc_t", [P, RING, SEQ], F32, A_KV + 2 * RING * 2048)
        qk = place("qk", [P, 2 * WA // P, TOK], F32, A_SH)
        q_rev = place("q_rev", [P, WA // P, TOK], F32, A_SH + 8 * ROW)
        vt = place("vt", [P, 4, TOK], F32, A_SH + 12 * ROW)
        qk_ret = place("qk_ret", [P, 8, TOK], F32, A_SH + 16 * ROW)
        A_T = A_SH + 24 * ROW
        va = place("va", [P, TT, WA], F32, A_T)
        vr = place("vr", [P, TT, WR], F32, A_T + TT * WA * 4)
        A_S2 = A_T + 2 * TT * WA * 4
        strip = place("strip", [P, RING, STRIP], F32, A_S2)
        dmask = place("dmask", [P, RING, SEQ], F32, A_S2 + RING * STRIP * 4)
        s_in = place("s_in", [P, HR, DR], F32, A_S2 + RING * STRIP * 4 + RING * SEQ * 4)
        assert A_S2 + RING * STRIP * 4 + RING * SEQ * 4 + HR * DR * 4 <= A_W
        kd_tok = place("kd_tok", [P, RING, TT, P], F32, A_SH)
        st_tmp = place("st_tmp", [P, 2, DR], F32, A_SH + 5120)
        st_swap = place("st_swap", [P, 2, DR], F32, A_SH + 6144)
        st_out = place("st_out", [P, RING, 2, DR], F32, A_SH + 7168)
        stage = place("stage", [P, TT, D], F32, A_SH)
        ffn = place("ffn", [P, KD, 2, TOK], F32R, A_SH)
        act = place("act", [P, FT, 2, TOK], F32R, A_SH + 2 * KD * ROW)
        ffn_sq = place("ffn_sq", [P, KD, TOK], F32, A_SH + 2 * KD * ROW)
        mix_sq = qk_ret
        w_raw = place("w_raw", [P, RING, FT, P], F32, A_W)
        w_hi = place("w_hi", [P, RING, FT, P], F32R, A_W + RING * UNIT)
        w_lo = place("w_lo", [P, RING, FT, P], F32R, A_W + 2 * RING * UNIT)

        def sb(name, shape, dt=F32):
            return ctx.enter_context(nc.sbuf_tensor(name, shape, dt))

        cst = sb("cst", [P, C_ALL])
        row_f = sb("row_f", [P, TOK])
        rcos = sb("rcos", [P, TOK])
        rsin = sb("rsin", [P, TOK])
        work = sb("work", [P, 3, TOK])
        pt = sb("pt", [P, RING, SEQ])
        o_tok = sb("o_tok", [P, RING, TT, P])
        qd = sb("qd", [P, RING, DEC])
        spread = sb("spread", [16, KD * P])
        qk_col = work[0:16, 2, :]
        gain_rows = pt[0:DEPTH * GAINS, 0, 0:P]
        gains = sb("gains", [P, DEPTH, GAINS])
        gain = sb("gain", [P, GAINS])
        root = sb("root", [P, TT])
        inv = sb("inv", [P, TT])
        qroot = sb("qroot", [P, TT, 16])
        qinv = sb("qinv", [P, TT, 16])
        least = sb("least", [P, 4])
        sums = sb("sums", [P, RING, TT])
        rsum = sb("rsum", [P, RING, TT])
        bn = sb("bn", [P, TT, 6])
        mv = sb("mv", [P, TT, 2])
        gnr = sb("gnr", [P, TT])
        gni = sb("gni", [P, TT])

        ps = ctx.enter_context(nc.psum_tensor("ps", [P, 8, 512], F32))

        def sem(name):
            return ctx.enter_context(nc.semaphore(name))

        raw_loaded = [sem(f"raw_loaded{s}") for s in range(RING)]
        hi_done, lo_done, w_used, evacuated = sem("hi_done"), sem("lo_done"), sem("w_used"), sem("evacuated")
        const_in, x_in, gains_in, gains_ps, gains_set, gain_cur = (sem(n) for n in (
            "const_in", "x_in", "gains_in", "gains_ps", "gains_set", "gain_cur"))
        rel_in, line_made, line_out = sem("rel_in"), sem("line_made"), sem("line_out")
        x_ps = sem("x_ps")
        h_hi, h_lo, sq_done = sem("h_hi"), sem("h_lo"), sem("sq_done")
        rms_stat, rms_root, rms_inv, rms_bcast, rms_row = (sem(n) for n in (
            "rms_stat", "rms_root", "rms_inv", "rms_bcast", "rms_row"))
        rope_rows = sem("rope_rows")
        qk_stat, qk_root, qk_inv, qk_bcast, qk_normed = (sem(n) for n in (
            "qk_stat", "qk_root", "qk_inv", "qk_bcast", "qk_normed"))
        qk_cols_ps, qk_cols = sem("qk_cols_ps"), sem("qk_cols")
        ret_ready, tok_ps, tok_evac, g_silu = (sem(n) for n in ("ret_ready", "tok_ps", "tok_evac", "g_silu"))
        ka_out, va_out = sem("ka_out"), sem("va_out")
        strip_loaded = [sem(f"strip_loaded{s}") for s in range(RING)]
        strip_masked = sem("strip_masked")
        kv_loaded = [sem(f"kv_loaded{s}") for s in range(RING)]
        kct_ps, kct_evac = sem("kct_ps"), sem("kct_evac")
        s_ps, biased, exped, pt_ps, pt_evac, pv_done = (sem(n) for n in (
            "s_ps", "biased", "exped", "pt_ps", "pt_evac", "pv_done"))
        sums_inv, o_normed, ot_ps, ot_hi, ot_lo = (sem(n) for n in (
            "sums_inv", "o_normed", "ot_ps", "ot_hi", "ot_lo"))
        dmask_loaded = [sem(f"dmask_loaded{s}") for s in range(RING)]
        state_loaded = sem("state_loaded")
        kd_ps, kd_evac, r_ps, decayed, sv_done, qd_ready = (sem(n) for n in (
            "kd_ps", "kd_evac", "r_ps", "decayed", "sv_done", "qd_ready"))
        bn_parts, bn_done, gn_root, gn_inv, gn_normed, or_ps, or_done, or_hi, or_lo = (sem(n) for n in (
            "bn_parts", "bn_done", "gn_root", "gn_inv", "gn_normed", "or_ps", "or_done", "or_hi", "or_lo"))
        st_ps, st_sum, st_swapped, st_done = (sem(n) for n in ("st_ps", "st_sum", "st_swapped", "st_done"))
        st_stored = [sem(f"st_stored{s}") for s in range(RING)]
        gate_silu, act_f, act_hi, act_lo = (sem(n) for n in ("gate_silu", "act_f", "act_hi", "act_lo"))
        passed = {e.engine: sem(f"passed_{i}") for i, e in enumerate((nc.gpsimd, nc.scalar, nc.vector, nc.tensor))}
        y_ps, y_copied, y_out = sem("y_ps"), sem("y_copied"), sem("y_out")

        block = ctx.enter_context(nc.Block())

        ident = cst[:, C_ID:C_ID + P]
        cos, sin = cst[:, C_COS:C_COS + SEQ], cst[:, C_SIN:C_SIN + SEQ]

        def dense(s):
            return ps[:, 2 * s:2 * s + 2, 0:HALF]

        def halves(ap):
            return ap.rearrange("p (a b) -> p a b", a=2)

        def head_rows(h):
            return slice(DA * (h % 2), DA * (h % 2) + DA)

        def x_count(l, which):
            return U_LAYER * l + (RING if which == 0 else U_IN + EV)

        def wait_apart(eng, *waits):
            for semaphore, count in waits:
                eng.wait_ge(semaphore, count)
            eng.sem_inc(passed[eng.engine], 1)

        FIRST_OUT = U_IN
        FIRST_FFN = U_IN + U_OUT
        DOWN = 2 * FT

        ITEMS_A = [(h, t) for h in range(HA) for t in range(TT)]
        ITEMS_R = [(h, t) for h in range(HR) for t in range(TT)]
        NA, NR = len(ITEMS_A), len(ITEMS_R)

        @block.sync
        def _(sp):
            sp.dma_start(stage[:, 0:QT, :], x_prompt[0].rearrange("(t p) d -> p t d", p=P)).then_inc(x_in, 16)
            sp.dma_start(stage[0:DEC, QT, :], x_sample[0]).then_inc(x_in, 16)
            sp.dma_start(cst[:], const).then_inc(const_in, 16)
            sp.dma_start(spread[:], spread_in).then_inc(const_in, 16)

            def load(slot, n, src, k):
                sp.wait_ge(hi_done, n + 1)
                sp.wait_ge(lo_done, n + 1)
                sp.dma_start(w_raw[:, slot, 0:k, :], src).then_inc(raw_loaded[slot], 16)

            with sp.Fori(0, DEPTH) as l:
                with sp.Fori(0, U_IN // 2) as c2:
                    c = 2 * c2
                    for s in range(2):
                        load(s, U_LAYER * l + c + s,
                             w_in[l].rearrange("(k p) n -> p k n", p=P)[:, :, bass.ds((c + s) * P, P)], KD)

                def load_out(c, s):
                    load(s, U_LAYER * l + FIRST_OUT + c + s,
                         w_out[l].rearrange("(k p) n -> p k n", p=P)[:, :, bass.ds((c + s) * P, P)], KD)

                for s in range(2):
                    load_out(0, s)
                sp.wait_ge(tok_evac, 3 * TT * l + TT)
                sp.dma_start(nv_prompt[l, 0].rearrange("(t p) h d -> p t (h d)", p=P), va[:, 0:QT, :]).then_inc(va_out, 16)
                sp.dma_start(nv_sample[l, 0].rearrange("p h d -> p (h d)"), va[0:DEC, QT, :]).then_inc(va_out, 16)
                def load_mask(h):
                    if h >= RING:
                        sp.wait_ge(decayed, NR * l + TT * (h - RING + 1))
                    sp.dma_start(dmask[:, h % RING, :], decay[h]).then_inc(dmask_loaded[h % RING], 16)

                for h in range(RING):
                    load_mask(h)
                for h in range(HR):
                    sp.wait_ge(st_done, HR * l + h + 1)
                    for i, dst in enumerate((ns_prompt, ns_sample)):
                        sp.dma_start(dst[l, 0, h], st_out[:, h % RING, i, :]).then_inc(st_stored[h % RING], 16)
                    if h + RING < HR:
                        load_mask(h + RING)
                with sp.Fori(1, U_OUT // 2) as c2:
                    c = 2 * c2
                    for s in range(2):
                        load_out(c, s)
                with sp.Fori(0, GROUPS) as g:
                    with sp.Fori(0, FT) as f:
                        for s, w in enumerate((w_gate, w_up)):
                            load(s, U_LAYER * l + U_GROUP * g + 2 * f + (FIRST_FFN + s),
                                 w[l].rearrange("(k p) n -> p k n", p=P)[:, :, bass.ds((g * FT + f) * P, P)], KD)
                    with sp.Fori(0, U_OUT // 2) as c2:
                        c = 2 * c2
                        for s in range(2):
                            load(s, U_LAYER * l + U_GROUP * g + c + (FIRST_FFN + DOWN + s),
                                 w_down[l].rearrange("(g k p) n -> g p k n", g=GROUPS, p=P)[g, :, :, bass.ds((c + s) * P, P)], FT)
            sp.wait_ge(y_copied, TT)
            sp.dma_start(y_prompt[0].rearrange("(t p) d -> p t d", p=P), stage[:, 0:QT, :]).then_inc(y_out, 16)
            sp.dma_start(y_sample[0], stage[0:DEC, QT, :]).then_inc(y_out, 16)
            sp.wait_ge(y_out, 32)
            sp.wait_ge(ka_out, 32 * DEPTH)
            sp.wait_ge(va_out, 32 * DEPTH)
            for s in range(RING):
                sp.wait_ge(st_stored[s], 2 * 16 * HR // RING * DEPTH)

        @block.gpsimd
        def _(pool):
            for l in range(DEPTH):
                r = GAINS * l
                pool.dma_start(gain_rows[r:r + KD, :], norm_mix[l].rearrange("(k p) -> k p", p=P)).then_inc(gains_in, 16)
                pool.dma_start(gain_rows[r + KD:r + 2 * KD, :], norm_ffn[l].rearrange("(k p) -> k p", p=P)).then_inc(gains_in, 16)
                for i, src in enumerate((q_norm, k_norm)):
                    for half in range(2):
                        pool.dma_start(gain_rows[r + 2 * KD + i:r + 2 * KD + i + 1, DA * half:DA * half + DA],
                                       src[l:l + 1, :]).then_inc(gains_in, 16)
                pool.dma_start(gain_rows[r + 2 * KD + 2:r + GAINS, :], ret_norm[l].rearrange("(k p) -> k p", p=P)).then_inc(gains_in, 16)
            pool.dma_start(work[0:DEPTH * HA, 2, 0:2 * REL + 1], rel_table.rearrange("l h r -> (l h) r")).then_inc(rel_in, 16)
            pool.wait_ge(line_made, 1)
            pool.dma_start(lines[:, 0:LINE], work[0:DEPTH * HA].rearrange("p a b -> p (a b)")[:, 0:LINE]).then_inc(line_out, 16)
            pool.wait_ge(line_out, 16)
            with pool.Fori(0, DEPTH) as l:
                def load_strip(h):
                    if h >= RING:
                        wait_apart(pool, (biased, NA * l + TT * (h - RING + 1)))
                    window = lines[bass.ds(l * HA + h, 1), 0:STRIP]
                    src = bass.AP(tensor=window.tensor, offset=window.offset, ap=[[1, P], [1, STRIP]])
                    pool.dma_start(strip[:, h % RING, :], src).then_inc(strip_loaded[h % RING], 16)

                def mask_strip(h):
                    wait_apart(pool, (strip_loaded[h % RING], 16 * (HA // RING) * l + 16 * (h // RING + 1)))
                    nc.gpsimd.memset(strip[CHUNK:P, h % RING, STRIP - CHUNK:STRIP], MASKED).then_inc(strip_masked, 1)

                def load_cache(p):
                    if p >= RING:
                        wait_apart(pool, (pv_done, NA * l + 2 * TT * (p - RING + 1)))
                    for dst, src in ((kc_tok, cache_k), (vc_tok, cache_v)):
                        pool.dma_start(dst[:, p % RING, :, :],
                                       src[l, 0, :, 2 * p:2 * p + 2, :].rearrange("(t p) h d -> p t (h d)", p=P)
                                       ).then_inc(kv_loaded[p % RING], 16)

                wait_apart(pool, (w_used, U_LAYER * l + RING))
                for h in range(RING):
                    load_strip(h)
                pool.dma_start(s_in[:], state_in[l, 0].rearrange("h d e -> d h e")).then_inc(state_loaded, 16)
                for h in range(RING):
                    mask_strip(h)
                wait_apart(pool, (tok_evac, 3 * TT * l + 2 * TT))
                pool.dma_start(nk_prompt[l, 0].rearrange("(t p) h d -> p t (h d)", p=P), vr[:, 0:QT, :]).then_inc(ka_out, 16)
                pool.dma_start(nk_sample[l, 0].rearrange("p h d -> p (h d)"), vr[0:DEC, QT, :]).then_inc(ka_out, 16)
                wait_apart(pool, (w_used, U_LAYER * l + U_IN + RING))
                for p in range(RING):
                    load_cache(p)
                for h in range(RING, HA):
                    load_strip(h)
                    mask_strip(h)
                    if h % 2 and h // 2 + 1 < HA // 2:
                        load_cache(h // 2 + 1)

        @block.scalar
        def _(eng):
            def hi(slot, count, n, k):
                eng.wait_ge(raw_loaded[slot], count)
                eng.wait_ge(w_used, n + 1)
                nc.scalar.activation(w_hi[:, slot, 0:k, :], w_raw[:, slot, 0:k, :], ACT.Copy).then_inc(hi_done, 1)

            def norm_in(l, which, dst, k):
                eng.wait_ge(evacuated, x_count(l, which) + k + 1)
                nc.scalar.activation(dst[:, k, 0, :], x[:, k, :], ACT.Copy,
                                     scale=gain[:, which * KD + k:which * KD + k + 1]).then_inc(h_hi, 1)

            def square_in(l, which, sq, k):
                eng.wait_ge(evacuated, x_count(l, which) + k + 1)
                nc.scalar.activation(sq[:, k, :], x[:, k, :], ACT.Square).then_inc(sq_done, 1)

            def rms_sqrt(l, which):
                eng.wait_ge(rms_stat, 2 * l + which + 1)
                nc.scalar.activation(root[:, 0:QT], ps[:, 6, 0:QT], ACT.Sqrt, scale=1.0 / D,
                                     bias=cst[:, C_EPS:C_EPS + 1])
                nc.scalar.activation(root[0:DEC, QT:TT], ps[0:DEC, 6, QT:TT], ACT.Sqrt, scale=1.0 / D,
                                     bias=cst[0:DEC, C_EPS:C_EPS + 1]).then_inc(rms_root, 1)

            def tok_copy(l, group, dst, t):
                eng.wait_ge(tok_ps, 3 * TT * l + TT * group + t + 1)
                nc.scalar.activation(dst[0:rows(t), t, :], ps[0:rows(t), 4 + t % 4, :], ACT.Copy).then_inc(tok_evac, 1)

            eng.sem_inc(hi_done, RING)
            with eng.Fori(0, DEPTH) as l:
                def unit_hi(n, k=KD):
                    hi(n % 2, 16 * (U_LAYER // 2) * l + 16 * (n // 2 + 1), U_LAYER * l + n, k)

                unit_hi(0)
                eng.wait_ge(gain_cur, l + 1)
                for k in range(KD):
                    norm_in(l, 0, mix, k)
                for k in range(KD):
                    square_in(l, 0, mix_sq, k)
                unit_hi(1)
                rms_sqrt(l, 0)
                unit_hi(2)
                for n in range(0, 2):
                    eng.wait_ge(evacuated, U_LAYER * l + n + EV + 1)
                    nc.scalar.activation(mix_sq[:, n, :], qk[:, n, :], ACT.Square).then_inc(sq_done, 1)
                for n in range(2, 8):
                    unit_hi(n + 1)
                    eng.wait_ge(evacuated, U_LAYER * l + n + EV + 1)
                    nc.scalar.activation(mix_sq[:, n, :], qk[:, n, :], ACT.Square).then_inc(sq_done, 1)
                for n in range(8, 12):
                    unit_hi(n + 1)
                eng.wait_ge(qk_stat, l + 1)
                qs = ps[:, 7, 0:TT * 16].rearrange("p (t j) -> p t j", t=TT)
                nc.scalar.activation(qroot[:, 0:QT, :], qs[:, 0:QT, :], ACT.Sqrt, scale=1.0 / DA,
                                     bias=cst[:, C_EPS:C_EPS + 1])
                nc.scalar.activation(qroot[0:DEC, QT, :], qs[0:DEC, QT, :], ACT.Sqrt, scale=1.0 / DA,
                                     bias=cst[0:DEC, C_EPS:C_EPS + 1]).then_inc(qk_root, 1)
                unit_hi(13)
                unit_hi(14)
                for t in range(TT):
                    tok_copy(l, 0, va, t)
                for n in range(15, 25):
                    unit_hi(n)
                for t in range(TT):
                    tok_copy(l, 1, vr, t)
                unit_hi(25)
                eng.wait_ge(ka_out, 32 * l + 32)
                for t in range(TT):
                    tok_copy(l, 2, vr, t)
                for n in range(24, 28):
                    if n > 24:
                        unit_hi(n + 1)
                    eng.wait_ge(evacuated, U_LAYER * l + n + EV + 1)
                    nc.scalar.activation(vt[:, n - 24, :], vt[:, n - 24, :], ACT.Silu).then_inc(g_silu, 1)

                def cache_keys(p):
                    eng.wait_ge(kct_ps, HA // 2 * l + p + 1)
                    nc.scalar.activation(kc_t[:, p % RING, :], ps[:, 0, :], ACT.Copy).then_inc(kct_evac, 1)

                def attn_out_hi(p):
                    eng.wait_ge(ot_ps, HA // 2 * l + p + 1)
                    nc.scalar.activation(mix[:, p, 0, 0:SEQ].rearrange("p (t q) -> p t q", t=QT),
                                         backwards(ps[:, 0, :].rearrange("p (t q) -> p t q", t=QT), P), ACT.Copy)
                    nc.scalar.activation(mix[:, p, 0, SEQ:TOK], backwards(ps[:, 1, 0:DEC], DEC),
                                         ACT.Copy).then_inc(ot_hi, 1)

                cache_keys(0)
                for k in range(NA + 5):
                    if k >= 14 and (k - 14) % 10 == 0:
                        attn_out_hi((k - 14) // 10)
                    if k and k % 10 == 0 and k < NA:
                        cache_keys(k // 10)
                    if k >= NA:
                        continue
                    h, t = ITEMS_A[k]
                    r, w = rows(t), P * (t + 1) if t < QT else TOK
                    if k >= 2 * TT:
                        eng.wait_ge(sums_inv, HA * l + h - 1)
                    eng.wait_ge(biased, NA * l + k + 1)
                    nc.scalar.activation(work[0:r, k % 3, 0:w], work[0:r, k % 3, 0:w], ACT.Exp, scale=-1.0,
                                         bias=least[0:r, k % 4:k % 4 + 1],
                                         accum_out=sums[0:r, h % 2, t:t + 1]).then_inc(exped, 1)
                for h in range(HR + 2):
                    if h < HR:
                        eng.wait_ge(kd_ps, HR * l + h + 1)
                        if h >= RING:
                            eng.wait_ge(st_ps, HR * l + h - 1)
                        for t in range(TT):
                            bank, c = (0, P * t) if t < QT else (1, 0)
                            last = nc.scalar.activation(kd_tok[0:rows(t), h % 2, t, :], ps[0:rows(t), bank, c:c + P], ACT.Copy,
                                                        scale=cst[0:rows(t), C_KDEC + HR * t + h:C_KDEC + HR * t + h + 1])
                        last.then_inc(kd_evac, 1)
                    if 1 <= h <= HR:
                        eng.wait_ge(bn_done, HR * l + h)
                        nc.scalar.activation(gnr[:, 0:QT], mv[:, 0:QT, 1], ACT.Sqrt, bias=cst[:, C_EPS + 1:C_EPS + 2])
                        nc.scalar.activation(gnr[0:DEC, QT:TT], mv[0:DEC, QT:TT, 1], ACT.Sqrt,
                                             bias=cst[0:DEC, C_EPS + 1:C_EPS + 2]).then_inc(gn_root, 1)
                        eng.wait_ge(or_done, HR * l + h)
                        nc.scalar.activation(mix[:, 3 + h, 0, :], pt[:].rearrange("p a b -> p (a b)")[:, 0:TOK],
                                             ACT.Copy).then_inc(or_hi, 1)
                eng.wait_ge(va_out, 32 * l + 32)
                for s in range(RING):
                    eng.wait_ge(st_stored[s], 2 * 16 * HR // RING * l + 2 * 16 * HR // RING)
                for c in range(U_OUT):
                    if c + 1 < U_OUT:
                        unit_hi(FIRST_OUT + c + 1)
                    norm_in(l, 1, ffn, c)
                    square_in(l, 1, ffn_sq, c)
                for g in range(GROUPS):
                    def group_hi(i, s, k=KD):
                        hi(s, 8 * U_LAYER * l + 8 * i + (8 * (FIRST_FFN + U_GROUP * g - s) + 16),
                           U_LAYER * l + i + (FIRST_FFN + U_GROUP * g), k)

                    def silu(f):
                        eng.wait_ge(evacuated, U_LAYER * l + 2 * f + (FIRST_FFN + U_GROUP * g + EV + 1))
                        nc.scalar.activation(work[:, 0, :], work[:, 0, :], ACT.Silu).then_inc(gate_silu, 1)

                    def act_high(f):
                        wait_apart(eng, (act_f, GROUPS * FT * l + f + (FT * g + 1)))
                        nc.scalar.activation(act[:, bass.ds(f, 1), 0, :].rearrange("p a b -> p (a b)"), work[:, 2, :],
                                             ACT.Copy).then_inc(act_hi, 1)

                    def gate_up(f, early=False):
                        if early:
                            group_hi(2 * f + 2, 0)
                        silu(f)
                        if not early:
                            group_hi(2 * f + 2, 0)
                        act_high(f)
                        group_hi(2 * f + 3, 1)

                    if g == 0:
                        group_hi(0, 0)
                        group_hi(1, 1)
                        rms_sqrt(l, 1)
                    gate_up(0, early=g == 0)
                    with eng.Fori(1, FT - 1) as f:
                        gate_up(f)
                    silu(FT - 1)
                    group_hi(DOWN, 0, FT)
                    act_high(FT - 1)
                    group_hi(DOWN + 1, 1, FT)
                    with eng.Fori(1, U_OUT // 2) as c2:
                        c = 2 * c2
                        for s in range(2):
                            group_hi(c + (DOWN + s), s, FT)
                    if g + 1 < GROUPS:
                        group_hi(U_GROUP, 0)
                        group_hi(U_GROUP + 1, 1)
            for t in range(TT):
                eng.wait_ge(y_ps, t + 1)
                nc.scalar.activation(stage[0:rows(t), t, :].rearrange("p (a b) -> p a b", a=2),
                                     ps[0:rows(t), 2 * (t % 2):2 * (t % 2) + 2, :], ACT.Copy).then_inc(y_copied, 1)

        @block.vector
        def _(dve):
            def lo(slot, n, k=KD):
                dve.wait_ge(hi_done, n + RING + 1)
                nc.vector.tensor_tensor(w_lo[:, slot, 0:k, :], w_raw[:, slot, 0:k, :],
                                        w_hi[:, slot, 0:k, :].bitcast(F32), ALU.subtract).then_inc(lo_done, 1)

            def projected(n):
                dve.wait_ge(w_used, n + RING + 1)

            def scaled(n, s, dst):
                projected(n)
                nc.vector.tensor_tensor(halves(dst), dense(s), halves(row_f[:]), ALU.mult).then_inc(evacuated, 1)

            def norm_lo(l, which, dst, k):
                dve.wait_ge(h_hi, 2 * KD * l + which * KD + k + 1)
                nc.vector.scalar_tensor_tensor(dst[:, k, 1, :], x[:, k, :], gain[:, which * KD + k:which * KD + k + 1],
                                               dst[:, k, 0, :].bitcast(F32), ALU.mult, ALU.subtract).then_inc(h_lo, 1)

            def rms_invert(l, which):
                dve.wait_ge(rms_root, 2 * l + which + 1)
                nc.vector.reciprocal(inv[:, 0:QT], root[:, 0:QT])
                nc.vector.reciprocal(inv[0:DEC, QT:TT], root[0:DEC, QT:TT]).then_inc(rms_inv, 1)

            def rms_rows(l, which):
                dve.wait_ge(rms_bcast, 2 * l + which + 1)
                nc.vector.tensor_copy(row_f[:, 0:SEQ], ps[:, 4, :])
                nc.vector.tensor_copy(row_f[:, SEQ:TOK], ps[:, 5, 0:DEC]).then_inc(rms_row, 1)
                dve.wait_ge(rms_row, 2 * l + which + 1)

            dve.sem_inc(lo_done, RING)
            dve.sem_inc(evacuated, RING)
            dve.wait_ge(gains_ps, 1)
            cols = ps[:, 0, 0:DEPTH * GAINS].rearrange("p (l g) -> p l g", l=DEPTH)
            nc.vector.tensor_copy(gains[:], cols).then_inc(gains_set, 1)
            dve.wait_ge(gains_set, 1)
            nc.vector.tensor_scalar(gains[:, :, 2 * KD], cols[:, :, 2 * KD], -(DA ** -0.5), None, ALU.mult).then_inc(gains_set, 1)
            dve.wait_ge(rel_in, 16)
            line = work[0:DEPTH * HA].rearrange("p a b -> p (a b)")
            far = LINE - (2 * REL - 1)
            nc.vector.tensor_scalar(line[:, 0:far], line[:, 2 * TOK + 2 * REL:2 * TOK + 2 * REL + 1].to_broadcast([DEPTH * HA, far]),
                                    -1.0, None, ALU.mult)
            nc.vector.tensor_scalar(line[:, far:LINE], backwards(line[:, 2 * TOK + 1:2 * TOK + 2 * REL], 2 * REL - 1),
                                    -1.0, None, ALU.mult).then_inc(line_made, 1)
            for k in range(KD):
                b = 4 + 2 * (k % 2)
                dve.wait_ge(x_ps, k + 1)
                nc.vector.tensor_copy(x[:, k, 0:SEQ], ps[:, b, :])
                nc.vector.tensor_copy(x[:, k, SEQ:TOK], ps[:, b + 1, 0:DEC]).then_inc(evacuated, 1)
            dve.wait_ge(gains_set, 2)
            dve.wait_ge(line_out, 16)
            with dve.Fori(0, DEPTH) as l:
                def unit_lo(n, k=KD):
                    lo(n % 2, U_LAYER * l + n, k)

                dve.wait_ge(const_in, 32)
                nc.vector.tensor_copy(gain[:], gains[:, bass.ds(l, 1), :].rearrange("p a b -> p (a b)")).then_inc(gain_cur, 1)
                dve.wait_ge(gain_cur, l + 1)
                unit_lo(0)
                for k in range(KD):
                    norm_lo(l, 0, mix, k)
                unit_lo(1)
                rms_invert(l, 0)
                unit_lo(2)
                rms_rows(l, 0)
                for n in range(2):
                    scaled(U_LAYER * l + n, n % 2, qk[:, n, :])
                for dst, table in ((rcos, cos), (rsin, sin)):
                    nc.vector.tensor_tensor(dst[:, 0:SEQ], row_f[:, 0:SEQ], table, ALU.mult)
                    last = nc.vector.tensor_tensor(dst[:, SEQ:TOK], row_f[:, SEQ:TOK], table[:, 0:DEC], ALU.mult)
                last.then_inc(rope_rows, 1)
                for n in range(2, 12):
                    unit_lo(n + 1)
                    scaled(U_LAYER * l + n, n % 2, qk[:, n, :] if n < 8 else vt[:, n - 8, :])
                dve.wait_ge(qk_root, l + 1)
                nc.vector.reciprocal(qinv[:, 0:QT, :], qroot[:, 0:QT, :])
                nc.vector.reciprocal(qinv[0:DEC, QT, :], qroot[0:DEC, QT, :]).then_inc(qk_inv, 1)

                def rotated(n):
                    s = n % 2
                    projected(U_LAYER * l + n)
                    if n > 12:
                        dve.wait_ge(ret_ready, 8 * l + n - 12)
                    nc.vector.tensor_tensor(halves(work[:, 0, :]), dense(s), halves(rcos[:]), ALU.mult)
                    H = P // 2
                    nc.vector.tensor_tensor(halves(work[0:H, 1, :]), ps[H:P, 2 * s:2 * s + 2, 0:HALF], halves(rsin[H:P, :]), ALU.mult)
                    nc.vector.tensor_tensor(halves(work[H:P, 1, :]), ps[0:H, 2 * s:2 * s + 2, 0:HALF], halves(rsin[0:H, :]),
                                            ALU.mult).then_inc(evacuated, 1)
                    dve.wait_ge(evacuated, U_LAYER * l + n + EV + 1)
                    nc.vector.tensor_tensor(qk_ret[:, n - 12, :], work[:, 0, :], work[:, 1, :], ALU.add).then_inc(ret_ready, 1)

                def qk_normalise(j):
                    b = 4 + 2 * (j % 2)
                    dve.wait_ge(qk_bcast, 8 * l + j + 1)
                    g = gain[:, 2 * KD + j // 4:2 * KD + j // 4 + 1]
                    src = (qk[:, j, 0:SEQ], qk[:, j, SEQ:TOK])
                    if j < 4:
                        tiles = q_rev[:, j, 0:SEQ].rearrange("p (t q) -> p t q", t=QT)
                        nc.vector.scalar_tensor_tensor(backwards(tiles, P), src[0].rearrange("p (t q) -> p t q", t=QT), g,
                                                       ps[:, b, :].rearrange("p (t q) -> p t q", t=QT), ALU.mult, ALU.mult)
                        dst = backwards(q_rev[:, j, SEQ:TOK], DEC)
                    else:
                        nc.vector.scalar_tensor_tensor(src[0], src[0], g, ps[:, b, :], ALU.mult, ALU.mult)
                        dst = src[1]
                    nc.vector.scalar_tensor_tensor(dst, src[1], g, ps[:, b + 1, 0:DEC], ALU.mult, ALU.mult).then_inc(qk_normed, 1)

                dve.wait_ge(rope_rows, l + 1)
                for n in range(12, 20):
                    unit_lo(n + 1)
                    rotated(n)
                dve.wait_ge(qk_cols_ps, l + 1)
                nc.vector.tensor_copy(qk_col[:, 0:SEQ], ps[0:16, 6, :])
                nc.vector.tensor_copy(qk_col[:, SEQ:TOK], ps[0:16, 7, 0:DEC]).then_inc(qk_cols, 1)
                for j in range(8):
                    qk_normalise(j)
                for n in range(20, 28):
                    unit_lo(n + 1)
                    if n == 20:
                        dve.wait_ge(tok_ps, 3 * TT * l + TT)
                    if n == 24:
                        dve.wait_ge(tok_ps, 3 * TT * l + 3 * TT)
                    scaled(U_LAYER * l + n, n % 2, vt[:, n - 20 if n < 24 else n - 24, :])

                def add_bias(k):
                    h, t = ITEMS_A[k]
                    r, w = rows(t), P * (t + 1) if t < QT else TOK
                    waits = [(s_ps, NA * l + k + 1)]
                    if t == 0:
                        waits.append((strip_masked, HA * l + h + 1))
                    if k >= 3:
                        waits.append((pt_ps, NA * l + k - 2))
                    wait_apart(dve, *waits)
                    if t < QT:
                        src, bias = ps[:, 2 + (QT * h + t) % 2, 0:w], strip[:, h % RING, STRIP - w:STRIP]
                        dst = work[:, k % 3, 0:w]
                    else:
                        src, bias = ps[0:r, 0:2, 0:HALF], halves(strip[P - DEC:P, h % RING, 0:TOK])
                        dst = halves(work[0:r, k % 3, :])
                    nc.vector.tensor_tensor_reduce(out=dst, in0=src, in1=bias, scale=1.0, scalar=3e38, op0=ALU.add,
                                                   op1=ALU.min, accum_out=least[0:r, k % 4:k % 4 + 1]).then_inc(biased, 1)

                def probs_out(k):
                    h, t = ITEMS_A[k]
                    dve.wait_ge(pt_ps, NA * l + k + 1)
                    if k >= 2:
                        dve.wait_ge(pv_done, NA * l + k - 1)
                    if t < QT:
                        nc.vector.tensor_copy(pt[:, k % 2, 0:P * (t + 1)], ps[:, 4 + k % 2, 0:P * (t + 1)]).then_inc(pt_evac, 1)
                    else:
                        c = QT * DEC
                        nc.vector.tensor_copy(pt[:, k % 2, 0:c], ps[:, 4 + k % 2, 0:c])
                        nc.vector.tensor_copy(pt[0:DEC, k % 2, c:c + DEC], ps[0:DEC, 4 + k % 2, c:c + DEC]).then_inc(pt_evac, 1)

                def head_normalise(h):
                    dve.wait_ge(exped, NA * l + TT * (h + 1))
                    nc.vector.reciprocal(rsum[:, h % 2, 0:QT], sums[:, h % 2, 0:QT])
                    nc.vector.reciprocal(rsum[0:DEC, h % 2, QT:TT], sums[0:DEC, h % 2, QT:TT]).then_inc(sums_inv, 1)
                    dve.wait_ge(sums_inv, HA * l + h + 1)
                    dve.wait_ge(pv_done, NA * l + TT * (h + 1))
                    p, c = h // 2, DA * (h % 2)
                    if p >= RING:
                        dve.wait_ge(ot_ps, HA // 2 * l + p - 1)
                    nc.vector.tensor_tensor(o_tok[:, p % 2, 0:QT, c:c + DA],
                                            ps[:, 6 + h % 2, 0:QT * DA].rearrange("p (t d) -> p t d", t=QT),
                                            rsum[:, h % 2, 0:QT].unsqueeze(2).to_broadcast([P, QT, DA]), ALU.mult)
                    nc.vector.tensor_scalar(o_tok[0:DEC, p % 2, QT, c:c + DA], ps[0:DEC, 6 + h % 2, QT * DA:TT * DA],
                                            rsum[0:DEC, h % 2, QT:TT], None, ALU.mult).then_inc(o_normed, 1)

                def attn_out_lo(p):
                    dve.wait_ge(ot_hi, HA // 2 * l + p + 1)
                    nc.vector.tensor_tensor(mix[:, p, 1, 0:SEQ].rearrange("p (t q) -> p t q", t=QT),
                                            backwards(ps[:, 0, :].rearrange("p (t q) -> p t q", t=QT), P),
                                            mix[:, p, 0, 0:SEQ].bitcast(F32).rearrange("p (t q) -> p t q", t=QT), ALU.subtract)
                    nc.vector.tensor_tensor(mix[:, p, 1, SEQ:TOK], backwards(ps[:, 1, 0:DEC], DEC),
                                            mix[:, p, 0, SEQ:TOK].bitcast(F32), ALU.subtract).then_inc(ot_lo, 1)

                for k in range(NA + 5):
                    if k >= 14 and (k - 14) % 10 == 0:
                        attn_out_lo((k - 14) // 10)
                    if k < NA:
                        add_bias(k)
                    if k >= 8 and (k - 8) % 5 == 0 and (k - 8) // 5 < HA:
                        head_normalise((k - 8) // 5)
                    if 0 <= k - 2 < NA:
                        probs_out(k - 2)

                def mask_scores(k):
                    h, t = ITEMS_R[k]
                    r, w = rows(t), P * (t + 1) if t < QT else DEC
                    c = SEQ - w if t < QT else SEQ - P
                    dve.wait_ge(r_ps, NR * l + k + 1)
                    if t == 0:
                        dve.wait_ge(dmask_loaded[h % RING], 16 * HR // RING * l + 16 * (h // RING + 1))
                    if k >= 3:
                        dve.wait_ge(sv_done, NR * l + k - 2)
                    nc.vector.tensor_tensor(work[0:r, k % 3, 0:w], ps[0:r, 2 + k % 2, 0:w], dmask[0:r, h % RING, c:c + w],
                                            ALU.mult).then_inc(decayed, 1)

                def query_decay(h):
                    dve.wait_ge(ret_ready, 8 * l + 8)
                    if h >= RING:
                        dve.wait_ge(sv_done, NR * l + TT * (h - RING + 1))
                    nc.vector.tensor_tensor(qd[:, h % RING, :], qk_ret[:, h, SEQ:TOK],
                                            cst[:, C_QDEC + DEC * h:C_QDEC + DEC * h + DEC], ALU.mult).then_inc(qd_ready, 1)

                def ret_tile(h, t):
                    return ps[:, 4 + h % 2, P * t:P * t + P] if t < QT else ps[0:DEC, 6 + h % 2, 0:P]

                def group_stats(h):
                    dve.wait_ge(sv_done, NR * l + TT * (h + 1))
                    for t in range(TT):
                        last = nc.vector.bn_stats(bn[0:rows(t), t, :], ret_tile(h, t))
                    last.then_inc(bn_parts, 1)
                    wait_apart(dve, (bn_parts, HR * l + h + 1))
                    for t in range(TT):
                        last = nc.vector.bn_aggr(mv[0:rows(t), t, :], bn[0:rows(t), t, :])
                    last.then_inc(bn_done, 1)

                def group_normalise(h):
                    dve.wait_ge(gn_root, HR * l + h + 1)
                    nc.vector.reciprocal(gni[:, 0:QT], gnr[:, 0:QT])
                    nc.vector.reciprocal(gni[0:DEC, QT:TT], gnr[0:DEC, QT:TT]).then_inc(gn_inv, 1)
                    dve.wait_ge(gn_inv, HR * l + h + 1)
                    if h >= RING:
                        dve.wait_ge(or_ps, HR * l + h - 1)
                    for t in range(TT):
                        last = nc.vector.tensor_scalar(o_tok[0:rows(t), h % 2, t, :], ret_tile(h, t), mv[0:rows(t), t, 0:1],
                                                       gni[0:rows(t), t:t + 1], ALU.subtract, ALU.mult)
                    last.then_inc(gn_normed, 1)

                y_f = pt[:].rearrange("p a b -> p (a b)")[:, 0:TOK]

                def gated(h):
                    dve.wait_ge(or_ps, HR * l + h + 1)
                    dve.wait_ge(g_silu, HR * l + HR)
                    g = gain[:, 2 * KD + 2 + h:2 * KD + 3 + h]
                    nc.vector.scalar_tensor_tensor(y_f[:, 0:SEQ], ps[:, 0, :], g, vt[:, h, 0:SEQ], ALU.mult, ALU.mult)
                    nc.vector.scalar_tensor_tensor(y_f[:, SEQ:TOK], ps[:, 1, 0:DEC], g, vt[:, h, SEQ:TOK],
                                                   ALU.mult, ALU.mult).then_inc(or_done, 1)

                def gated_lo(h):
                    dve.wait_ge(or_hi, HR * l + h + 1)
                    nc.vector.tensor_tensor(mix[:, 4 + h, 1, :], y_f, mix[:, 4 + h, 0, :].bitcast(F32), ALU.subtract).then_inc(or_lo, 1)

                def states(h):
                    H = P // 2
                    dve.wait_ge(st_ps, HR * l + h + 1)
                    nc.vector.tensor_copy(st_tmp[:, 0, :], ps[:, 1, P:2 * P])
                    nc.vector.scalar_tensor_tensor(st_tmp[:, 1, :], s_in[:, h, :], float(gamma(h) ** DEC), ps[:, 1, 2 * P:3 * P],
                                                   ALU.mult, ALU.add).then_inc(st_sum, 1)
                    dve.wait_ge(st_sum, HR * l + h + 1)
                    if h >= RING:
                        dve.wait_ge(st_stored[h % RING], 32 * (HR // RING) * l + 32 * (h // RING))
                    for i in range(2):
                        c = C_ROT + 2 * i + 1
                        nc.vector.tensor_scalar(st_swap[0:H, i, :], st_tmp[H:P, i, :], cst[H:P, c:c + 1], None, ALU.mult)
                        last = nc.vector.tensor_scalar(st_swap[H:P, i, :], st_tmp[0:H, i, :], cst[0:H, c:c + 1], None, ALU.mult)
                    last.then_inc(st_swapped, 1)
                    dve.wait_ge(st_swapped, HR * l + h + 1)
                    for i in range(2):
                        c = C_ROT + 2 * i
                        last = nc.vector.scalar_tensor_tensor(st_out[:, h % RING, i, :], st_tmp[:, i, :], cst[:, c:c + 1],
                                                              st_swap[:, i, :], ALU.mult, ALU.add)
                    last.then_inc(st_done, 1)

                dve.wait_ge(state_loaded, 16 * l + 16)
                dve.wait_ge(pt_ps, NA * l + NA)
                for k in range(NR + 7):
                    h, i = k // TT, k % TT
                    if i == 0 and h >= 2:
                        gated(h - 2)
                    if i == 0 and h < HR:
                        query_decay(h)
                    if k < NR:
                        mask_scores(k)
                    if i == 1 and h >= 2:
                        gated_lo(h - 2)
                    if i == 2 and 1 <= h <= HR:
                        group_stats(h - 1)
                    if i == 3 and 1 <= h <= HR:
                        group_normalise(h - 1)
                    if i == 4 and h < HR:
                        states(h)

                def add_to_x(n, s, c):
                    projected(n)
                    xc = x[:, bass.ds(c, 1), :].rearrange("p o (a b) -> p (o a) b", a=2)
                    nc.vector.tensor_tensor(xc, dense(s), xc, ALU.add).then_inc(evacuated, 1)

                for c in range(U_OUT):
                    if c + 1 < U_OUT:
                        unit_lo(FIRST_OUT + c + 1)
                    add_to_x(U_LAYER * l + FIRST_OUT + c, c % 2, c)
                    if c:
                        norm_lo(l, 1, ffn, c - 1)
                unit_lo(FIRST_FFN)
                norm_lo(l, 1, ffn, KD - 1)
                for g in range(GROUPS):
                    first = FIRST_FFN + U_GROUP * g

                    def group_lo(i, s, k=KD):
                        lo(s, U_LAYER * l + i + first, k)

                    def up_out(f):
                        scaled(U_LAYER * l + 2 * f + (first + 1), 1, work[:, 1, :])

                    def product(f):
                        dve.wait_ge(gate_silu, GROUPS * FT * l + f + (FT * g + 1))
                        dve.wait_ge(evacuated, U_LAYER * l + 2 * f + (first + 1 + EV + 1))
                        nc.vector.tensor_tensor(work[:, 2, :], work[:, 0, :], work[:, 1, :], ALU.mult).then_inc(act_f, 1)

                    def act_low(f):
                        dve.wait_ge(act_hi, GROUPS * FT * l + f + (FT * g + 1))
                        a = act[:, bass.ds(f, 1), :, :]
                        nc.vector.tensor_tensor(a[:, :, 1, :].rearrange("p a b -> p (a b)"), work[:, 2, :],
                                                a[:, :, 0, :].rearrange("p a b -> p (a b)").bitcast(F32), ALU.subtract).then_inc(act_lo, 1)

                    group_lo(1, 1)
                    if g == 0:
                        rms_invert(l, 1)
                        group_lo(2, 0)
                        rms_rows(l, 1)
                    scaled(U_LAYER * l + first, 0, work[:, 0, :])
                    if g:
                        group_lo(2, 0)
                    up_out(0)
                    product(0)
                    with dve.Fori(1, FT - 1) as f:
                        group_lo(2 * f + 1, 1)
                        scaled(U_LAYER * l + 2 * f + first, 0, work[:, 0, :])
                        act_low(f - 1)
                        group_lo(2 * f + 2, 0)
                        up_out(f)
                        product(f)
                    f = FT - 1
                    group_lo(2 * f + 1, 1)
                    scaled(U_LAYER * l + 2 * f + first, 0, work[:, 0, :])
                    act_low(f - 1)
                    group_lo(DOWN, 0, FT)
                    up_out(f)
                    product(f)
                    act_low(f)
                    with dve.Fori(0, (U_OUT - 2) // 2) as c2:
                        c = 2 * c2
                        for s in range(2):
                            group_lo(c + (DOWN + s + 1), 1 - s, FT)
                            add_to_x(U_LAYER * l + c + (first + DOWN + s), s, c + s)
                    group_lo(DOWN + U_OUT - 1, 1, FT)
                    add_to_x(U_LAYER * l + first + DOWN + U_OUT - 2, 0, U_OUT - 2)
                    if g + 1 < GROUPS:
                        group_lo(U_GROUP, 0)
                    add_to_x(U_LAYER * l + first + DOWN + U_OUT - 1, 1, U_OUT - 1)

        @block.tensor
        def _(pe):
            def unit(n, slot, nk, src, ready=None):
                pe.wait_ge(lo_done, n + RING + 1)
                pe.wait_ge(evacuated, n + EV - 1)
                for k in range(nk):
                    if ready:
                        ready(k)
                    for i, (w, part) in enumerate(((w_hi, 0), (w_hi, 1), (w_lo, 0))):
                        for half in range(2):
                            last = nc.tensor.matmul(ps[:, 2 * slot + half, 0:HALF], w[:, slot, k, :],
                                                    src[:, k, part, HALF * half:HALF * half + HALF],
                                                    start=k == 0 and i == 0, stop=k == nk - 1 and i == 2)
                last.then_inc(w_used, 1)

            def rms_sums(l, which, sq):
                pe.wait_ge(sq_done, 3 * KD * l + KD * (2 * which + 1))
                for t in range(TT):
                    for k in range(KD):
                        last = nc.tensor.matmul(ps[0:rows(t), 6, t:t + 1], sq[:, k, tok(t)], cst[:, C_ONE:C_ONE + 1],
                                                start=k == 0, stop=k == KD - 1)
                last.then_inc(rms_stat, 1)

            def rms_spread(l, which):
                pe.wait_ge(rms_inv, 2 * l + which + 1)
                for t in range(TT):
                    r = rows(t)
                    dst = ps[:, 4, tok(t)] if t < QT else ps[:, 5, 0:DEC]
                    last = nc.tensor.transpose(dst, inv[0:r, t:t + 1].to_broadcast([r, P]), ident[0:r, 0:r])
                last.then_inc(rms_bcast, 1)

            def to_tokens(l, group, tiles):
                for t in range(TT):
                    if t == 4:
                        wait_apart(pe, (tok_evac, 3 * TT * l + TT * group + 1))
                    for j in range(4):
                        last = nc.tensor.transpose(ps[0:rows(t), 4 + t % 4, P * j:P * j + P], tiles[:, j, tok(t)], ident)
                    last.then_inc(tok_ps, 1)

            pe.sem_inc(w_used, RING)
            pe.wait_ge(const_in, 32)
            pe.wait_ge(gains_in, 16 * 7 * DEPTH)
            n = DEPTH * GAINS
            nc.tensor.transpose(ps[:, 0, 0:n], gain_rows, ident[0:n, 0:n]).then_inc(gains_ps, 1)
            pe.wait_ge(x_in, 32)
            for k in range(KD):
                b = 4 + 2 * (k % 2)
                if k >= 2:
                    pe.wait_ge(evacuated, RING + k - 1)
                for t in range(TT):
                    r = rows(t)
                    dst = ps[:, b, tok(t)] if t < QT else ps[:, b + 1, 0:DEC]
                    last = nc.tensor.transpose(dst, stage[0:r, t, P * k:P * k + P], ident[0:r, 0:r])
                last.then_inc(x_ps, 1)
            with pe.Fori(0, DEPTH) as l:
                def in_unit(n, slot, ready=None):
                    unit(U_LAYER * l + n, slot, KD, mix, ready)

                def mix_ready(k):
                    pe.wait_ge(h_lo, 2 * KD * l + k + 1)

                def in_units(a, b):
                    with pe.Fori(a // 2, b // 2) as n2:
                        n = 2 * n2
                        for s in range(2):
                            in_unit(n + s, s)

                in_unit(0, 0, mix_ready)
                rms_sums(l, 0, mix_sq)
                in_unit(1, 1)
                rms_spread(l, 0)
                in_units(2, 10)
                pe.wait_ge(sq_done, 3 * KD * l + 2 * KD)
                for t in range(TT):
                    for j in range(8):
                        last = nc.tensor.matmul(ps[0:rows(t), 7, 16 * t + 2 * j:16 * t + 2 * j + 2], mix_sq[:, j, tok(t)],
                                                cst[:, C_SEL:C_SEL + 2], start=True, stop=True)
                last.then_inc(qk_stat, 1)
                in_units(10, 14)
                pe.wait_ge(evacuated, U_LAYER * l + 11 + EV + 1)
                pe.wait_ge(qk_root, l + 1)
                to_tokens(l, 0, vt)
                in_units(14, 20)
                pe.wait_ge(qk_inv, l + 1)
                pe.wait_ge(tok_evac, 3 * TT * l + TT)
                for t in range(TT):
                    r = rows(t)
                    dst = ps[0:16, 6, tok(t)] if t < QT else ps[0:16, 7, 0:DEC]
                    last = nc.tensor.transpose(dst, qinv[0:r, t, :], ident[0:r, 0:r])
                last.then_inc(qk_cols_ps, 1)
                pe.wait_ge(qk_cols, l + 1)
                for j in range(8):
                    b = 4 + 2 * (j % 2)
                    if j >= 2:
                        pe.wait_ge(qk_normed, 8 * l + j - 1)
                    nc.tensor.matmul(ps[:, b, :], spread[:, P * j:P * j + P], qk_col[:, 0:SEQ], start=True, stop=True)
                    nc.tensor.matmul(ps[:, b + 1, 0:DEC], spread[:, P * j:P * j + P], qk_col[:, SEQ:TOK],
                                     start=True, stop=True).then_inc(qk_bcast, 1)
                in_units(20, 24)
                pe.wait_ge(qk_normed, 8 * l + 8)
                to_tokens(l, 1, qk[:, 4:8, :])
                in_unit(24, 0)
                pe.wait_ge(evacuated, U_LAYER * l + 23 + EV + 1)
                pe.wait_ge(tok_evac, 3 * TT * l + 2 * TT)
                to_tokens(l, 2, vt)
                for n in range(25, 28):
                    in_unit(n, n % 2)

                def cache_keys(p):
                    pe.wait_ge(kv_loaded[p % RING], 32 * (HA // 2 // RING) * l + 32 * (p // RING + 1))
                    if p:
                        pe.wait_ge(biased, NA * l + 2 * TT * p)
                    for t in range(QT):
                        last = nc.tensor.transpose(ps[:, 0, P * t:P * t + P], kc_tok[:, p % RING, t, :], ident)
                    last.then_inc(kct_ps, 1)

                def scores(k):
                    h, t = ITEMS_A[k]
                    hr = head_rows(h)
                    q, keys = q_rev[hr, h // 2, tok(t)], qk[hr, 4 + h // 2, :]
                    if t < QT:
                        i = QT * h + t
                        if i >= 2:
                            j = ITEMS_A.index(((i - 2) // QT, (i - 2) % QT))
                            pe.wait_ge(biased, NA * l + j + 1)
                        nc.tensor.matmul(ps[:, 2 + i % 2, 0:P * (t + 1)], q, keys[:, 0:P * (t + 1)],
                                         start=True, stop=True).then_inc(s_ps, 1)
                    else:
                        cached = kc_t[hr, (h // 2) % RING, :]
                        waits = [(kct_evac, HA // 2 * l + h // 2 + 1)]
                        if h % 2:
                            waits.append((biased, NA * l + TT * h))
                        elif h:
                            waits.append((ot_lo, HA // 2 * l + h // 2))
                        wait_apart(pe, *waits)
                        nc.tensor.matmul(ps[0:DEC, 0, 0:HALF], q, cached[:, 0:HALF], start=True, stop=True)
                        nc.tensor.matmul(ps[0:DEC, 1, 0:SEQ - HALF], q, cached[:, HALF:SEQ], start=True, stop=True)
                        nc.tensor.matmul(ps[0:DEC, 1, SEQ - HALF:HALF], q, keys[:, SEQ:TOK],
                                         start=True, stop=True).then_inc(s_ps, 1)

                def probs(k):
                    h, t = ITEMS_A[k]
                    waits = [(exped, NA * l + k + 1)]
                    if k >= 2:
                        waits.append((pt_evac, NA * l + k - 1))
                    wait_apart(pe, *waits)
                    b, src = 4 + k % 2, work[:, k % 3, :]
                    if t < QT:
                        for s in range(t + 1):
                            last = nc.tensor.transpose(ps[:, b, P * s:P * s + P], src[:, P * s:P * s + P], ident)
                    else:
                        idr = ident[0:DEC, 0:DEC]
                        for s in range(QT):
                            nc.tensor.transpose(ps[:, b, DEC * s:DEC * s + DEC], src[0:DEC, P * s:P * s + P], idr)
                        last = nc.tensor.transpose(ps[0:DEC, b, QT * DEC:TT * DEC], src[0:DEC, SEQ:TOK], idr)
                    last.then_inc(pt_ps, 1)

                def values(k):
                    h, t = ITEMS_A[k]
                    b, c, src = 6 + h % 2, DA * h, pt[:, k % 2, :]
                    pe.wait_ge(pt_evac, NA * l + k + 1)
                    if t == 0 and h >= 2:
                        pe.wait_ge(o_normed, HA * l + h - 1)
                    if t < QT:
                        for s in range(t + 1):
                            last = nc.tensor.matmul(ps[:, b, DA * t:DA * t + DA], src[:, P * s:P * s + P], va[:, s, c:c + DA],
                                                    start=s == 0, stop=s == t)
                    else:
                        vc = vc_tok[:, (h // 2) % RING, :, :]
                        out = ps[0:DEC, b, QT * DA:TT * DA]
                        for s in range(QT):
                            nc.tensor.matmul(out, src[:, DEC * s:DEC * s + DEC], vc[:, s, DA * (h % 2):DA * (h % 2) + DA],
                                             start=s == 0, stop=False)
                        last = nc.tensor.matmul(out, src[0:DEC, QT * DEC:TT * DEC], va[0:DEC, QT, c:c + DA],
                                                start=False, stop=True)
                    last.then_inc(pv_done, 1)

                def pair_out(p):
                    pe.wait_ge(o_normed, HA * l + 2 * p + 2)
                    if p + 1 < HA // 2:
                        pe.wait_ge(kct_evac, HA // 2 * l + p + 2)
                    else:
                        pe.wait_ge(biased, NA * l + NA)
                    for t in range(TT):
                        r = rows(t)
                        dst = ps[:, 0, tok(t)] if t < QT else ps[:, 1, 0:DEC]
                        last = nc.tensor.transpose(dst, o_tok[0:r, p % 2, t, :], ident[0:r, 0:r])
                    last.then_inc(ot_ps, 1)

                pe.wait_ge(evacuated, U_LAYER * l + U_IN + EV)
                pe.wait_ge(tok_evac, 3 * TT * l + 3 * TT)
                cache_keys(0)
                for k in range(NA + 4):
                    if k and k % (2 * TT) == 0 and k < NA:
                        cache_keys(k // (2 * TT))
                    if k < NA:
                        scores(k)
                    if 0 <= k - 2 < NA:
                        probs(k - 2)
                    if 0 <= k - 3 < NA:
                        values(k - 3)
                    if k >= 13 and (k - 13) % 10 == 0:
                        pair_out((k - 13) // 10)

                def ret_keys(h):
                    if h >= 2:
                        pe.wait_ge(or_done, HR * l + h - 1)
                    elif h == 1:
                        pe.wait_ge(st_sum, HR * l + 1)
                    for t in range(TT):
                        dst = ps[:, 0, tok(t)] if t < QT else ps[0:DEC, 1, 0:P]
                        last = nc.tensor.transpose(dst, qk_ret[:, 4 + h, tok(t)], ident)
                    last.then_inc(kd_ps, 1)

                def ret_scores(k):
                    h, t = ITEMS_R[k]
                    if k >= 2:
                        wait_apart(pe, (decayed, NR * l + k - 1))
                    if t < QT:
                        for s in range(t + 1):
                            last = nc.tensor.matmul(ps[:, 2 + k % 2, P * s:P * s + P], qk_ret[:, 4 + h, tok(s)],
                                                    qk_ret[:, h, tok(t)], start=True, stop=True)
                    else:
                        last = nc.tensor.matmul(ps[0:DEC, 2 + k % 2, 0:DEC], qk_ret[:, 4 + h, tok(t)],
                                                qk_ret[:, h, tok(t)], start=True, stop=True)
                    last.then_inc(r_ps, 1)

                def ret_values(k):
                    h, t = ITEMS_R[k]
                    pe.wait_ge(decayed, NR * l + k + 1)
                    if t == 0 and h >= 2:
                        pe.wait_ge(gn_normed, HR * l + h - 1)
                    v = vr[:, :, DR * h:DR * h + DR]
                    if t < QT:
                        for s in range(t + 1):
                            last = nc.tensor.matmul(ps[:, 4 + h % 2, P * t:P * t + P], work[:, k % 3, P * s:P * s + P], v[:, s, :],
                                                    start=s == 0, stop=s == t)
                    else:
                        pe.wait_ge(qd_ready, HR * l + h + 1)
                        nc.tensor.matmul(ps[0:DEC, 6 + h % 2, 0:P], qd[:, h % RING, :], s_in[:, h, :], start=True, stop=False)
                        last = nc.tensor.matmul(ps[0:DEC, 6 + h % 2, 0:P], work[0:DEC, k % 3, 0:DEC], v[0:DEC, QT, :],
                                                start=False, stop=True)
                    last.then_inc(sv_done, 1)

                def ret_states(h):
                    pe.wait_ge(kd_evac, HR * l + h + 1)
                    v = vr[:, :, DR * h:DR * h + DR]
                    for t in range(QT):
                        nc.tensor.matmul(ps[:, 1, P:2 * P], kd_tok[:, h % 2, t, :], v[:, t, :], start=t == 0, stop=t == QT - 1)
                    nc.tensor.matmul(ps[:, 1, 2 * P:3 * P], kd_tok[0:DEC, h % 2, QT, :], v[0:DEC, QT, :],
                                     start=True, stop=True).then_inc(st_ps, 1)

                def ret_out(h):
                    pe.wait_ge(gn_normed, HR * l + h + 1)
                    pe.wait_ge(st_sum, HR * l + min(h + 2, HR))
                    for t in range(TT):
                        r = rows(t)
                        dst = ps[:, 0, tok(t)] if t < QT else ps[:, 1, 0:DEC]
                        last = nc.tensor.transpose(dst, o_tok[0:r, h % 2, t, :], ident[0:r, 0:r])
                    last.then_inc(or_ps, 1)

                pe.wait_ge(ot_lo, HA // 2 * l + HA // 2)
                pe.wait_ge(ret_ready, 8 * l + 8)
                pe.wait_ge(state_loaded, 16 * l + 16)
                for k in range(NR + 5):
                    h, i = k // TT, k % TT
                    if i == 0 and h < HR:
                        ret_keys(h)
                    if k < NR:
                        ret_scores(k)
                    if 0 <= k - 2 < NR:
                        ret_values(k - 2)
                    if i == 3 and h < HR:
                        ret_states(h)
                    if i == 4 and h >= 1:
                        ret_out(h - 1)

                pe.wait_ge(or_done, HR * l + HR)

                def mixed(k):
                    if k < 4:
                        pe.wait_ge(ot_lo, HA // 2 * l + k + 1)
                    else:
                        pe.wait_ge(or_lo, HR * l + k - 3)

                unit(U_LAYER * l + FIRST_OUT, 0, KD, mix, mixed)
                unit(U_LAYER * l + FIRST_OUT + 1, 1, KD, mix)
                with pe.Fori(1, U_OUT // 2) as c2:
                    c = 2 * c2
                    for s in range(2):
                        unit(U_LAYER * l + c + (FIRST_OUT + s), s, KD, mix)

                def ffn_ready(k):
                    pe.wait_ge(h_lo, 2 * KD * l + KD + k + 1)

                for g in range(GROUPS):
                    first = FIRST_FFN + U_GROUP * g
                    if g == 0:
                        unit(U_LAYER * l + first, 0, KD, ffn, ffn_ready)
                        rms_sums(l, 1, ffn_sq)
                        unit(U_LAYER * l + first + 1, 1, KD, ffn)
                        rms_spread(l, 1)
                    with pe.Fori(1 if g == 0 else 0, FT) as f:
                        for s in range(2):
                            unit(U_LAYER * l + 2 * f + (first + s), s, KD, ffn)

                    def act_ready(k):
                        pe.wait_ge(act_lo, GROUPS * FT * l + FT * g + k + 1)

                    unit(U_LAYER * l + first + DOWN, 0, FT, act, act_ready)
                    unit(U_LAYER * l + first + DOWN + 1, 1, FT, act)
                    with pe.Fori(1, U_OUT // 2) as c2:
                        c = 2 * c2
                        for s in range(2):
                            unit(U_LAYER * l + c + (first + DOWN + s), s, FT, act)
            pe.wait_ge(evacuated, DEPTH * U_LAYER + EV)
            for t in range(TT):
                if t >= 2:
                    pe.wait_ge(y_copied, t - 1)
                for k in range(KD):
                    b = 2 * (t % 2) + k // 4
                    last = nc.tensor.transpose(ps[0:rows(t), b, P * (k % 4):P * (k % 4) + P], x[:, k, tok(t)], ident)
                last.then_inc(y_ps, 1)


OUTPUTS = [
    ("y_prompt", (1, SEQ, D)), ("y_sample", (1, DEC, D)),
    ("nk_prompt", (DEPTH, 1, SEQ, HA, DA)), ("nv_prompt", (DEPTH, 1, SEQ, HA, DA)), ("ns_prompt", (DEPTH, 1, HR, DR, DR)),
    ("nk_sample", (DEPTH, 1, DEC, HA, DA)), ("nv_sample", (DEPTH, 1, DEC, HA, DA)), ("ns_sample", (DEPTH, 1, HR, DR, DR)),
]


def tables():
    import numpy as np

    half = DR // 2
    inv = (np.float32(10000.0) ** (-np.arange(half, dtype=np.float32) / np.float32(half))).astype(np.float32)

    def angles(pos):
        return (inv[:, None] * np.asarray(pos, np.float32)[None, :]).astype(np.float32).astype(np.float64)

    c = np.zeros((P, C_ALL))
    c[:, C_ID:C_ID + P] = np.eye(P)
    a = angles(np.arange(SEQ))
    c[:, C_COS:C_COS + SEQ] = np.concatenate([np.cos(a)] * 2)
    c[:, C_SIN:C_SIN + SEQ] = np.concatenate([np.sin(a), -np.sin(a)])
    scale = DR ** -0.5
    decay = np.zeros((HR, P, SEQ))
    for h in range(HR):
        lg = np.log(gamma(h))
        c[:, C_QDEC + DEC * h:C_QDEC + DEC * h + DEC] = np.exp((np.arange(DEC) + 1.0) * lg)
        for t in range(QT):
            c[:, C_KDEC + HR * t + h] = scale * np.exp((SEQ - 1.0 - P * t - np.arange(P)) * lg)
        c[0:DEC, C_KDEC + HR * QT + h] = scale * np.exp((DEC - 1.0 - np.arange(DEC)) * lg)
        for b in range(QT):
            diff = P * (QT - 1 - b) + np.arange(P)[None, :] - np.arange(P)[:, None]
            decay[h, :, P * b:P * b + P] = np.where(diff >= 0, scale * np.exp(np.maximum(diff, 0) * lg), 0.0)
    for i, pos in enumerate((-SEQ, -DEC)):
        a = angles([pos])[:, 0]
        c[:, C_ROT + 2 * i] = np.concatenate([np.cos(a)] * 2)
        c[:, C_ROT + 2 * i + 1] = np.concatenate([np.sin(a), -np.sin(a)])
    c[0:DA, C_SEL] = 1.0
    c[DA:P, C_SEL + 1] = 1.0
    c[:, C_ONE] = 1.0
    c[:, C_EPS] = RMS_EPS
    c[:, C_EPS + 1] = GN_EPS
    return c.astype(np.float32), np.repeat(np.eye(16, dtype=np.float32), DA, axis=1), decay.astype(np.float32)


def kernel(x_prompt, x_sample, cache_a_k, cache_a_v, state_ret, norm_mix, w_in, q_norm, k_norm, rel_table,
           ret_norm, w_out, norm_ffn, w_gate, w_up, w_down):
    import numpy as np
    import concourse.bacc as bacc
    from concourse.bass_utils import run_bass_kernel_spmd

    nc = bacc.Bacc("TRN2", target_bir_lowering=False, num_devices=1)
    const, spread, decay = tables()
    arrays = dict(x_prompt=x_prompt, x_sample=x_sample, cache_k=cache_a_k, cache_v=cache_a_v, state_in=state_ret,
                  norm_mix=norm_mix, w_in=w_in, q_norm=q_norm, k_norm=k_norm, rel_table=rel_table, ret_norm=ret_norm,
                  w_out=w_out, norm_ffn=norm_ffn, w_gate=w_gate, w_up=w_up, w_down=w_down, const=const, spread=spread, decay=decay)
    arrays = {f"in_{name}": np.ascontiguousarray(a) for name, a in arrays.items()}
    aps = [nc.dram_tensor(name, a.shape, mybir.dt.from_np(a.dtype), kind="ExternalInput").ap() for name, a in arrays.items()]
    aps += [nc.dram_tensor(f"out_{name}", shape, F32, kind="ExternalOutput").ap() for name, shape in OUTPUTS]
    lines = nc.dram_tensor("bias_lines", (DEPTH * HA, 6 * P), F32, kind="Internal").ap()
    build(nc, *aps, lines)
    r = run_bass_kernel_spmd(nc, [arrays], core_ids=[0])
    return tuple(r.results[0][f"out_{name}"] for name, _ in OUTPUTS)
```

```python
import concourse.bass as bass
from concourse import mybir
from contextlib import ExitStack

F32 = mybir.dt.float32
F32R = mybir.dt.float32r
ALU = mybir.AluOpType
ACT = mybir.ActivationFunctionType

P = 128
DEPTH = 2
D = 1024
KD = D // P
SEQ, DEC, PAST = 512, 64, 1024
TOK = SEQ + DEC
HALF = TOK // 2
QT = SEQ // P
TT = QT + 1
HA, DA = 8, 64
HR, DR = 4, 128
WA, WR = HA * DA, HR * DR
CHUNK = 64
REL = 128
DFF = 2816
GROUPS = 2
FT = DFF // P // GROUPS
U_IN = (3 * WA + 4 * WR) // P
U_OUT = D // P
U_GROUP = 2 * FT + U_OUT
U_LAYER = U_IN + U_OUT + GROUPS * U_GROUP
RING = 2
STRIP = 5 * P
LINE = STRIP + P - 1
GAINS = 2 * KD + 2 + WR // P
EV = RING + KD
RMS_EPS, GN_EPS = 1e-6, 1e-5
MASKED = 1e30

C_ID = 0
C_COS = C_ID + P
C_SIN = C_COS + SEQ
C_QDEC = C_SIN + SEQ
C_KDEC = C_QDEC + HR * DEC
C_ROT = C_KDEC + TT * HR
C_SEL = C_ROT + 4
C_ONE = C_SEL + 2 * WA // P * 16
C_EPS = C_ONE + 1
C_ALL = C_EPS + 2


def gamma(h):
    return 1.0 - 2.0 ** (-5.0 - h)


def tok(t):
    return slice(t * P, t * P + rows(t))


def rows(t):
    return P if t < QT else DEC


def backwards(ap, n):
    dims = [list(d) for d in ap.ap]
    step, count = dims[-1]
    assert count == n
    dims[-1] = [-step, n]
    return bass.AP(tensor=ap.tensor, offset=ap.offset + step * (n - 1), ap=dims)


def build(nc, x_prompt, x_sample, cache_k, cache_v, state_in, norm_mix, w_in, q_norm, k_norm, rel_table,
          ret_norm, w_out, norm_ffn, w_gate, w_up, w_down, const, spread_in, decay,
          y_prompt, y_sample, nk_prompt, nv_prompt, ns_prompt, nk_sample, nv_sample, ns_sample, lines):
    ctx = ExitStack()
    with ctx:
        ROW = TOK * 4
        base = (nc.sbuf_base + 31) // 32 * 32
        A_X = base
        A_MIX = A_X + KD * ROW
        A_SH = A_MIX + 2 * KD * ROW
        A_W = A_SH + 2 * KD * ROW + 2 * FT * ROW
        UNIT = FT * P * 4
        A_MISC = A_W + 3 * RING * UNIT

        def place(name, shape, dt, at):
            return nc.alloc_sbuf_tensor_at(name, shape, dt, offset=at)

        nc.alloc_sbuf_tensor("arena", [P, (A_MISC - base) // 4], F32)
        x = place("x", [P, KD, TOK], F32, A_X)
        mix = place("mix", [P, KD, 2, TOK], F32R, A_MIX)
        qk = place("qk", [P, 2 * WA // P, TOK], F32, A_SH)
        kc_tok = place("kc_tok", [P, QT, P], F32, A_SH)
        kc_t = place("kc_t", [P, SEQ], F32, A_SH + SEQ * 4)
        vc_tok = place("vc_tok", [P, RING, QT, P], F32, A_SH + 2 * SEQ * 4)
        q_rev = place("q_rev", [P, WA // P, TOK], F32, A_SH + 8 * ROW)
        vt = place("vt", [P, 4, TOK], F32, A_SH + 12 * ROW)
        qk_ret = place("qk_ret", [P, 8, TOK], F32, A_SH + 16 * ROW)
        A_T = A_SH + 24 * ROW
        va = place("va", [P, TT, WA], F32, A_T)
        vr = place("vr", [P, TT, WR], F32, A_T + TT * WA * 4)
        A_S2 = A_T + 2 * TT * WA * 4
        strip = place("strip", [P, RING, STRIP], F32, A_S2)
        dmask = place("dmask", [P, RING, SEQ], F32, A_S2 + RING * STRIP * 4)
        s_in = place("s_in", [P, HR, DR], F32, A_S2 + RING * STRIP * 4 + RING * SEQ * 4)
        assert A_S2 + RING * STRIP * 4 + RING * SEQ * 4 + HR * DR * 4 <= A_W
        gate = qk[:, 4:8, :]
        kd_tok = place("kd_tok", [P, RING, TT, P], F32, A_SH)
        st_tmp = place("st_tmp", [P, 2, DR], F32, A_SH + 5120)
        st_swap = place("st_swap", [P, 2, DR], F32, A_SH + 6144)
        st_out = place("st_out", [P, RING, 2, DR], F32, A_SH + 7168)
        stage = place("stage", [P, TT, D], F32, A_SH)
        ffn = place("ffn", [P, KD, 2, TOK], F32R, A_SH)
        act = place("act", [P, FT, 2, TOK], F32R, A_SH + 2 * KD * ROW)
        ffn_sq = place("ffn_sq", [P, KD, TOK], F32, A_SH + 2 * KD * ROW)
        mix_sq = qk_ret
        w_raw = place("w_raw", [P, RING, FT, P], F32, A_W)
        w_hi = place("w_hi", [P, RING, FT, P], F32R, A_W + RING * UNIT)
        w_lo = place("w_lo", [P, RING, FT, P], F32R, A_W + 2 * RING * UNIT)

        def sb(name, shape, dt=F32):
            return ctx.enter_context(nc.sbuf_tensor(name, shape, dt))

        cst = sb("cst", [P, C_ALL])
        row_f = sb("row_f", [P, TOK])
        rcos = sb("rcos", [P, TOK])
        rsin = sb("rsin", [P, TOK])
        work = sb("work", [P, 3, TOK])
        pt = sb("pt", [P, RING, SEQ])
        o_tok = sb("o_tok", [P, RING, TT, P])
        qd = sb("qd", [P, RING, DEC])
        spread = sb("spread", [16, KD * P])
        qk_root_col, qk_col = work[0:16, 1, :], work[0:16, 2, :]
        gain_rows = pt[0:DEPTH * GAINS, 0, 0:P]
        gains = sb("gains", [P, DEPTH, GAINS])
        gain = sb("gain", [P, GAINS])
        root = sb("root", [P, TT])
        inv = sb("inv", [P, TT])
        least = sb("least", [P, 4])
        sums = sb("sums", [P, RING, TT])
        rsum = sb("rsum", [P, RING, TT])
        bn = sb("bn", [P, TT, 6])
        mv = sb("mv", [P, TT, 2])
        gnr = sb("gnr", [P, TT])
        gni = sb("gni", [P, TT])

        ps = ctx.enter_context(nc.psum_tensor("ps", [P, 8, 512], F32))

        def sem(name):
            return ctx.enter_context(nc.semaphore(name))

        raw_loaded = [sem(f"raw_loaded{s}") for s in range(RING)]
        hi_done, lo_done, w_used, evacuated = sem("hi_done"), sem("lo_done"), sem("w_used"), sem("evacuated")
        ident_in, const_in, gains_in, gains_ps, gains_set, gain_cur = (sem(n) for n in (
            "ident_in", "const_in", "gains_in", "gains_ps", "gains_set", "gain_cur"))
        rel_in, line_made, line_out = sem("rel_in"), sem("line_made"), sem("line_out")
        x_ps = sem("x_ps")
        x_in = [sem(f"x_in{s}") for s in range(2)]
        h_hi, h_lo, sq_done, sq_sum = sem("h_hi"), sem("h_lo"), sem("sq_done"), sem("sq_sum")
        half_ps, half_out = sem("half_ps"), sem("half_out")
        rms_stat, rms_root, rms_inv, rms_bcast, rms_row = (sem(n) for n in (
            "rms_stat", "rms_root", "rms_inv", "rms_bcast", "rms_row"))
        rope_rows = sem("rope_rows")
        qk_stat, qk_root, qk_inv, qk_bcast, qk_normed = (sem(n) for n in (
            "qk_stat", "qk_root", "qk_inv", "qk_bcast", "qk_normed"))
        ret_ready, tok_ps, tok_evac, g_silu = (sem(n) for n in ("ret_ready", "tok_ps", "tok_evac", "g_silu"))
        ka_out, va_out = sem("ka_out"), sem("va_out")
        strip_loaded = [sem(f"strip_loaded{s}") for s in range(RING)]
        strip_masked = sem("strip_masked")
        kc_loaded = sem("kc_loaded")
        vc_loaded = [sem(f"vc_loaded{s}") for s in range(RING)]
        kct_ps, kct_evac = sem("kct_ps"), sem("kct_evac")
        s_ps, biased, exped, pt_ps, pt_evac, pv_done = (sem(n) for n in (
            "s_ps", "biased", "exped", "pt_ps", "pt_evac", "pv_done"))
        sums_inv, o_normed, ot_ps, ot_out, ot_hi, ot_lo = (sem(n) for n in (
            "sums_inv", "o_normed", "ot_ps", "ot_out", "ot_hi", "ot_lo"))
        dmask_loaded = [sem(f"dmask_loaded{s}") for s in range(RING)]
        state_loaded = sem("state_loaded")
        kd_ps, kd_evac, r_ps, decayed, sv_done, qd_ready = (sem(n) for n in (
            "kd_ps", "kd_evac", "r_ps", "decayed", "sv_done", "qd_ready"))
        bn_parts, bn_done, gn_root, gn_inv, gn_normed, or_ps, or_done, or_hi, or_lo = (sem(n) for n in (
            "bn_parts", "bn_done", "gn_root", "gn_inv", "gn_normed", "or_ps", "or_done", "or_hi", "or_lo"))
        st_ps, st_sum, st_swapped, st_done = (sem(n) for n in ("st_ps", "st_sum", "st_swapped", "st_done"))
        st_stored = [sem(f"st_stored{s}") for s in range(RING)]
        gate_silu, act_f, act_hi, act_lo = (sem(n) for n in ("gate_silu", "act_f", "act_hi", "act_lo"))
        passed = {e.engine: sem(f"passed_{i}") for i, e in enumerate((nc.gpsimd, nc.scalar, nc.vector, nc.tensor))}
        y_ps, y_copied, y_out = sem("y_ps"), sem("y_copied"), sem("y_out")

        block = ctx.enter_context(nc.Block())

        ident = cst[:, C_ID:C_ID + P]
        cos, sin = cst[:, C_COS:C_COS + SEQ], cst[:, C_SIN:C_SIN + SEQ]

        def dense(s):
            return ps[:, 2 * s:2 * s + 2, 0:HALF]

        def halves(ap):
            return ap.rearrange("p (a b) -> p a b", a=2)

        def head_rows(h):
            return slice(DA * (h % 2), DA * (h % 2) + DA)

        def x_count(l, which):
            return U_LAYER * l + (RING if which == 0 else U_IN + EV)

        def wait_apart(eng, *waits):
            for semaphore, count in waits:
                eng.wait_ge(semaphore, count)
            eng.sem_inc(passed[eng.engine], 1)

        FIRST_OUT = U_IN
        FIRST_FFN = U_IN + U_OUT
        DOWN = 2 * FT

        ITEMS_A = [(h, t) for h in range(HA) for t in range(TT)]
        ITEMS_R = [(h, t) for h in range(HR) for t in range(TT)]
        NA, NR = len(ITEMS_A), len(ITEMS_R)
        STEPS_A = NA + 4

        FIRST_HALF = 3 * WA // P
        HALVES = 2 * (U_IN - FIRST_HALF)
        PRE = 6
        NORM_ORDER = [j + 4 * i for j in range(4) for i in range(2)]

        def halves_before(k):
            if k > NA:
                return min(HALVES, HALVES - 2 + (k - NA))
            return PRE + (HALVES - 2 - PRE) * k // NA

        @block.sync
        def _(sp):
            sp.dma_start(cst[:, C_ID:C_ID + P], const[:, C_ID:C_ID + P]).then_inc(ident_in, 16)
            for s in range(2):
                c = slice(D // 2 * s, D // 2 * s + D // 2)
                sp.dma_start(stage[:, 0:QT, c], x_prompt[0].rearrange("(t p) d -> p t d", p=P)[:, :, c]).then_inc(x_in[s], 16)
                sp.dma_start(stage[0:DEC, QT, c], x_sample[0][:, c]).then_inc(x_in[s], 16)
            sp.dma_start(cst[:, P:C_ALL], const[:, P:C_ALL]).then_inc(const_in, 16)
            sp.dma_start(spread[:], spread_in).then_inc(const_in, 16)

            def load(slot, n, src, k):
                sp.wait_ge(hi_done, n + 1)
                sp.wait_ge(lo_done, n + 1)
                sp.dma_start(w_raw[:, slot, 0:k, :], src).then_inc(raw_loaded[slot], 16)

            with sp.Fori(0, DEPTH) as l:
                with sp.Fori(0, U_IN // 2) as c2:
                    c = 2 * c2
                    for s in range(2):
                        load(s, U_LAYER * l + c + s,
                             w_in[l].rearrange("(k p) n -> p k n", p=P)[:, :, bass.ds((c + s) * P, P)], KD)

                def load_out(c, s):
                    load(s, U_LAYER * l + FIRST_OUT + c + s,
                         w_out[l].rearrange("(k p) n -> p k n", p=P)[:, :, bass.ds((c + s) * P, P)], KD)

                for s in range(2):
                    load_out(0, s)
                sp.wait_ge(tok_evac, 3 * TT * l + TT)
                sp.dma_start(nv_prompt[l, 0].rearrange("(t p) h d -> p t (h d)", p=P), va[:, 0:QT, :]).then_inc(va_out, 16)
                sp.dma_start(nv_sample[l, 0].rearrange("p h d -> p (h d)"), va[0:DEC, QT, :]).then_inc(va_out, 16)
                def load_mask(h):
                    if h >= RING:
                        sp.wait_ge(decayed, NR * l + TT * (h - RING + 1))
                    sp.dma_start(dmask[:, h % RING, :], decay[h]).then_inc(dmask_loaded[h % RING], 16)

                for h in range(RING):
                    load_mask(h)
                for h in range(HR):
                    sp.wait_ge(st_done, HR * l + h + 1)
                    for i, dst in enumerate((ns_prompt, ns_sample)):
                        sp.dma_start(dst[l, 0, h], st_out[:, h % RING, i, :]).then_inc(st_stored[h % RING], 16)
                    if h + RING < HR:
                        load_mask(h + RING)
                with sp.Fori(1, U_OUT // 2) as c2:
                    c = 2 * c2
                    for s in range(2):
                        load_out(c, s)
                with sp.Fori(0, GROUPS) as g:
                    with sp.Fori(0, FT) as f:
                        for s, w in enumerate((w_gate, w_up)):
                            load(s, U_LAYER * l + U_GROUP * g + 2 * f + (FIRST_FFN + s),
                                 w[l].rearrange("(k p) n -> p k n", p=P)[:, :, bass.ds((g * FT + f) * P, P)], KD)
                    with sp.Fori(0, U_OUT // 2) as c2:
                        c = 2 * c2
                        for s in range(2):
                            load(s, U_LAYER * l + U_GROUP * g + c + (FIRST_FFN + DOWN + s),
                                 w_down[l].rearrange("(g k p) n -> g p k n", g=GROUPS, p=P)[g, :, :, bass.ds((c + s) * P, P)], FT)
            sp.wait_ge(y_copied, TT)
            sp.dma_start(y_prompt[0].rearrange("(t p) d -> p t d", p=P), stage[:, 0:QT, :]).then_inc(y_out, 16)
            sp.dma_start(y_sample[0], stage[0:DEC, QT, :]).then_inc(y_out, 16)
            sp.wait_ge(y_out, 32)
            sp.wait_ge(ka_out, 32 * DEPTH)
            sp.wait_ge(va_out, 32 * DEPTH)
            for s in range(RING):
                sp.wait_ge(st_stored[s], 2 * 16 * HR // RING * DEPTH)

        @block.gpsimd
        def _(pool):
            pool.dma_start(work[0:DEPTH * HA, 2, 0:2 * REL + 1], rel_table.rearrange("l h r -> (l h) r")).then_inc(rel_in, 16)
            pool.wait_ge(line_made, 1)
            pool.dma_start(lines[:, 0:LINE], work[0:DEPTH * HA].rearrange("p a b -> p (a b)")[:, 0:LINE]).then_inc(line_out, 16)
            pool.wait_ge(line_out, 16)
            with pool.Fori(0, DEPTH) as l:
                def load_strip(h):
                    if h >= RING:
                        wait_apart(pool, (biased, NA * l + TT * (h - RING + 1)))
                    window = lines[bass.ds(l * HA + h, 1), 0:STRIP]
                    src = bass.AP(tensor=window.tensor, offset=window.offset, ap=[[1, P], [1, STRIP]])
                    pool.dma_start(strip[:, h % RING, :], src).then_inc(strip_loaded[h % RING], 16)

                def mask_strip(h):
                    wait_apart(pool, (strip_loaded[h % RING], 16 * (HA // RING) * l + 16 * (h // RING + 1)))
                    nc.gpsimd.memset(strip[CHUNK:P, h % RING, STRIP - CHUNK:STRIP], MASKED).then_inc(strip_masked, 1)

                def cache_of(src, p):
                    return src[l, 0, :, 2 * p:2 * p + 2, :].rearrange("(t p) h d -> p t (h d)", p=P)

                def load_cached_keys(p):
                    if p:
                        wait_apart(pool, (kct_ps, HA // 2 * l + p))
                    pool.dma_start(kc_tok[:], cache_of(cache_k, p)).then_inc(kc_loaded, 16)

                def load_cached_values(p):
                    if p >= RING:
                        wait_apart(pool, (pv_done, NA * l + 2 * TT * (p - RING + 1)))
                    pool.dma_start(vc_tok[:, p % RING, :, :], cache_of(cache_v, p)).then_inc(vc_loaded[p % RING], 16)

                wait_apart(pool, (w_used, U_LAYER * l + RING))
                for h in range(RING):
                    load_strip(h)
                pool.dma_start(s_in[:], state_in[l, 0].rearrange("h d e -> d h e")).then_inc(state_loaded, 16)
                for h in range(RING):
                    mask_strip(h)
                wait_apart(pool, (qk_normed, 8 * l + 8))
                load_cached_keys(0)
                for p in range(RING):
                    load_cached_values(p)
                wait_apart(pool, (tok_evac, 3 * TT * l + 2 * TT))
                pool.dma_start(nk_prompt[l, 0].rearrange("(t p) h d -> p t (h d)", p=P), vr[:, 0:QT, :]).then_inc(ka_out, 16)
                pool.dma_start(nk_sample[l, 0].rearrange("p h d -> p (h d)"), vr[0:DEC, QT, :]).then_inc(ka_out, 16)
                load_cached_keys(1)
                for h in range(RING, HA):
                    load_strip(h)
                    mask_strip(h)
                    p = h // 2 + 1
                    if h % 2 and p < HA // 2:
                        load_cached_keys(p)
                        load_cached_values(p)

        @block.scalar
        def _(eng):
            def hi(slot, count, n, k):
                eng.wait_ge(raw_loaded[slot], count)
                eng.wait_ge(w_used, n + 1)
                nc.scalar.activation(w_hi[:, slot, 0:k, :], w_raw[:, slot, 0:k, :], ACT.Copy).then_inc(hi_done, 1)

            def norm_in(l, which, dst, k):
                eng.wait_ge(evacuated, x_count(l, which) + k + 1)
                nc.scalar.activation(dst[:, k, 0, :], x[:, k, :], ACT.Copy,
                                     scale=gain[:, which * KD + k:which * KD + k + 1]).then_inc(h_hi, 1)

            def square_in(l, which, sq, k):
                eng.wait_ge(evacuated, x_count(l, which) + k + 1)
                nc.scalar.activation(sq[:, k, :], x[:, k, :], ACT.Square).then_inc(sq_done, 1)

            def rms_sqrt(l, which):
                eng.wait_ge(rms_stat, 2 * l + which + 1)
                nc.scalar.activation(root[:, 0:QT], ps[:, 6, 0:QT], ACT.Sqrt, scale=1.0 / D,
                                     bias=cst[:, C_EPS:C_EPS + 1])
                nc.scalar.activation(root[0:DEC, QT:TT], ps[0:DEC, 6, QT:TT], ACT.Sqrt, scale=1.0 / D,
                                     bias=cst[0:DEC, C_EPS:C_EPS + 1]).then_inc(rms_root, 1)

            def tok_copy(l, group, dst, t):
                eng.wait_ge(tok_ps, 3 * TT * l + TT * group + t + 1)
                nc.scalar.activation(dst[0:rows(t), t, :], ps[0:rows(t), 4 + t % 4, :], ACT.Copy).then_inc(tok_evac, 1)

            for l in range(DEPTH):
                r = GAINS * l
                eng.dma_start(gain_rows[r:r + KD, :], norm_mix[l].rearrange("(k p) -> k p", p=P)).then_inc(gains_in, 16)
                eng.dma_start(gain_rows[r + KD:r + 2 * KD, :], norm_ffn[l].rearrange("(k p) -> k p", p=P)).then_inc(gains_in, 16)
                for i, src in enumerate((q_norm, k_norm)):
                    for half in range(2):
                        eng.dma_start(gain_rows[r + 2 * KD + i:r + 2 * KD + i + 1, DA * half:DA * half + DA],
                                       src[l:l + 1, :]).then_inc(gains_in, 16)
                eng.dma_start(gain_rows[r + 2 * KD + 2:r + GAINS, :], ret_norm[l].rearrange("(k p) -> k p", p=P)).then_inc(gains_in, 16)
            eng.sem_inc(hi_done, RING)
            with eng.Fori(0, DEPTH) as l:
                def unit_hi(n, k=KD):
                    hi(n % 2, 16 * (U_LAYER // 2) * l + 16 * (n // 2 + 1), U_LAYER * l + n, k)

                unit_hi(0)
                eng.wait_ge(gain_cur, l + 1)
                for k in range(KD):
                    norm_in(l, 0, mix, k)
                unit_hi(1)
                for k in range(KD):
                    square_in(l, 0, mix_sq, k)
                rms_sqrt(l, 0)
                unit_hi(2)
                for n in range(8):
                    if n >= 2:
                        unit_hi(n + 1)
                    eng.wait_ge(evacuated, U_LAYER * l + n + EV + 1)
                    nc.scalar.activation(mix_sq[:, n, :], qk[:, n, :], ACT.Square).then_inc(sq_done, 1)
                for n in range(9, 12):
                    unit_hi(n)
                eng.wait_ge(qk_stat, l + 1)
                nc.scalar.activation(qk_root_col[:, 0:SEQ], ps[0:16, 6, :], ACT.Sqrt, scale=1.0 / DA,
                                     bias=cst[0:16, C_EPS:C_EPS + 1])
                nc.scalar.activation(qk_root_col[:, SEQ:TOK], ps[0:16, 7, 0:DEC], ACT.Sqrt, scale=1.0 / DA,
                                     bias=cst[0:16, C_EPS:C_EPS + 1]).then_inc(qk_root, 1)
                unit_hi(12)

                def half_unit(i):
                    if i % 2 == 0:
                        unit_hi(FIRST_HALF + i // 2 + 1)

                for i in range(PRE):
                    half_unit(i)
                    if i == 0:
                        for t in range(TT):
                            tok_copy(l, 0, va, t)
                for t in range(TT):
                    tok_copy(l, 1, vr, t)

                def cache_keys(p):
                    eng.wait_ge(kct_ps, HA // 2 * l + p + 1)
                    nc.scalar.activation(kc_t[:], ps[:, 3, :], ACT.Copy).then_inc(kct_evac, 1)

                def attn_out(p):
                    eng.wait_ge(ot_ps, HA // 2 * l + p + 1)
                    nc.scalar.activation(q_rev[:, p, 0:SEQ].rearrange("p (t q) -> p t q", t=QT),
                                         backwards(ps[:, 2, :].rearrange("p (t q) -> p t q", t=QT), P), ACT.Copy)
                    nc.scalar.activation(q_rev[:, p, SEQ:TOK], backwards(ps[:, 3, 0:DEC], DEC), ACT.Copy).then_inc(ot_out, 1)

                for k in range(STEPS_A + 1):
                    for i in range(halves_before(k), halves_before(k + 1)):
                        half_unit(i)
                    if k >= 14 and (k - 14) % 10 == 0:
                        attn_out((k - 14) // 10)
                    if k % 10 == 0 and k < NA:
                        cache_keys(k // 10)
                    if k >= NA:
                        continue
                    h, t = ITEMS_A[k]
                    r, w = rows(t), P * (t + 1) if t < QT else TOK
                    if k >= 2 * TT:
                        eng.wait_ge(sums_inv, HA * l + h - 1)
                    eng.wait_ge(biased, NA * l + k + 1)
                    nc.scalar.activation(work[0:r, k % 3, 0:w], work[0:r, k % 3, 0:w], ACT.Exp, scale=-1.0,
                                         bias=least[0:r, k % 4:k % 4 + 1],
                                         accum_out=sums[0:r, h % 2, t:t + 1]).then_inc(exped, 1)
                eng.wait_ge(ka_out, 32 * l + 32)
                for t in range(TT):
                    tok_copy(l, 2, vr, t)

                def attn_hi(p):
                    eng.wait_ge(w_used, U_LAYER * l + U_IN + RING)
                    eng.wait_ge(ot_out, HA // 2 * l + p + 1)
                    nc.scalar.activation(mix[:, p, 0, :], q_rev[:, p, :], ACT.Copy).then_inc(ot_hi, 1)

                for h in range(HR + 2):
                    if h == 1:
                        for n in range(HR):
                            eng.wait_ge(evacuated, U_LAYER * l + 3 * HR + FIRST_HALF + n + EV + 1)
                            nc.scalar.activation(gate[:, n, :], gate[:, n, :], ACT.Silu).then_inc(g_silu, 1)
                    if h < HR:
                        eng.wait_ge(kd_ps, HR * l + h + 1)
                        if h >= RING:
                            eng.wait_ge(st_ps, HR * l + h - 1)
                        for t in range(TT):
                            bank, c = (0, P * t) if t < QT else (1, 0)
                            last = nc.scalar.activation(kd_tok[0:rows(t), h % 2, t, :], ps[0:rows(t), bank, c:c + P], ACT.Copy,
                                                        scale=cst[0:rows(t), C_KDEC + HR * t + h:C_KDEC + HR * t + h + 1])
                        last.then_inc(kd_evac, 1)
                        attn_hi(h)
                    if 1 <= h <= HR:
                        eng.wait_ge(bn_done, HR * l + h)
                        nc.scalar.activation(gnr[:, 0:QT], mv[:, 0:QT, 1], ACT.Sqrt, bias=cst[:, C_EPS + 1:C_EPS + 2])
                        nc.scalar.activation(gnr[0:DEC, QT:TT], mv[0:DEC, QT:TT, 1], ACT.Sqrt,
                                             bias=cst[0:DEC, C_EPS + 1:C_EPS + 2]).then_inc(gn_root, 1)
                        eng.wait_ge(or_done, HR * l + h)
                        nc.scalar.activation(mix[:, 3 + h, 0, :], gate[:, h - 1, :], ACT.Copy).then_inc(or_hi, 1)
                eng.wait_ge(va_out, 32 * l + 32)
                for s in range(RING):
                    eng.wait_ge(st_stored[s], 2 * 16 * HR // RING * l + 2 * 16 * HR // RING)
                for c in range(U_OUT):
                    if c + 1 < U_OUT:
                        unit_hi(FIRST_OUT + c + 1)
                    norm_in(l, 1, ffn, c)
                    square_in(l, 1, ffn_sq, c)
                for g in range(GROUPS):
                    def group_hi(i, s, k=KD):
                        hi(s, 8 * U_LAYER * l + 8 * i + (8 * (FIRST_FFN + U_GROUP * g - s) + 16),
                           U_LAYER * l + i + (FIRST_FFN + U_GROUP * g), k)

                    def silu(f):
                        eng.wait_ge(evacuated, U_LAYER * l + 2 * f + (FIRST_FFN + U_GROUP * g + EV + 1))
                        nc.scalar.activation(work[:, 0, :], work[:, 0, :], ACT.Silu).then_inc(gate_silu, 1)

                    def act_high(f):
                        wait_apart(eng, (act_f, GROUPS * FT * l + f + (FT * g + 1)))
                        nc.scalar.activation(act[:, bass.ds(f, 1), 0, :].rearrange("p a b -> p (a b)"), work[:, 2, :],
                                             ACT.Copy).then_inc(act_hi, 1)

                    def gate_up(f, early=False):
                        if early:
                            group_hi(2 * f + 2, 0)
                        silu(f)
                        if not early:
                            group_hi(2 * f + 2, 0)
                        act_high(f)
                        group_hi(2 * f + 3, 1)

                    if g == 0:
                        group_hi(0, 0)
                        group_hi(1, 1)
                        rms_sqrt(l, 1)
                    gate_up(0, early=g == 0)
                    with eng.Fori(1, FT - 1) as f:
                        gate_up(f)
                    silu(FT - 1)
                    group_hi(DOWN, 0, FT)
                    act_high(FT - 1)
                    group_hi(DOWN + 1, 1, FT)
                    with eng.Fori(1, U_OUT // 2) as c2:
                        c = 2 * c2
                        for s in range(2):
                            group_hi(c + (DOWN + s), s, FT)
                    if g + 1 < GROUPS:
                        group_hi(U_GROUP, 0)
                        group_hi(U_GROUP + 1, 1)
            for t in range(TT):
                eng.wait_ge(y_ps, t + 1)
                nc.scalar.activation(stage[0:rows(t), t, :].rearrange("p (a b) -> p a b", a=2),
                                     ps[0:rows(t), 2 * (t % 2):2 * (t % 2) + 2, :], ACT.Copy).then_inc(y_copied, 1)

        @block.vector
        def _(dve):
            def lo(slot, n, k=KD):
                dve.wait_ge(hi_done, n + RING + 1)
                nc.vector.tensor_tensor(w_lo[:, slot, 0:k, :], w_raw[:, slot, 0:k, :],
                                        w_hi[:, slot, 0:k, :].bitcast(F32), ALU.subtract).then_inc(lo_done, 1)

            def projected(n):
                dve.wait_ge(w_used, n + RING + 1)

            def scaled(n, s, dst):
                projected(n)
                nc.vector.tensor_tensor(halves(dst), dense(s), halves(row_f[:]), ALU.mult).then_inc(evacuated, 1)

            def norm_lo(l, which, dst, k):
                dve.wait_ge(h_hi, 2 * KD * l + which * KD + k + 1)
                nc.vector.scalar_tensor_tensor(dst[:, k, 1, :], x[:, k, :], gain[:, which * KD + k:which * KD + k + 1],
                                               dst[:, k, 0, :].bitcast(F32), ALU.mult, ALU.subtract).then_inc(h_lo, 1)

            def add_square(l, which, sq, k):
                dve.wait_ge(sq_done, 3 * KD * l + 2 * KD * which + k + 1)
                if k > 1:
                    dve.wait_ge(sq_sum, 2 * (KD - 1) * l + (KD - 1) * which + k - 1)
                nc.vector.tensor_tensor(sq[:, 0, :], sq[:, 0, :], sq[:, k, :], ALU.add).then_inc(sq_sum, 1)

            def rms_invert(l, which):
                dve.wait_ge(rms_root, 2 * l + which + 1)
                nc.vector.reciprocal(inv[:, 0:QT], root[:, 0:QT])
                nc.vector.reciprocal(inv[0:DEC, QT:TT], root[0:DEC, QT:TT]).then_inc(rms_inv, 1)

            def rms_rows(l, which):
                dve.wait_ge(rms_bcast, 2 * l + which + 1)
                nc.vector.tensor_copy(row_f[:, 0:SEQ], ps[:, 7, :])
                nc.vector.tensor_copy(row_f[:, SEQ:TOK], ps[:, 6, P:P + DEC]).then_inc(rms_row, 1)
                dve.wait_ge(rms_row, 2 * l + which + 1)

            dve.sem_inc(lo_done, RING)
            dve.sem_inc(evacuated, RING)
            for k in range(KD):
                b = 4 + 2 * (k % 2)
                dve.wait_ge(x_ps, k + 1)
                nc.vector.tensor_copy(x[:, k, 0:SEQ], ps[:, b, :])
                nc.vector.tensor_copy(x[:, k, SEQ:TOK], ps[:, b + 1, 0:DEC]).then_inc(evacuated, 1)
            dve.wait_ge(gains_ps, 1)
            cols = ps[:, 0, 0:DEPTH * GAINS].rearrange("p (l g) -> p l g", l=DEPTH)
            nc.vector.tensor_copy(gains[:], cols).then_inc(gains_set, 1)
            dve.wait_ge(gains_set, 1)
            nc.vector.tensor_scalar(gains[:, :, 2 * KD], cols[:, :, 2 * KD], -(DA ** -0.5), None, ALU.mult).then_inc(gains_set, 1)
            dve.wait_ge(rel_in, 16)
            line = work[0:DEPTH * HA].rearrange("p a b -> p (a b)")
            far = LINE - (2 * REL - 1)
            nc.vector.tensor_scalar(line[:, 0:far], line[:, 2 * TOK + 2 * REL:2 * TOK + 2 * REL + 1].to_broadcast([DEPTH * HA, far]),
                                    -1.0, None, ALU.mult)
            nc.vector.tensor_scalar(line[:, far:LINE], backwards(line[:, 2 * TOK + 1:2 * TOK + 2 * REL], 2 * REL - 1),
                                    -1.0, None, ALU.mult).then_inc(line_made, 1)
            dve.wait_ge(gains_set, 2)
            dve.wait_ge(line_out, 16)
            with dve.Fori(0, DEPTH) as l:
                def unit_lo(n, k=KD):
                    lo(n % 2, U_LAYER * l + n, k)

                dve.wait_ge(const_in, 32)
                nc.vector.tensor_copy(gain[:], gains[:, bass.ds(l, 1), :].rearrange("p a b -> p (a b)")).then_inc(gain_cur, 1)
                dve.wait_ge(gain_cur, l + 1)
                unit_lo(0)
                for k in range(KD):
                    norm_lo(l, 0, mix, k)
                unit_lo(1)
                for k in range(1, KD):
                    add_square(l, 0, mix_sq, k)
                rms_invert(l, 0)
                unit_lo(2)
                rms_rows(l, 0)
                for n in range(2):
                    scaled(U_LAYER * l + n, n % 2, qk[:, n, :])
                unit_lo(3)
                projected(U_LAYER * l + 2)
                nc.vector.tensor_tensor(halves(qk[:, 2, :]), ps[:, 4:6, 0:HALF], halves(row_f[:]), ALU.mult).then_inc(evacuated, 1)
                for dst, table in ((rcos, cos), (rsin, sin)):
                    nc.vector.tensor_tensor(dst[:, 0:SEQ], row_f[:, 0:SEQ], table, ALU.mult)
                    last = nc.vector.tensor_tensor(dst[:, SEQ:TOK], row_f[:, SEQ:TOK], table[:, 0:DEC], ALU.mult)
                last.then_inc(rope_rows, 1)
                for n in range(3, 12):
                    if n < 11:
                        unit_lo(n + 1)
                    if n == 10:
                        dve.wait_ge(qk_root, l + 1)
                        nc.vector.reciprocal(qk_col, qk_root_col).then_inc(qk_inv, 1)
                    scaled(U_LAYER * l + n, n % 2, qk[:, n, :] if n < 8 else vt[:, n - 8, :])
                unit_lo(12)

                def half_unit(i):
                    n, half = FIRST_HALF + i // 2, i % 2
                    c = slice(HALF * half, HALF * half + HALF)
                    bank = ps[:, half, 0:HALF]
                    if half == 0:
                        unit_lo(n + 1)
                        dve.wait_ge(half_ps, (U_IN - FIRST_HALF) * l + n - FIRST_HALF + 1)
                    else:
                        projected(U_LAYER * l + n)
                    out = evacuated if half else half_out
                    if n < FIRST_HALF + 8:
                        if i >= 2:
                            dve.wait_ge(ret_ready, 16 * l + i - 1)
                        dst, H = qk_ret[:, n - FIRST_HALF, c], P // 2
                        nc.vector.tensor_tensor(dst, bank, rcos[:, c], ALU.mult)
                        nc.vector.tensor_tensor(vt[0:H, 0, c], bank[H:P, :], rsin[H:P, c], ALU.mult)
                        nc.vector.tensor_tensor(vt[H:P, 0, c], bank[0:H, :], rsin[0:H, c], ALU.mult).then_inc(out, 1)
                        dve.wait_ge(*(out, U_LAYER * l + n + EV + 1) if half else (out, (U_IN - FIRST_HALF) * l + n - FIRST_HALF + 1))
                        nc.vector.tensor_tensor(dst, dst, vt[:, 0, c], ALU.add).then_inc(ret_ready, 1)
                    else:
                        j = n - FIRST_HALF - 8
                        if i == 16 + half:
                            dve.wait_ge(ret_ready, 16 * l + 16)
                        dst = vt[:, j, c] if j < 4 else gate[:, j - 4, c]
                        nc.vector.tensor_tensor(dst, bank, row_f[:, c], ALU.mult).then_inc(out, 1)

                def qk_normalise(i):
                    j, b = NORM_ORDER[i], 4 + 2 * (i % 2)
                    dve.wait_ge(qk_bcast, 8 * l + i + 1)
                    g = gain[:, 2 * KD + j // 4:2 * KD + j // 4 + 1]
                    src = (qk[:, j, 0:SEQ], qk[:, j, SEQ:TOK])
                    if j < 4:
                        tiles = q_rev[:, j, 0:SEQ].rearrange("p (t q) -> p t q", t=QT)
                        nc.vector.scalar_tensor_tensor(backwards(tiles, P), src[0].rearrange("p (t q) -> p t q", t=QT), g,
                                                       ps[:, b, :].rearrange("p (t q) -> p t q", t=QT), ALU.mult, ALU.mult)
                        dst = backwards(q_rev[:, j, SEQ:TOK], DEC)
                    else:
                        nc.vector.scalar_tensor_tensor(src[0], src[0], g, ps[:, b, :], ALU.mult, ALU.mult)
                        dst = src[1]
                    nc.vector.scalar_tensor_tensor(dst, src[1], g, ps[:, b + 1, 0:DEC], ALU.mult, ALU.mult).then_inc(qk_normed, 1)

                dve.wait_ge(rope_rows, l + 1)
                for i in range(PRE):
                    if i == 0:
                        dve.wait_ge(tok_ps, 3 * TT * l + TT)
                    half_unit(i)
                    if 1 <= i <= 4:
                        qk_normalise(2 * i - 2)
                        qk_normalise(2 * i - 1)

                def add_bias(k):
                    h, t = ITEMS_A[k]
                    r, w = rows(t), P * (t + 1) if t < QT else TOK
                    waits = [(s_ps, NA * l + k + 1)]
                    if t == 0:
                        waits.append((strip_masked, HA * l + h + 1))
                    if k >= 3:
                        waits.append((pt_ps, NA * l + k - 2))
                    wait_apart(dve, *waits)
                    if t < QT:
                        src, bias = ps[:, 2 + t % 2, 0:w], strip[:, h % RING, STRIP - w:STRIP]
                        dst = work[:, k % 3, 0:w]
                    else:
                        src, bias = ps[0:r, 2:4, 0:HALF], halves(strip[P - DEC:P, h % RING, 0:TOK])
                        dst = halves(work[0:r, k % 3, :])
                    nc.vector.tensor_tensor_reduce(out=dst, in0=src, in1=bias, scale=1.0, scalar=3e38, op0=ALU.add,
                                                   op1=ALU.min, accum_out=least[0:r, k % 4:k % 4 + 1]).then_inc(biased, 1)

                def probs_out(k):
                    h, t = ITEMS_A[k]
                    dve.wait_ge(pt_ps, NA * l + k + 1)
                    if k >= 2:
                        dve.wait_ge(pv_done, NA * l + k - 1)
                    if t < QT:
                        nc.vector.tensor_copy(pt[:, k % 2, 0:P * (t + 1)], ps[:, 4 + k % 2, 0:P * (t + 1)]).then_inc(pt_evac, 1)
                    else:
                        c = QT * DEC
                        nc.vector.tensor_copy(pt[:, k % 2, 0:c], ps[:, 4 + k % 2, 0:c])
                        nc.vector.tensor_copy(pt[0:DEC, k % 2, c:c + DEC], ps[0:DEC, 4 + k % 2, c:c + DEC]).then_inc(pt_evac, 1)

                def head_normalise(h):
                    dve.wait_ge(exped, NA * l + TT * (h + 1))
                    nc.vector.reciprocal(rsum[:, h % 2, 0:QT], sums[:, h % 2, 0:QT])
                    nc.vector.reciprocal(rsum[0:DEC, h % 2, QT:TT], sums[0:DEC, h % 2, QT:TT]).then_inc(sums_inv, 1)
                    dve.wait_ge(sums_inv, HA * l + h + 1)
                    dve.wait_ge(pv_done, NA * l + TT * (h + 1))
                    p, c = h // 2, DA * (h % 2)
                    if p >= RING:
                        dve.wait_ge(ot_ps, HA // 2 * l + p - 1)
                    nc.vector.tensor_tensor(o_tok[:, p % 2, 0:QT, c:c + DA],
                                            ps[:, 6 + h % 2, 0:QT * DA].rearrange("p (t d) -> p t d", t=QT),
                                            rsum[:, h % 2, 0:QT].unsqueeze(2).to_broadcast([P, QT, DA]), ALU.mult)
                    nc.vector.tensor_scalar(o_tok[0:DEC, p % 2, QT, c:c + DA], ps[0:DEC, 6 + h % 2, QT * DA:TT * DA],
                                            rsum[0:DEC, h % 2, QT:TT], None, ALU.mult).then_inc(o_normed, 1)

                def attn_lo(p):
                    dve.wait_ge(ot_hi, HA // 2 * l + p + 1)
                    nc.vector.tensor_tensor(mix[:, p, 1, :], q_rev[:, p, :], mix[:, p, 0, :].bitcast(F32), ALU.subtract).then_inc(ot_lo, 1)

                for k in range(STEPS_A):
                    for i in range(halves_before(k), halves_before(k + 1)):
                        half_unit(i)
                    if k < NA:
                        add_bias(k)
                    if k >= 8 and (k - 8) % 5 == 0 and (k - 8) // 5 < HA:
                        head_normalise((k - 8) // 5)
                    if 0 <= k - 2 < NA:
                        probs_out(k - 2)

                def mask_scores(k):
                    h, t = ITEMS_R[k]
                    r, w = rows(t), P * (t + 1) if t < QT else DEC
                    c = SEQ - w if t < QT else SEQ - P
                    dve.wait_ge(r_ps, NR * l + k + 1)
                    if t == 0:
                        dve.wait_ge(dmask_loaded[h % RING], 16 * HR // RING * l + 16 * (h // RING + 1))
                    if k >= 3:
                        dve.wait_ge(sv_done, NR * l + k - 2)
                    nc.vector.tensor_tensor(work[0:r, k % 3, 0:w], ps[0:r, 2 + k % 2, 0:w], dmask[0:r, h % RING, c:c + w],
                                            ALU.mult).then_inc(decayed, 1)

                def query_decay(h):
                    dve.wait_ge(ret_ready, 16 * l + 16)
                    if h >= RING:
                        dve.wait_ge(sv_done, NR * l + TT * (h - RING + 1))
                    nc.vector.tensor_tensor(qd[:, h % RING, :], qk_ret[:, h, SEQ:TOK],
                                            cst[:, C_QDEC + DEC * h:C_QDEC + DEC * h + DEC], ALU.mult).then_inc(qd_ready, 1)

                def ret_tile(h, t):
                    return ps[:, 4 + h % 2, P * t:P * t + P] if t < QT else ps[0:DEC, 6 + h % 2, 0:P]

                def group_stats(h):
                    dve.wait_ge(sv_done, NR * l + TT * (h + 1))
                    for t in range(TT):
                        last = nc.vector.bn_stats(bn[0:rows(t), t, :], ret_tile(h, t))
                    last.then_inc(bn_parts, 1)
                    wait_apart(dve, (bn_parts, HR * l + h + 1))
                    for t in range(TT):
                        last = nc.vector.bn_aggr(mv[0:rows(t), t, :], bn[0:rows(t), t, :])
                    last.then_inc(bn_done, 1)

                def group_normalise(h):
                    dve.wait_ge(gn_root, HR * l + h + 1)
                    nc.vector.reciprocal(gni[:, 0:QT], gnr[:, 0:QT])
                    nc.vector.reciprocal(gni[0:DEC, QT:TT], gnr[0:DEC, QT:TT]).then_inc(gn_inv, 1)
                    dve.wait_ge(gn_inv, HR * l + h + 1)
                    if h >= RING:
                        dve.wait_ge(or_ps, HR * l + h - 1)
                    for t in range(TT):
                        last = nc.vector.tensor_scalar(o_tok[0:rows(t), h % 2, t, :], ret_tile(h, t), mv[0:rows(t), t, 0:1],
                                                       gni[0:rows(t), t:t + 1], ALU.subtract, ALU.mult)
                    last.then_inc(gn_normed, 1)

                def gated(h):
                    dve.wait_ge(or_ps, HR * l + h + 1)
                    dve.wait_ge(g_silu, HR * l + HR)
                    g = gain[:, 2 * KD + 2 + h:2 * KD + 3 + h]
                    nc.vector.scalar_tensor_tensor(gate[:, h, 0:SEQ], ps[:, 0, :], g, gate[:, h, 0:SEQ], ALU.mult, ALU.mult)
                    nc.vector.scalar_tensor_tensor(gate[:, h, SEQ:TOK], ps[:, 1, 0:DEC], g, gate[:, h, SEQ:TOK],
                                                   ALU.mult, ALU.mult).then_inc(or_done, 1)

                def gated_lo(h):
                    dve.wait_ge(or_hi, HR * l + h + 1)
                    nc.vector.tensor_tensor(mix[:, 4 + h, 1, :], gate[:, h, :], mix[:, 4 + h, 0, :].bitcast(F32), ALU.subtract).then_inc(or_lo, 1)

                def states(h):
                    H = P // 2
                    dve.wait_ge(st_ps, HR * l + h + 1)
                    nc.vector.tensor_copy(st_tmp[:, 0, :], ps[:, 1, P:2 * P])
                    nc.vector.scalar_tensor_tensor(st_tmp[:, 1, :], s_in[:, h, :], float(gamma(h) ** DEC), ps[:, 1, 2 * P:3 * P],
                                                   ALU.mult, ALU.add).then_inc(st_sum, 1)
                    dve.wait_ge(st_sum, HR * l + h + 1)
                    if h >= RING:
                        dve.wait_ge(st_stored[h % RING], 32 * (HR // RING) * l + 32 * (h // RING))
                    for i in range(2):
                        c = C_ROT + 2 * i + 1
                        nc.vector.tensor_scalar(st_swap[0:H, i, :], st_tmp[H:P, i, :], cst[H:P, c:c + 1], None, ALU.mult)
                        last = nc.vector.tensor_scalar(st_swap[H:P, i, :], st_tmp[0:H, i, :], cst[0:H, c:c + 1], None, ALU.mult)
                    last.then_inc(st_swapped, 1)
                    dve.wait_ge(st_swapped, HR * l + h + 1)
                    for i in range(2):
                        c = C_ROT + 2 * i
                        last = nc.vector.scalar_tensor_tensor(st_out[:, h % RING, i, :], st_tmp[:, i, :], cst[:, c:c + 1],
                                                              st_swap[:, i, :], ALU.mult, ALU.add)
                    last.then_inc(st_done, 1)

                dve.wait_ge(state_loaded, 16 * l + 16)
                dve.wait_ge(pt_ps, NA * l + NA)
                for k in range(NR + 7):
                    h, i = k // TT, k % TT
                    if i == 0 and h >= 2:
                        gated(h - 2)
                    if i == 0 and h < HR:
                        query_decay(h)
                    if k < NR:
                        mask_scores(k)
                    if i == 1 and h >= 2:
                        gated_lo(h - 2)
                    if i == 1 and h < HR:
                        attn_lo(h)
                    if i == 2 and 1 <= h <= HR:
                        group_stats(h - 1)
                    if i == 3 and 1 <= h <= HR:
                        group_normalise(h - 1)
                    if i == 4 and h < HR:
                        states(h)

                def add_to_x(n, s, c):
                    projected(n)
                    xc = x[:, bass.ds(c, 1), :].rearrange("p o (a b) -> p (o a) b", a=2)
                    nc.vector.tensor_tensor(xc, dense(s), xc, ALU.add).then_inc(evacuated, 1)

                for c in range(U_OUT):
                    if c + 1 < U_OUT:
                        unit_lo(FIRST_OUT + c + 1)
                    add_to_x(U_LAYER * l + FIRST_OUT + c, c % 2, c)
                    if c:
                        norm_lo(l, 1, ffn, c - 1)
                    if c > 1:
                        add_square(l, 1, ffn_sq, c - 1)
                unit_lo(FIRST_FFN)
                norm_lo(l, 1, ffn, KD - 1)
                add_square(l, 1, ffn_sq, KD - 1)
                for g in range(GROUPS):
                    first = FIRST_FFN + U_GROUP * g

                    def group_lo(i, s, k=KD):
                        lo(s, U_LAYER * l + i + first, k)

                    def up_out(f):
                        scaled(U_LAYER * l + 2 * f + (first + 1), 1, work[:, 1, :])

                    def product(f):
                        dve.wait_ge(gate_silu, GROUPS * FT * l + f + (FT * g + 1))
                        dve.wait_ge(evacuated, U_LAYER * l + 2 * f + (first + 1 + EV + 1))
                        nc.vector.tensor_tensor(work[:, 2, :], work[:, 0, :], work[:, 1, :], ALU.mult).then_inc(act_f, 1)

                    def act_low(f):
                        dve.wait_ge(act_hi, GROUPS * FT * l + f + (FT * g + 1))
                        a = act[:, bass.ds(f, 1), :, :]
                        nc.vector.tensor_tensor(a[:, :, 1, :].rearrange("p a b -> p (a b)"), work[:, 2, :],
                                                a[:, :, 0, :].rearrange("p a b -> p (a b)").bitcast(F32), ALU.subtract).then_inc(act_lo, 1)

                    group_lo(1, 1)
                    if g == 0:
                        rms_invert(l, 1)
                        group_lo(2, 0)
                        rms_rows(l, 1)
                    scaled(U_LAYER * l + first, 0, work[:, 0, :])
                    if g:
                        group_lo(2, 0)
                    up_out(0)
                    product(0)
                    with dve.Fori(1, FT - 1) as f:
                        group_lo(2 * f + 1, 1)
                        scaled(U_LAYER * l + 2 * f + first, 0, work[:, 0, :])
                        act_low(f - 1)
                        group_lo(2 * f + 2, 0)
                        up_out(f)
                        product(f)
                    f = FT - 1
                    group_lo(2 * f + 1, 1)
                    scaled(U_LAYER * l + 2 * f + first, 0, work[:, 0, :])
                    act_low(f - 1)
                    group_lo(DOWN, 0, FT)
                    up_out(f)
                    product(f)
                    act_low(f)
                    with dve.Fori(0, (U_OUT - 2) // 2) as c2:
                        c = 2 * c2
                        for s in range(2):
                            group_lo(c + (DOWN + s + 1), 1 - s, FT)
                            add_to_x(U_LAYER * l + c + (first + DOWN + s), s, c + s)
                    group_lo(DOWN + U_OUT - 1, 1, FT)
                    add_to_x(U_LAYER * l + first + DOWN + U_OUT - 2, 0, U_OUT - 2)
                    if g + 1 < GROUPS:
                        group_lo(U_GROUP, 0)
                    add_to_x(U_LAYER * l + first + DOWN + U_OUT - 1, 1, U_OUT - 1)

        @block.tensor
        def _(pe):
            PASSES = ((w_hi, 0), (w_hi, 1), (w_lo, 0))

            def unit(n, slot, nk, src, ready=None, bank=None, midway=None):
                pe.wait_ge(lo_done, n + RING + 1)
                if bank is None:
                    pe.wait_ge(evacuated, n + EV - 1)
                    bank = 2 * slot
                for k in range(nk):
                    if ready:
                        ready(k)
                    if midway and k == nk // 2:
                        midway()
                    for i, (w, part) in enumerate(PASSES):
                        for half in range(2):
                            last = nc.tensor.matmul(ps[:, bank + half, 0:HALF], w[:, slot, k, :],
                                                    src[:, k, part, HALF * half:HALF * half + HALF],
                                                    start=k == 0 and i == 0, stop=k == nk - 1 and i == 2)
                last.then_inc(w_used, 1)

            def rms_sums(l, which, sq):
                pe.wait_ge(sq_sum, (KD - 1) * (2 * l + which + 1))
                for t in range(TT):
                    last = nc.tensor.matmul(ps[0:rows(t), 6, t:t + 1], sq[:, 0, tok(t)], cst[:, C_ONE:C_ONE + 1],
                                            start=True, stop=True)
                last.then_inc(rms_stat, 1)

            def rms_spread(l, which):
                pe.wait_ge(rms_inv, 2 * l + which + 1)
                for t in range(TT):
                    r = rows(t)
                    dst = ps[:, 7, tok(t)] if t < QT else ps[:, 6, P:P + DEC]
                    last = nc.tensor.transpose(dst, inv[0:r, t:t + 1].to_broadcast([r, P]), ident[0:r, 0:r])
                last.then_inc(rms_bcast, 1)

            def to_tokens(l, group, tiles):
                for t in range(TT):
                    if t == 4:
                        wait_apart(pe, (tok_evac, 3 * TT * l + TT * group + 1))
                    for j in range(4):
                        last = nc.tensor.transpose(ps[0:rows(t), 4 + t % 4, P * j:P * j + P], tiles[:, j, tok(t)], ident)
                    last.then_inc(tok_ps, 1)

            pe.sem_inc(w_used, RING)
            pe.wait_ge(ident_in, 16)
            for k in range(KD):
                b = 4 + 2 * (k % 2)
                if k % 4 == 0:
                    pe.wait_ge(x_in[k // 4], 32)
                if k >= 2:
                    pe.wait_ge(evacuated, RING + k - 1)
                for t in range(TT):
                    r = rows(t)
                    dst = ps[:, b, tok(t)] if t < QT else ps[:, b + 1, 0:DEC]
                    last = nc.tensor.transpose(dst, stage[0:r, t, P * k:P * k + P], ident[0:r, 0:r])
                last.then_inc(x_ps, 1)
            pe.wait_ge(gains_in, 16 * 7 * DEPTH)
            n = DEPTH * GAINS
            nc.tensor.transpose(ps[:, 0, 0:n], gain_rows, ident[0:n, 0:n]).then_inc(gains_ps, 1)
            pe.wait_ge(gains_set, 2)
            pe.wait_ge(const_in, 32)
            with pe.Fori(0, DEPTH) as l:
                def in_unit(n, slot, ready=None):
                    unit(U_LAYER * l + n, slot, KD, mix, ready)

                def mix_ready(k):
                    pe.wait_ge(h_lo, 2 * KD * l + k + 1)

                def in_units(a, b):
                    with pe.Fori(a // 2, b // 2) as n2:
                        n = 2 * n2
                        for s in range(2):
                            in_unit(n + s, s)

                in_unit(0, 0, mix_ready)
                in_unit(1, 1)
                rms_sums(l, 0, mix_sq)
                unit(U_LAYER * l + 2, 0, KD, mix, bank=4, midway=lambda: rms_spread(l, 0))
                in_unit(3, 1)
                in_units(4, 10)
                pe.wait_ge(sq_done, 3 * KD * l + 2 * KD)
                for j in range(8):
                    sel = cst[:, C_SEL + 16 * j:C_SEL + 16 * j + 16]
                    nc.tensor.matmul(ps[0:16, 6, :], sel, mix_sq[:, j, 0:SEQ], start=j == 0, stop=j == 7)
                    last = nc.tensor.matmul(ps[0:16, 7, 0:DEC], sel, mix_sq[:, j, SEQ:TOK], start=j == 0, stop=j == 7)
                last.then_inc(qk_stat, 1)
                in_units(10, 12)

                def half_unit(i):
                    n, half = FIRST_HALF + i // 2, i % 2
                    if half == 0:
                        pe.wait_ge(lo_done, U_LAYER * l + n + RING + 1)
                    if i < 2:
                        pe.wait_ge(evacuated, U_LAYER * l + n - 2 + EV + 1)
                    elif half == 0:
                        pe.wait_ge(half_out, (U_IN - FIRST_HALF) * l + n - FIRST_HALF)
                    else:
                        pe.wait_ge(evacuated, U_LAYER * l + n - 1 + EV + 1)
                    for k in range(KD):
                        for j, (w, part) in enumerate(PASSES):
                            last = nc.tensor.matmul(ps[:, half, 0:HALF], w[:, n % 2, k, :],
                                                    mix[:, k, part, HALF * half:HALF * half + HALF],
                                                    start=k == 0 and j == 0, stop=k == KD - 1 and j == 2)
                    last.then_inc(w_used if half else half_ps, 1)

                def spread_roots(i):
                    j, b = NORM_ORDER[i], 4 + 2 * (i % 2)
                    if i >= 2:
                        pe.wait_ge(qk_normed, 8 * l + i - 1)
                    nc.tensor.matmul(ps[:, b, :], spread[:, P * j:P * j + P], qk_col[:, 0:SEQ], start=True, stop=True)
                    nc.tensor.matmul(ps[:, b + 1, 0:DEC], spread[:, P * j:P * j + P], qk_col[:, SEQ:TOK],
                                     start=True, stop=True).then_inc(qk_bcast, 1)

                for i in range(PRE):
                    half_unit(i)
                    if i == 0:
                        pe.wait_ge(evacuated, U_LAYER * l + 11 + EV + 1)
                        pe.wait_ge(qk_root, l + 1)
                        to_tokens(l, 0, vt)
                    elif i <= 4:
                        if i == 1:
                            pe.wait_ge(qk_inv, l + 1)
                            pe.wait_ge(tok_evac, 3 * TT * l + TT)
                        spread_roots(2 * i - 2)
                        spread_roots(2 * i - 1)
                pe.wait_ge(qk_normed, 8 * l + 8)
                to_tokens(l, 1, qk[:, 4:8, :])

                def cache_keys(p):
                    pe.wait_ge(kc_loaded, 16 * (HA // 2) * l + 16 * (p + 1))
                    if p:
                        pe.wait_ge(biased, NA * l + 2 * TT * p)
                    for t in range(QT):
                        last = nc.tensor.transpose(ps[:, 3, P * t:P * t + P], kc_tok[:, t, :], ident)
                    last.then_inc(kct_ps, 1)

                def scores(k):
                    h, t = ITEMS_A[k]
                    hr = head_rows(h)
                    q, keys = q_rev[hr, h // 2, tok(t)], qk[hr, 4 + h // 2, :]
                    waits = []
                    if t in (0, QT) and k:
                        waits.append((biased, NA * l + k))
                    elif k >= 2:
                        waits.append((biased, NA * l + k - 1))
                    if t == 1 and h % 2 == 0:
                        waits.append((kct_evac, HA // 2 * l + h // 2 + 1))
                    if t == QT and h and h % 2 == 0:
                        waits.append((ot_out, HA // 2 * l + h // 2))
                    if t < QT:
                        for semaphore, count in waits:
                            pe.wait_ge(semaphore, count)
                        nc.tensor.matmul(ps[:, 2 + t % 2, 0:P * (t + 1)], q, keys[:, 0:P * (t + 1)],
                                         start=True, stop=True).then_inc(s_ps, 1)
                    else:
                        wait_apart(pe, *waits)
                        cached = kc_t[hr, :]
                        nc.tensor.matmul(ps[0:DEC, 2, 0:HALF], q, cached[:, 0:HALF], start=True, stop=True)
                        nc.tensor.matmul(ps[0:DEC, 3, 0:SEQ - HALF], q, cached[:, HALF:SEQ], start=True, stop=True)
                        nc.tensor.matmul(ps[0:DEC, 3, SEQ - HALF:HALF], q, keys[:, SEQ:TOK],
                                         start=True, stop=True).then_inc(s_ps, 1)

                def probs(k):
                    h, t = ITEMS_A[k]
                    waits = [(exped, NA * l + k + 1)]
                    if k >= 2:
                        waits.append((pt_evac, NA * l + k - 1))
                    wait_apart(pe, *waits)
                    b, src = 4 + k % 2, work[:, k % 3, :]
                    if t < QT:
                        for s in range(t + 1):
                            last = nc.tensor.transpose(ps[:, b, P * s:P * s + P], src[:, P * s:P * s + P], ident)
                    else:
                        idr = ident[0:DEC, 0:DEC]
                        for s in range(QT):
                            nc.tensor.transpose(ps[:, b, DEC * s:DEC * s + DEC], src[0:DEC, P * s:P * s + P], idr)
                        last = nc.tensor.transpose(ps[0:DEC, b, QT * DEC:TT * DEC], src[0:DEC, SEQ:TOK], idr)
                    last.then_inc(pt_ps, 1)

                def values(k):
                    h, t = ITEMS_A[k]
                    b, c, src = 6 + h % 2, DA * h, pt[:, k % 2, :]
                    pe.wait_ge(pt_evac, NA * l + k + 1)
                    if t == 0 and h >= 2:
                        pe.wait_ge(o_normed, HA * l + h - 1)
                    if t < QT:
                        for s in range(t + 1):
                            last = nc.tensor.matmul(ps[:, b, DA * t:DA * t + DA], src[:, P * s:P * s + P], va[:, s, c:c + DA],
                                                    start=s == 0, stop=s == t)
                    else:
                        p = h // 2
                        pe.wait_ge(vc_loaded[p % RING], 16 * (HA // 2 // RING) * l + 16 * (p // RING + 1))
                        vc = vc_tok[:, p % RING, :, :]
                        out = ps[0:DEC, b, QT * DA:TT * DA]
                        for s in range(QT):
                            nc.tensor.matmul(out, src[:, DEC * s:DEC * s + DEC], vc[:, s, DA * (h % 2):DA * (h % 2) + DA],
                                             start=s == 0, stop=False)
                        last = nc.tensor.matmul(out, src[0:DEC, QT * DEC:TT * DEC], va[0:DEC, QT, c:c + DA],
                                                start=False, stop=True)
                    last.then_inc(pv_done, 1)

                def pair_out(p):
                    pe.wait_ge(o_normed, HA * l + 2 * p + 2)
                    pe.wait_ge(biased, NA * l + min(2 * TT * (p + 1) + QT, NA))
                    for t in range(TT):
                        r = rows(t)
                        dst = ps[:, 2, tok(t)] if t < QT else ps[:, 3, 0:DEC]
                        last = nc.tensor.transpose(dst, o_tok[0:r, p % 2, t, :], ident[0:r, 0:r])
                    last.then_inc(ot_ps, 1)

                pe.wait_ge(evacuated, U_LAYER * l + FIRST_HALF + EV)
                for k in range(STEPS_A):
                    for i in range(halves_before(k), halves_before(k + 1)):
                        half_unit(i)
                    if k % (2 * TT) == 0 and k < NA:
                        cache_keys(k // (2 * TT))
                    if k < NA:
                        scores(k)
                    if 0 <= k - 2 < NA:
                        probs(k - 2)
                    if 0 <= k - 3 < NA:
                        values(k - 3)
                    if k >= 13 and (k - 13) % 10 == 0:
                        pair_out((k - 13) // 10)
                pe.wait_ge(evacuated, U_LAYER * l + U_IN + EV)
                pe.wait_ge(o_normed, HA * l + HA)
                to_tokens(l, 2, vt)

                def ret_keys(h):
                    if h >= 2:
                        pe.wait_ge(or_done, HR * l + h - 1)
                    elif h == 1:
                        pe.wait_ge(st_sum, HR * l + 1)
                    for t in range(TT):
                        dst = ps[:, 0, tok(t)] if t < QT else ps[0:DEC, 1, 0:P]
                        last = nc.tensor.transpose(dst, qk_ret[:, 4 + h, tok(t)], ident)
                    last.then_inc(kd_ps, 1)

                def ret_scores(k):
                    h, t = ITEMS_R[k]
                    if k >= 2:
                        wait_apart(pe, (decayed, NR * l + k - 1))
                    if t < QT:
                        for s in range(t + 1):
                            last = nc.tensor.matmul(ps[:, 2 + k % 2, P * s:P * s + P], qk_ret[:, 4 + h, tok(s)],
                                                    qk_ret[:, h, tok(t)], start=True, stop=True)
                    else:
                        last = nc.tensor.matmul(ps[0:DEC, 2 + k % 2, 0:DEC], qk_ret[:, 4 + h, tok(t)],
                                                qk_ret[:, h, tok(t)], start=True, stop=True)
                    last.then_inc(r_ps, 1)

                def ret_values(k):
                    h, t = ITEMS_R[k]
                    pe.wait_ge(decayed, NR * l + k + 1)
                    if t == 0 and h >= 2:
                        pe.wait_ge(gn_normed, HR * l + h - 1)
                    v = vr[:, :, DR * h:DR * h + DR]
                    if t < QT:
                        for s in range(t + 1):
                            last = nc.tensor.matmul(ps[:, 4 + h % 2, P * t:P * t + P], work[:, k % 3, P * s:P * s + P], v[:, s, :],
                                                    start=s == 0, stop=s == t)
                    else:
                        pe.wait_ge(qd_ready, HR * l + h + 1)
                        nc.tensor.matmul(ps[0:DEC, 6 + h % 2, 0:P], qd[:, h % RING, :], s_in[:, h, :], start=True, stop=False)
                        last = nc.tensor.matmul(ps[0:DEC, 6 + h % 2, 0:P], work[0:DEC, k % 3, 0:DEC], v[0:DEC, QT, :],
                                                start=False, stop=True)
                    last.then_inc(sv_done, 1)

                def ret_states(h):
                    pe.wait_ge(kd_evac, HR * l + h + 1)
                    v = vr[:, :, DR * h:DR * h + DR]
                    for t in range(QT):
                        nc.tensor.matmul(ps[:, 1, P:2 * P], kd_tok[:, h % 2, t, :], v[:, t, :], start=t == 0, stop=t == QT - 1)
                    nc.tensor.matmul(ps[:, 1, 2 * P:3 * P], kd_tok[0:DEC, h % 2, QT, :], v[0:DEC, QT, :],
                                     start=True, stop=True).then_inc(st_ps, 1)

                def ret_out(h):
                    pe.wait_ge(gn_normed, HR * l + h + 1)
                    pe.wait_ge(st_sum, HR * l + min(h + 2, HR))
                    for t in range(TT):
                        r = rows(t)
                        dst = ps[:, 0, tok(t)] if t < QT else ps[:, 1, 0:DEC]
                        last = nc.tensor.transpose(dst, o_tok[0:r, h % 2, t, :], ident[0:r, 0:r])
                    last.then_inc(or_ps, 1)

                pe.wait_ge(ot_out, HA // 2 * l + HA // 2)
                pe.wait_ge(tok_evac, 3 * TT * l + 3 * TT)
                pe.wait_ge(ret_ready, 16 * l + 16)
                pe.wait_ge(state_loaded, 16 * l + 16)
                for k in range(NR + 5):
                    h, i = k // TT, k % TT
                    if i == 0 and h < HR:
                        ret_keys(h)
                    if k < NR:
                        ret_scores(k)
                    if 0 <= k - 2 < NR:
                        ret_values(k - 2)
                    if i == 3 and h < HR:
                        ret_states(h)
                    if i == 4 and h >= 1:
                        ret_out(h - 1)

                pe.wait_ge(or_done, HR * l + HR)

                def mixed(k):
                    if k < 4:
                        pe.wait_ge(ot_lo, HA // 2 * l + k + 1)
                    else:
                        pe.wait_ge(or_lo, HR * l + k - 3)

                unit(U_LAYER * l + FIRST_OUT, 0, KD, mix, mixed)
                unit(U_LAYER * l + FIRST_OUT + 1, 1, KD, mix)
                with pe.Fori(1, U_OUT // 2) as c2:
                    c = 2 * c2
                    for s in range(2):
                        unit(U_LAYER * l + c + (FIRST_OUT + s), s, KD, mix)

                def ffn_ready(k):
                    pe.wait_ge(h_lo, 2 * KD * l + KD + k + 1)

                for g in range(GROUPS):
                    first = FIRST_FFN + U_GROUP * g
                    if g == 0:
                        unit(U_LAYER * l + first, 0, KD, ffn, ffn_ready)
                        rms_sums(l, 1, ffn_sq)
                        unit(U_LAYER * l + first + 1, 1, KD, ffn, midway=lambda: rms_spread(l, 1))
                    with pe.Fori(1 if g == 0 else 0, FT) as f:
                        for s in range(2):
                            unit(U_LAYER * l + 2 * f + (first + s), s, KD, ffn)

                    def act_ready(k):
                        pe.wait_ge(act_lo, GROUPS * FT * l + FT * g + k + 1)

                    unit(U_LAYER * l + first + DOWN, 0, FT, act, act_ready)
                    unit(U_LAYER * l + first + DOWN + 1, 1, FT, act)
                    with pe.Fori(1, U_OUT // 2) as c2:
                        c = 2 * c2
                        for s in range(2):
                            unit(U_LAYER * l + c + (first + DOWN + s), s, FT, act)
            pe.wait_ge(evacuated, DEPTH * U_LAYER + EV)
            for t in range(TT):
                if t >= 2:
                    pe.wait_ge(y_copied, t - 1)
                for k in range(KD):
                    b = 2 * (t % 2) + k // 4
                    last = nc.tensor.transpose(ps[0:rows(t), b, P * (k % 4):P * (k % 4) + P], x[:, k, tok(t)], ident)
                last.then_inc(y_ps, 1)


OUTPUTS = [
    ("y_prompt", (1, SEQ, D)), ("y_sample", (1, DEC, D)),
    ("nk_prompt", (DEPTH, 1, SEQ, HA, DA)), ("nv_prompt", (DEPTH, 1, SEQ, HA, DA)), ("ns_prompt", (DEPTH, 1, HR, DR, DR)),
    ("nk_sample", (DEPTH, 1, DEC, HA, DA)), ("nv_sample", (DEPTH, 1, DEC, HA, DA)), ("ns_sample", (DEPTH, 1, HR, DR, DR)),
]


def tables():
    import numpy as np

    half = DR // 2
    inv = (np.float32(10000.0) ** (-np.arange(half, dtype=np.float32) / np.float32(half))).astype(np.float32)

    def angles(pos):
        return (inv[:, None] * np.asarray(pos, np.float32)[None, :]).astype(np.float32).astype(np.float64)

    c = np.zeros((P, C_ALL))
    c[:, C_ID:C_ID + P] = np.eye(P)
    a = angles(np.arange(SEQ))
    c[:, C_COS:C_COS + SEQ] = np.concatenate([np.cos(a)] * 2)
    c[:, C_SIN:C_SIN + SEQ] = np.concatenate([np.sin(a), -np.sin(a)])
    scale = DR ** -0.5
    decay = np.zeros((HR, P, SEQ))
    for h in range(HR):
        lg = np.log(gamma(h))
        c[:, C_QDEC + DEC * h:C_QDEC + DEC * h + DEC] = np.exp((np.arange(DEC) + 1.0) * lg)
        for t in range(QT):
            c[:, C_KDEC + HR * t + h] = scale * np.exp((SEQ - 1.0 - P * t - np.arange(P)) * lg)
        c[0:DEC, C_KDEC + HR * QT + h] = scale * np.exp((DEC - 1.0 - np.arange(DEC)) * lg)
        for b in range(QT):
            diff = P * (QT - 1 - b) + np.arange(P)[None, :] - np.arange(P)[:, None]
            decay[h, :, P * b:P * b + P] = np.where(diff >= 0, scale * np.exp(np.maximum(diff, 0) * lg), 0.0)
    for i, pos in enumerate((-SEQ, -DEC)):
        a = angles([pos])[:, 0]
        c[:, C_ROT + 2 * i] = np.concatenate([np.cos(a)] * 2)
        c[:, C_ROT + 2 * i + 1] = np.concatenate([np.sin(a), -np.sin(a)])
    for j in range(2 * WA // P):
        c[0:DA, C_SEL + 18 * j] = 1.0
        c[DA:P, C_SEL + 18 * j + 1] = 1.0
    c[:, C_ONE] = 1.0
    c[:, C_EPS] = RMS_EPS
    c[:, C_EPS + 1] = GN_EPS
    return c.astype(np.float32), np.repeat(np.eye(16, dtype=np.float32), DA, axis=1), decay.astype(np.float32)


def kernel(x_prompt, x_sample, cache_a_k, cache_a_v, state_ret, norm_mix, w_in, q_norm, k_norm, rel_table,
           ret_norm, w_out, norm_ffn, w_gate, w_up, w_down):
    import numpy as np
    import concourse.bacc as bacc
    from concourse.bass_utils import run_bass_kernel_spmd

    nc = bacc.Bacc("TRN2", target_bir_lowering=False, num_devices=1)
    const, spread, decay = tables()
    arrays = dict(x_prompt=x_prompt, x_sample=x_sample, cache_k=cache_a_k, cache_v=cache_a_v, state_in=state_ret,
                  norm_mix=norm_mix, w_in=w_in, q_norm=q_norm, k_norm=k_norm, rel_table=rel_table, ret_norm=ret_norm,
                  w_out=w_out, norm_ffn=norm_ffn, w_gate=w_gate, w_up=w_up, w_down=w_down, const=const, spread=spread, decay=decay)
    arrays = {f"in_{name}": np.ascontiguousarray(a) for name, a in arrays.items()}
    aps = [nc.dram_tensor(name, a.shape, mybir.dt.from_np(a.dtype), kind="ExternalInput").ap() for name, a in arrays.items()]
    aps += [nc.dram_tensor(f"out_{name}", shape, F32, kind="ExternalOutput").ap() for name, shape in OUTPUTS]
    lines = nc.dram_tensor("bias_lines", (DEPTH * HA, 6 * P), F32, kind="Internal").ap()
    build(nc, *aps, lines)
    r = run_bass_kernel_spmd(nc, [arrays], core_ids=[0])
    return tuple(r.results[0][f"out_{name}"] for name, _ in OUTPUTS)
```

```python
import concourse.bass as bass
from concourse import mybir
from contextlib import ExitStack

F32 = mybir.dt.float32
F32R = mybir.dt.float32r
ALU = mybir.AluOpType
ACT = mybir.ActivationFunctionType

P = 128
DEPTH = 2
D = 1024
KD = D // P
SEQ, DEC = 512, 64
TOK = SEQ + DEC
HALF = TOK // 2
QT = SEQ // P
TT = QT + 1
HA, DA = 8, 64
HR, DR = 4, 128
WA, WR = HA * DA, HR * DR
CHUNK = 64
REL = 128
DFF = 2816
GROUPS = 2
FT = DFF // P // GROUPS
U_IN = (3 * WA + 4 * WR) // P
U_OUT = D // P
U_GROUP = 2 * FT + U_OUT
U_LAYER = U_IN + U_OUT + GROUPS * U_GROUP
RING = 2
STRIP = 5 * P
LINE = STRIP + P - 1
GAINS = 2 * KD + 2 + WR // P
EV = RING + KD
RMS_EPS, GN_EPS = 1e-6, 1e-5
MASKED = 1e30

C_ID = 0
C_COS = C_ID + P
C_SIN = C_COS + SEQ
C_QDEC = C_SIN + SEQ
C_KDEC = C_QDEC + HR * DEC
C_ROT = C_KDEC + TT * HR
C_SEL = C_ROT + 4
C_ONE = C_SEL + 2 * WA // P * 16
C_EPS = C_ONE + 1
C_ALL = C_EPS + 2


def gamma(h):
    return 1.0 - 2.0 ** (-5.0 - h)


def tok(t):
    return slice(t * P, t * P + rows(t))


def rows(t):
    return P if t < QT else DEC


def backwards(ap, n):
    dims = [list(d) for d in ap.ap]
    step, count = dims[-1]
    assert count == n
    dims[-1] = [-step, n]
    return bass.AP(tensor=ap.tensor, offset=ap.offset + step * (n - 1), ap=dims)


def build(nc, x_prompt, x_sample, cache_k, cache_v, state_in, norm_mix, w_in, q_norm, k_norm, rel_table,
          ret_norm, w_out, norm_ffn, w_gate, w_up, w_down, const, spread_in, decay,
          y_prompt, y_sample, nk_prompt, nv_prompt, ns_prompt, nk_sample, nv_sample, ns_sample, lines):
    ctx = ExitStack()
    with ctx:
        ROW = TOK * 4
        base = (nc.sbuf_base + 31) // 32 * 32
        A_X = base
        A_MIX = A_X + KD * ROW
        A_SH = A_MIX + 2 * KD * ROW
        A_W = A_SH + 2 * KD * ROW + 2 * FT * ROW
        UNIT = FT * P * 4
        A_MISC = A_W + 3 * RING * UNIT

        def place(name, shape, dt, at):
            return nc.alloc_sbuf_tensor_at(name, shape, dt, offset=at)

        nc.alloc_sbuf_tensor("arena", [P, (A_MISC - base) // 4], F32)
        x = place("x", [P, KD, TOK], F32, A_X)
        mix = place("mix", [P, KD, 2, TOK], F32R, A_MIX)
        qk = place("qk", [P, 2 * WA // P, TOK], F32, A_SH)
        kc_tok = place("kc_tok", [P, QT, P], F32, A_SH)
        kc_t = place("kc_t", [P, SEQ], F32, A_SH + SEQ * 4)
        vc_tok = place("vc_tok", [P, RING, QT, P], F32, A_SH + 2 * SEQ * 4)
        q_rev = place("q_rev", [P, WA // P, TOK], F32, A_SH + 8 * ROW)
        vt = place("vt", [P, 4, TOK], F32, A_SH + 12 * ROW)
        qk_ret = place("qk_ret", [P, 8, TOK], F32, A_SH + 16 * ROW)
        A_T = A_SH + 24 * ROW
        va = place("va", [P, TT, WA], F32, A_T)
        vr = place("vr", [P, TT, WR], F32, A_T + TT * WA * 4)
        qk_part = place("qk_part", [16, 2, TOK], F32R, A_T + TT * WA * 4)
        spread_r = place("spread_r", [16, KD * P], F32R, A_T + TT * WA * 4 + 2 * TOK * 4)
        sel_r = place("sel_r", [P, KD * 16], F32R, A_T + TT * WA * 4 + (2 * TOK + KD * P) * 4)
        assert 2 * TOK + KD * P + KD * 16 <= TT * WR
        sq_hi = place("sq_hi", [P, KD, TOK], F32R, A_SH + 8 * ROW)
        sq_lo = place("sq_lo", [P, KD, TOK], F32R, A_SH + 16 * ROW)
        A_S2 = A_T + 2 * TT * WA * 4
        strip = place("strip", [P, RING, STRIP], F32, A_S2)
        dmask = place("dmask", [P, RING, SEQ], F32, A_S2 + RING * STRIP * 4)
        s_in = place("s_in", [P, HR, DR], F32, A_S2 + RING * STRIP * 4 + RING * SEQ * 4)
        assert A_S2 + RING * STRIP * 4 + RING * SEQ * 4 + HR * DR * 4 <= A_W
        gate = qk[:, 4:8, :]
        kd_tok = place("kd_tok", [P, RING, TT, P], F32, A_SH)
        st_tmp = place("st_tmp", [P, 2, DR], F32, A_SH + 5120)
        st_swap = place("st_swap", [P, 2, DR], F32, A_SH + 6144)
        st_out = place("st_out", [P, RING, 2, DR], F32, A_SH + 7168)
        stage = place("stage", [P, TT, D], F32, A_SH)
        ffn = place("ffn", [P, KD, 2, TOK], F32R, A_SH)
        act = place("act", [P, FT, 2, TOK], F32R, A_SH + 2 * KD * ROW)
        ffn_sq = place("ffn_sq", [P, KD, TOK], F32, A_SH + 2 * KD * ROW)
        mix_sq = qk_ret
        w_raw = place("w_raw", [P, RING, FT, P], F32, A_W)
        w_hi = place("w_hi", [P, RING, FT, P], F32R, A_W + RING * UNIT)
        w_lo = place("w_lo", [P, RING, FT, P], F32R, A_W + 2 * RING * UNIT)

        def sb(name, shape, dt=F32):
            return ctx.enter_context(nc.sbuf_tensor(name, shape, dt))

        cst = sb("cst", [P, C_ALL])
        row_f = sb("row_f", [P, TOK])
        rcos = sb("rcos", [P, TOK])
        rsin = sb("rsin", [P, TOK])
        work = sb("work", [P, 3, TOK])
        pt = sb("pt", [P, RING, SEQ])
        o_tok = sb("o_tok", [P, RING, TT, P])
        qd = sb("qd", [P, RING, DEC])
        spread = sb("spread", [16, KD * P])
        qk_root_col, qk_col = work[0:16, 1, :], work[0:16, 2, :]
        gain_rows = pt[0:DEPTH * GAINS, 0, 0:P]
        gains = sb("gains", [P, DEPTH + 1, GAINS])
        gain = sb("gain", [P, GAINS])
        root = sb("root", [P, TT])
        inv = sb("inv", [P, TT])
        least = sb("least", [P, 4])
        sums = sb("sums", [P, RING, TT])
        rsum = sb("rsum", [P, RING, TT])
        bn = sb("bn", [P, TT, 6])
        mv = sb("mv", [P, TT, 2])
        gnr = sb("gnr", [P, TT])
        gni = sb("gni", [P, TT])

        ps = ctx.enter_context(nc.psum_tensor("ps", [P, 8, 512], F32))

        def sem(name):
            return ctx.enter_context(nc.semaphore(name))

        raw_loaded = [sem(f"raw_loaded{s}") for s in range(RING)]
        hi_done, lo_done, w_used, evacuated = sem("hi_done"), sem("lo_done"), sem("w_used"), sem("evacuated")
        ident_in, const_in, gains_in, gains_ps, gains_set, gain_cur = (sem(n) for n in (
            "ident_in", "const_in", "gains_in", "gains_ps", "gains_set", "gain_cur"))
        rel_in, line_made, line_out = sem("rel_in"), sem("line_made"), sem("line_out")
        x_ps, x_tail = sem("x_ps"), sem("x_tail")
        x_in = [sem(f"x_in{s}") for s in range(2)]
        h_hi, h_lo, sq_done, sq_sum = sem("h_hi"), sem("h_lo"), sem("sq_done"), sem("sq_sum")
        half_ps, half_out = sem("half_ps"), sem("half_out")
        rms_stat, rms_root, rms_inv, rms_bcast, rms_row = (sem(n) for n in (
            "rms_stat", "rms_root", "rms_inv", "rms_bcast", "rms_row"))
        rope_rows = sem("rope_rows")
        qk_sq_hi, qk_sq_lo = sem("qk_sq_hi"), sem("qk_sq_lo")
        qk_stat, qk_root, qk_inv, qk_hi, qk_lo, qk_bcast, qk_normed = (sem(n) for n in (
            "qk_stat", "qk_root", "qk_inv", "qk_hi", "qk_lo", "qk_bcast", "qk_normed"))
        ret_ready, tok_ps, tok_evac, g_silu = (sem(n) for n in ("ret_ready", "tok_ps", "tok_evac", "g_silu"))
        ka_out, va_out = sem("ka_out"), sem("va_out")
        strip_loaded = [sem(f"strip_loaded{s}") for s in range(RING)]
        strip_masked = sem("strip_masked")
        kc_loaded = sem("kc_loaded")
        vc_loaded = [sem(f"vc_loaded{s}") for s in range(RING)]
        kct_ps, kct_evac = sem("kct_ps"), sem("kct_evac")
        s_ps, biased, exped, pt_ps, pt_dve, pt_act, pv_done = (sem(n) for n in (
            "s_ps", "biased", "exped", "pt_ps", "pt_dve", "pt_act", "pv_done"))
        sums_inv, o_normed, ot_ps, ot_out, ot_hi, ot_lo = (sem(n) for n in (
            "sums_inv", "o_normed", "ot_ps", "ot_out", "ot_hi", "ot_lo"))
        dmask_loaded = [sem(f"dmask_loaded{s}") for s in range(RING)]
        state_loaded = sem("state_loaded")
        kd_ps, kd_evac, r_ps, decayed, sv_done, qd_ready = (sem(n) for n in (
            "kd_ps", "kd_evac", "r_ps", "decayed", "sv_done", "qd_ready"))
        bn_parts, bn_done, gn_root, gn_inv, gn_normed, or_ps, or_done, or_hi, or_lo = (sem(n) for n in (
            "bn_parts", "bn_done", "gn_root", "gn_inv", "gn_normed", "or_ps", "or_done", "or_hi", "or_lo"))
        st_ps, st_sum, st_swapped, st_done = (sem(n) for n in ("st_ps", "st_sum", "st_swapped", "st_done"))
        st_stored = [sem(f"st_stored{s}") for s in range(RING)]
        gate_silu, act_f, act_hi, act_lo = (sem(n) for n in ("gate_silu", "act_f", "act_hi", "act_lo"))
        passed = {e.engine: sem(f"passed_{i}") for i, e in enumerate((nc.gpsimd, nc.scalar, nc.vector, nc.tensor))}
        y_ps, y_out = sem("y_ps"), sem("y_out")
        y_copied = [sem(f"y_copied{i}") for i in range(2)]

        block = ctx.enter_context(nc.Block())

        ident = cst[:, C_ID:C_ID + P]
        cos, sin = cst[:, C_COS:C_COS + SEQ], cst[:, C_SIN:C_SIN + SEQ]

        def dense(s):
            return ps[:, 2 * s:2 * s + 2, 0:HALF]

        def halves(ap):
            return ap.rearrange("p (a b) -> p a b", a=2)

        def head_rows(h):
            return slice(DA * (h % 2), DA * (h % 2) + DA)

        def x_count(l, which):
            return U_LAYER * l + (RING if which == 0 else U_IN + EV)

        def wait_apart(eng, *waits):
            for semaphore, count in waits:
                eng.wait_ge(semaphore, count)
            eng.sem_inc(passed[eng.engine], 1)

        FIRST_OUT = U_IN
        FIRST_FFN = U_IN + U_OUT
        DOWN = 2 * FT

        ITEMS_A = [(h, t) for h in range(HA) for t in range(TT)]
        ITEMS_R = [(h, t) for h in range(HR) for t in range(TT)]
        NA, NR = len(ITEMS_A), len(ITEMS_R)
        STEPS_A = NA + 4

        FIRST_HALF = 3 * WA // P
        UNITS_H = U_IN - FIRST_HALF
        PRE = 6
        AT_A = [2] + [k for k in range(1, NA + 1) if k % TT in (0, TT - 1)] + [NA + 2]
        AT_R = [k for k in range(1, NR + 1) if k % TT in (0, TT - 1)]
        FIRST_R = PRE + len(AT_A)
        assert FIRST_R + len(AT_R) == 2 * UNITS_H and FIRST_R == 2 * (UNITS_H - HR)
        NORM_ORDER = [j + 4 * i for j in range(4) for i in range(2)]

        def tok_bank(group, t):
            return 4 + t % (4 if group < 2 else 3)

        def by_act(k):
            return ITEMS_A[k][1] >= QT - 1

        def pt_out(l, k):
            n = sum(by_act(j) == by_act(k) for j in range(k + 1))
            total = sum(by_act(j) == by_act(k) for j in range(NA))
            return (pt_act if by_act(k) else pt_dve, total * l + n)

        def head_before(k):
            h, i = divmod(k - 3, TT)
            return h - 1 if i == 0 and 1 <= h <= HA else None

        def half_bank(i):
            return i % 2 if i < FIRST_R else 6 + i % 2

        @block.sync
        def _(sp):
            sp.dma_start(cst[:, C_ID:C_ID + P], const[:, C_ID:C_ID + P]).then_inc(ident_in, 16)
            for s in range(2):
                c = slice(D // 2 * s, D // 2 * s + D // 2)
                sp.dma_start(stage[:, 0:QT, c], x_prompt[0].rearrange("(t p) d -> p t d", p=P)[:, :, c]).then_inc(x_in[s], 16)
                sp.dma_start(stage[0:DEC, QT, c], x_sample[0][:, c]).then_inc(x_in[s], 16)

            def load(slot, n, src, k):
                sp.wait_ge(hi_done, n + 1)
                sp.wait_ge(lo_done, n + 1)
                sp.dma_start(w_raw[:, slot, 0:k, :], src).then_inc(raw_loaded[slot], 16)

            with sp.Fori(0, DEPTH) as l:
                with sp.Fori(0, U_IN // 2) as c2:
                    c = 2 * c2
                    for s in range(2):
                        load(s, U_LAYER * l + c + s,
                             w_in[l].rearrange("(k p) n -> p k n", p=P)[:, :, bass.ds((c + s) * P, P)], KD)

                def load_out(c, s):
                    load(s, U_LAYER * l + FIRST_OUT + c + s,
                         w_out[l].rearrange("(k p) n -> p k n", p=P)[:, :, bass.ds((c + s) * P, P)], KD)

                for s in range(2):
                    load_out(0, s)
                sp.wait_ge(tok_evac, 3 * TT * l + TT)
                sp.dma_start(nv_prompt[l, 0].rearrange("(t p) h d -> p t (h d)", p=P), va[:, 0:QT, :]).then_inc(va_out, 16)
                sp.dma_start(nv_sample[l, 0].rearrange("p h d -> p (h d)"), va[0:DEC, QT, :]).then_inc(va_out, 16)
                with sp.Fori(1, U_OUT // 2) as c2:
                    c = 2 * c2
                    for s in range(2):
                        load_out(c, s)
                with sp.Fori(0, GROUPS) as g:
                    with sp.Fori(0, FT) as f:
                        for s, w in enumerate((w_gate, w_up)):
                            load(s, U_LAYER * l + U_GROUP * g + 2 * f + (FIRST_FFN + s),
                                 w[l].rearrange("(k p) n -> p k n", p=P)[:, :, bass.ds((g * FT + f) * P, P)], KD)
                    with sp.Fori(0, U_OUT // 2) as c2:
                        c = 2 * c2
                        for s in range(2):
                            load(s, U_LAYER * l + U_GROUP * g + c + (FIRST_FFN + DOWN + s),
                                 w_down[l].rearrange("(g k p) n -> g p k n", g=GROUPS, p=P)[g, :, :, bass.ds((c + s) * P, P)], FT)
            for t in range(TT):
                for copied in y_copied:
                    sp.wait_ge(copied, t + 1)
                dst = y_prompt[0, tok(t), :] if t < QT else y_sample[0]
                sp.dma_start(dst, stage[0:rows(t), t, :]).then_inc(y_out, 16)
            sp.wait_ge(y_out, 16 * TT)
            sp.wait_ge(ka_out, 32 * DEPTH)
            sp.wait_ge(va_out, 32 * DEPTH)
            for s in range(RING):
                sp.wait_ge(st_stored[s], 2 * 16 * HR // RING * DEPTH)

        @block.gpsimd
        def _(pool):
            pool.dma_start(work[0:DEPTH * HA, 2, 0:2 * REL + 1], rel_table.rearrange("l h r -> (l h) r")).then_inc(rel_in, 16)
            pool.wait_ge(line_made, 1)
            pool.dma_start(lines[:, 0:LINE], work[0:DEPTH * HA].rearrange("p a b -> p (a b)")[:, 0:LINE]).then_inc(line_out, 16)
            pool.wait_ge(raw_loaded[0], 16)
            pool.dma_start(cst[:, P:C_ALL], const[:, P:C_ALL]).then_inc(const_in, 16)
            pool.dma_start(spread[:], spread_in).then_inc(const_in, 16)
            pool.wait_ge(line_out, 16)
            with pool.Fori(0, DEPTH) as l:
                def load_strip(h):
                    if h >= RING:
                        wait_apart(pool, (biased, NA * l + TT * (h - RING + 1)))
                    window = lines[bass.ds(l * HA + h, 1), 0:STRIP]
                    src = bass.AP(tensor=window.tensor, offset=window.offset, ap=[[1, P], [1, STRIP]])
                    pool.dma_start(strip[:, h % RING, :], src).then_inc(strip_loaded[h % RING], 16)

                def mask_strip(h):
                    wait_apart(pool, (strip_loaded[h % RING], 16 * (HA // RING) * l + 16 * (h // RING + 1)))
                    nc.gpsimd.memset(strip[CHUNK:P, h % RING, STRIP - CHUNK:STRIP], MASKED).then_inc(strip_masked, 1)

                def cache_of(src, p):
                    return src[l, 0, :, 2 * p:2 * p + 2, :].rearrange("(t p) h d -> p t (h d)", p=P)

                def load_cached_keys(p):
                    if p:
                        wait_apart(pool, (kct_ps, HA // 2 * l + p))
                    pool.dma_start(kc_tok[:], cache_of(cache_k, p)).then_inc(kc_loaded, 16)

                def load_cached_values(p):
                    if p >= RING:
                        wait_apart(pool, (pv_done, NA * l + 2 * TT * (p - RING + 1)))
                    pool.dma_start(vc_tok[:, p % RING, :, :], cache_of(cache_v, p)).then_inc(vc_loaded[p % RING], 16)

                def load_mask(h):
                    if h >= RING:
                        wait_apart(pool, (decayed, NR * l + TT * (h - RING + 1)))
                    pool.dma_start(dmask[:, h % RING, :], decay[h]).then_inc(dmask_loaded[h % RING], 16)

                wait_apart(pool, (w_used, U_LAYER * l + RING + 1))
                for h in range(RING):
                    load_strip(h)
                    load_mask(h)
                pool.dma_start(s_in[:], state_in[l, 0].rearrange("h d e -> d h e")).then_inc(state_loaded, 16)
                for h in range(RING):
                    mask_strip(h)
                wait_apart(pool, (qk_normed, 8 * l + 8))
                load_cached_keys(0)
                for p in range(RING):
                    load_cached_values(p)
                wait_apart(pool, (tok_evac, 3 * TT * l + 2 * TT))
                pool.dma_start(nk_prompt[l, 0].rearrange("(t p) h d -> p t (h d)", p=P), vr[:, 0:QT, :]).then_inc(ka_out, 16)
                pool.dma_start(nk_sample[l, 0].rearrange("p h d -> p (h d)"), vr[0:DEC, QT, :]).then_inc(ka_out, 16)
                load_cached_keys(1)
                for h in range(RING, HA):
                    load_strip(h)
                    mask_strip(h)
                    p = h // 2 + 1
                    if h % 2 and p < HA // 2:
                        load_cached_keys(p)
                        load_cached_values(p)
                for h in range(HR):
                    if h + RING < HR:
                        load_mask(h + RING)
                    wait_apart(pool, (st_done, HR * l + h + 1))
                    for i, dst in enumerate((ns_prompt, ns_sample)):
                        pool.dma_start(dst[l, 0, h], st_out[:, h % RING, i, :]).then_inc(st_stored[h % RING], 16)

        @block.scalar
        def _(eng):
            def hi(slot, count, n, k):
                eng.wait_ge(raw_loaded[slot], count)
                eng.wait_ge(w_used, n + 1)
                nc.scalar.activation(w_hi[:, slot, 0:k, :], w_raw[:, slot, 0:k, :], ACT.Copy).then_inc(hi_done, 1)

            def norm_in(l, which, dst, k):
                eng.wait_ge(evacuated, x_count(l, which) + k + 1)
                nc.scalar.activation(dst[:, k, 0, :], x[:, k, :], ACT.Copy,
                                     scale=gain[:, which * KD + k:which * KD + k + 1]).then_inc(h_hi, 1)

            def square_in(l, which, sq, k):
                eng.wait_ge(evacuated, x_count(l, which) + k + 1)
                nc.scalar.activation(sq[:, k, :], x[:, k, :], ACT.Square).then_inc(sq_done, 1)

            def rms_sqrt(l, which):
                eng.wait_ge(rms_stat, 2 * l + which + 1)
                nc.scalar.activation(root[:, 0:QT], ps[:, 6, 0:QT], ACT.Sqrt, scale=1.0 / D,
                                     bias=cst[:, C_EPS:C_EPS + 1])
                nc.scalar.activation(root[0:DEC, QT:TT], ps[0:DEC, 6, QT:TT], ACT.Sqrt, scale=1.0 / D,
                                     bias=cst[0:DEC, C_EPS:C_EPS + 1]).then_inc(rms_root, 1)

            def tok_copy(l, group, dst, t):
                eng.wait_ge(tok_ps, 3 * TT * l + TT * group + t + 1)
                nc.scalar.activation(dst[0:rows(t), t, :], ps[0:rows(t), tok_bank(group, t), :], ACT.Copy).then_inc(tok_evac, 1)

            at = 0
            for src in (norm_mix, norm_ffn, ret_norm):
                n = DEPTH * src.shape[1] // P
                eng.dma_start(gain_rows[at:at + n, :], src.rearrange("l (k p) -> (l k) p", p=P)).then_inc(gains_in, 16)
                at += n
            for src in (q_norm, k_norm):
                for half in range(2):
                    eng.dma_start(gain_rows[at:at + DEPTH, DA * half:DA * half + DA], src).then_inc(gains_in, 16)
                at += DEPTH
            eng.sem_inc(hi_done, RING)
            for k in range(KD):
                eng.wait_ge(x_ps, k + 1)
                nc.scalar.activation(x[:, k, SEQ:TOK], ps[:, 5 + 2 * (k % 2), 0:DEC], ACT.Copy).then_inc(x_tail, 1)
            eng.wait_ge(x_tail, KD)
            with eng.Fori(0, DEPTH) as l:
                def unit_hi(n, k=KD):
                    hi(n % 2, 16 * (U_LAYER // 2) * l + 16 * (n // 2 + 1), U_LAYER * l + n, k)

                unit_hi(0)
                eng.wait_ge(gain_cur, l + 1)
                for k in range(KD):
                    norm_in(l, 0, mix, k)
                unit_hi(1)
                for k in range(KD):
                    square_in(l, 0, mix_sq, k)
                unit_hi(2)
                rms_sqrt(l, 0)
                unit_hi(3)
                nc.scalar.activation(sel_r[:], cst[:, C_SEL:C_SEL + KD * 16], ACT.Copy)
                for n in range(8):
                    if n >= 3:
                        unit_hi(n + 1)
                    eng.wait_ge(evacuated, U_LAYER * l + n + EV + 1)
                    nc.scalar.activation(mix_sq[:, n, :], qk[:, n, :], ACT.Square).then_inc(sq_done, 1)
                    nc.scalar.activation(sq_hi[:, n, :], qk[:, n, :], ACT.Square).then_inc(qk_sq_hi, 1)
                unit_hi(9)
                unit_hi(10)
                eng.wait_ge(line_out, 16)
                eng.wait_ge(qk_stat, l + 1)
                nc.scalar.activation(qk_root_col[:, 0:SEQ], ps[0:16, 6, :], ACT.Sqrt, scale=1.0 / DA,
                                     bias=cst[0:16, C_EPS:C_EPS + 1])
                nc.scalar.activation(qk_root_col[:, SEQ:TOK], ps[0:16, 7, 0:DEC], ACT.Sqrt, scale=1.0 / DA,
                                     bias=cst[0:16, C_EPS:C_EPS + 1]).then_inc(qk_root, 1)
                unit_hi(11)
                unit_hi(12)
                nc.scalar.activation(spread_r[:], spread[:], ACT.Copy)
                eng.wait_ge(qk_inv, l + 1)
                nc.scalar.activation(qk_part[:, 0, :], qk_col, ACT.Copy).then_inc(qk_hi, 1)

                def half_unit(i):
                    if i % 2 == 0:
                        unit_hi(FIRST_HALF + i // 2 + 1)

                for i in range(PRE):
                    half_unit(i)
                    if i == 0:
                        for t in range(TT):
                            tok_copy(l, 0, va, t)
                for t in range(TT):
                    tok_copy(l, 1, vr, t)

                def cache_keys(p):
                    eng.wait_ge(kct_ps, HA // 2 * l + p + 1)
                    nc.scalar.activation(kc_t[:], ps[:, 6, :], ACT.Copy).then_inc(kct_evac, 1)

                def attn_out(p):
                    eng.wait_ge(ot_ps, HA // 2 * l + p + 1)
                    nc.scalar.activation(q_rev[:, p, 0:SEQ].rearrange("p (t q) -> p t q", t=QT),
                                         backwards(ps[:, 7, :].rearrange("p (t q) -> p t q", t=QT), P), ACT.Copy)
                    nc.scalar.activation(q_rev[:, p, SEQ:TOK], backwards(ps[:, 2, 0:DEC], DEC), ACT.Copy).then_inc(ot_out, 1)

                def probs_out(k):
                    h, t = ITEMS_A[k]
                    eng.wait_ge(pt_ps, NA * l + k + 1)
                    eng.wait_ge(pv_done, NA * l + k - 1)
                    if t < QT:
                        nc.scalar.activation(pt[:, k % 2, :], ps[:, 4 + k % 2, :], ACT.Copy).then_inc(pt_act, 1)
                    else:
                        c = QT * DEC
                        nc.scalar.activation(pt[:, k % 2, 0:c], ps[:, 4 + k % 2, 0:c], ACT.Copy)
                        nc.scalar.activation(pt[0:DEC, k % 2, c:c + DEC], ps[0:DEC, 4 + k % 2, c:c + DEC],
                                             ACT.Copy).then_inc(pt_act, 1)

                def exponentials(k):
                    h, t = ITEMS_A[k]
                    r, w = rows(t), P * (t + 1) if t < QT else TOK
                    if k >= 2 * TT:
                        eng.wait_ge(sums_inv, HA * l + h - 1)
                    eng.wait_ge(biased, NA * l + k + 1)
                    nc.scalar.activation(work[0:r, k % 3, 0:w], work[0:r, k % 3, 0:w], ACT.Exp, scale=-1.0,
                                         bias=least[0:r, k % 4:k % 4 + 1],
                                         accum_out=sums[0:r, h % 2, t:t + 1]).then_inc(exped, 1)

                for k in range(STEPS_A):
                    if k < NA and head_before(k - 1) in range(1, HA, 2):
                        attn_out(head_before(k - 1) // 2)
                    if k % (2 * TT) == 1 and k < NA:
                        cache_keys(k // (2 * TT))
                    if 0 <= k - 2 < NA and by_act(k - 2):
                        probs_out(k - 2)
                    if k < NA:
                        exponentials(k)
                    if k in AT_A:
                        half_unit(PRE + AT_A.index(k))
                eng.wait_ge(ka_out, 32 * l + 32)
                for t in range(3):
                    tok_copy(l, 2, vr, t)
                attn_out(HA // 2 - 1)

                def attn_hi(p):
                    eng.wait_ge(w_used, U_LAYER * l + U_IN + RING)
                    eng.wait_ge(ot_out, HA // 2 * l + p + 1)
                    nc.scalar.activation(mix[:, p, 0, :], q_rev[:, p, :], ACT.Copy).then_inc(ot_hi, 1)

                def ret_keys(h):
                    eng.wait_ge(kd_ps, HR * l + h + 1)
                    if h >= RING:
                        eng.wait_ge(st_ps, HR * l + h - 1)
                    for t in range(TT):
                        bank, c = (0, P * t) if t < QT else (1, 0)
                        last = nc.scalar.activation(kd_tok[0:rows(t), h % 2, t, :], ps[0:rows(t), bank, c:c + P], ACT.Copy,
                                                    scale=cst[0:rows(t), C_KDEC + HR * t + h:C_KDEC + HR * t + h + 1])
                    last.then_inc(kd_evac, 1)

                def group_root(h):
                    eng.wait_ge(bn_done, HR * l + h + 1)
                    nc.scalar.activation(gnr[:, 0:QT], mv[:, 0:QT, 1], ACT.Sqrt, bias=cst[:, C_EPS + 1:C_EPS + 2])
                    nc.scalar.activation(gnr[0:DEC, QT:TT], mv[0:DEC, QT:TT, 1], ACT.Sqrt,
                                         bias=cst[0:DEC, C_EPS + 1:C_EPS + 2]).then_inc(gn_root, 1)

                def gate_silu_of(h):
                    eng.wait_ge(evacuated, U_LAYER * l + U_IN - HR + h + EV + 1)
                    nc.scalar.activation(gate[:, h, :], gate[:, h, :], ACT.Silu).then_inc(g_silu, 1)

                def ret_hi(h):
                    eng.wait_ge(or_done, HR * l + h + 1)
                    nc.scalar.activation(mix[:, 4 + h, 0, :], gate[:, h, :], ACT.Copy).then_inc(or_hi, 1)

                for k in range(NR + 3):
                    h, i = k // TT, k % TT
                    if k in AT_R:
                        half_unit(FIRST_R + AT_R.index(k))
                    if i == 0 and h < HR:
                        ret_keys(h)
                    if k == 0:
                        for t in range(3, TT):
                            tok_copy(l, 2, vr, t)
                    if i == 1 and h == HR:
                        for p in range(HA // 2):
                            attn_hi(p)
                        for j in range(HR - 1):
                            ret_hi(j)
                        unit_hi(FIRST_OUT + 1)
                    if i == 1 and 1 <= h < HR:
                        gate_silu_of(h - 1)
                    if i == 2 and h >= 1:
                        group_root(h - 1)
                gate_silu_of(HR - 1)
                ret_hi(HR - 1)
                eng.wait_ge(va_out, 32 * l + 32)
                for s in range(RING):
                    eng.wait_ge(st_stored[s], 2 * 16 * HR // RING * l + 2 * 16 * HR // RING)
                for c in range(U_OUT):
                    if c + 1 < U_OUT:
                        unit_hi(FIRST_OUT + c + 2)
                    norm_in(l, 1, ffn, c)
                    square_in(l, 1, ffn_sq, c)
                for g in range(GROUPS):
                    def group_hi(i, s, k=KD):
                        hi(s, 8 * U_LAYER * l + 8 * i + (8 * (FIRST_FFN + U_GROUP * g - s) + 16),
                           U_LAYER * l + i + (FIRST_FFN + U_GROUP * g), k)

                    def silu(f):
                        eng.wait_ge(evacuated, U_LAYER * l + 2 * f + (FIRST_FFN + U_GROUP * g + EV + 1))
                        nc.scalar.activation(work[:, 0, :], work[:, 0, :], ACT.Silu).then_inc(gate_silu, 1)

                    def act_high(f):
                        wait_apart(eng, (act_f, GROUPS * FT * l + f + (FT * g + 1)))
                        nc.scalar.activation(act[:, bass.ds(f, 1), 0, :].rearrange("p a b -> p (a b)"), work[:, 2, :],
                                             ACT.Copy).then_inc(act_hi, 1)

                    def gate_up(f, early=False):
                        if early:
                            group_hi(2 * f + 2, 0)
                        silu(f)
                        if not early:
                            group_hi(2 * f + 2, 0)
                        act_high(f)
                        group_hi(2 * f + 3, 1)

                    if g == 0:
                        group_hi(1, 1)
                        rms_sqrt(l, 1)
                    gate_up(0, early=g == 0)
                    with eng.Fori(1, FT - 1) as f:
                        gate_up(f)
                    silu(FT - 1)
                    group_hi(DOWN, 0, FT)
                    act_high(FT - 1)
                    group_hi(DOWN + 1, 1, FT)
                    with eng.Fori(1, U_OUT // 2) as c2:
                        c = 2 * c2
                        for s in range(2):
                            group_hi(c + (DOWN + s), s, FT)
                    if g + 1 < GROUPS:
                        group_hi(U_GROUP, 0)
                        group_hi(U_GROUP + 1, 1)
            for t in range(TT):
                eng.wait_ge(y_ps, t + 1)
                nc.scalar.activation(stage[0:rows(t), t, 0:D // 2], ps[0:rows(t), 2 * (t % 2), :],
                                     ACT.Copy).then_inc(y_copied[0], 1)

        @block.vector
        def _(dve):
            def lo(slot, n, k=KD):
                dve.wait_ge(hi_done, n + RING + 1)
                nc.vector.tensor_tensor(w_lo[:, slot, 0:k, :], w_raw[:, slot, 0:k, :],
                                        w_hi[:, slot, 0:k, :].bitcast(F32), ALU.subtract).then_inc(lo_done, 1)

            def projected(n):
                dve.wait_ge(w_used, n + RING + 1)

            def scaled(n, s, dst):
                projected(n)
                nc.vector.tensor_tensor(halves(dst), dense(s), halves(row_f[:]), ALU.mult).then_inc(evacuated, 1)

            def norm_lo(l, which, dst, k):
                dve.wait_ge(h_hi, 2 * KD * l + which * KD + k + 1)
                nc.vector.scalar_tensor_tensor(dst[:, k, 1, :], x[:, k, :], gain[:, which * KD + k:which * KD + k + 1],
                                               dst[:, k, 0, :].bitcast(F32), ALU.mult, ALU.subtract).then_inc(h_lo, 1)

            def add_square(l, which, sq, k):
                dve.wait_ge(sq_done, 3 * KD * l + 2 * KD * which + k + 1)
                if k > 1:
                    dve.wait_ge(sq_sum, 2 * (KD - 1) * l + (KD - 1) * which + k - 1)
                nc.vector.tensor_tensor(sq[:, 0, :], sq[:, 0, :], sq[:, k, :], ALU.add).then_inc(sq_sum, 1)

            def rms_invert(l, which):
                dve.wait_ge(rms_root, 2 * l + which + 1)
                nc.vector.reciprocal(inv[:, 0:QT], root[:, 0:QT])
                nc.vector.reciprocal(inv[0:DEC, QT:TT], root[0:DEC, QT:TT]).then_inc(rms_inv, 1)

            def rms_rows(l, which):
                dve.wait_ge(rms_bcast, 2 * l + which + 1)
                nc.vector.tensor_copy(row_f[:, 0:SEQ], ps[:, 7, :])
                nc.vector.tensor_copy(row_f[:, SEQ:TOK], ps[:, 6, P:P + DEC]).then_inc(rms_row, 1)
                dve.wait_ge(rms_row, 2 * l + which + 1)

            dve.sem_inc(lo_done, RING)
            dve.sem_inc(evacuated, RING)
            dve.wait_ge(rel_in, 16)
            line = work[0:DEPTH * HA].rearrange("p a b -> p (a b)")
            far = LINE - (2 * REL - 1)
            nc.vector.tensor_scalar(line[:, 0:far], line[:, 2 * TOK + 2 * REL:2 * TOK + 2 * REL + 1].to_broadcast([DEPTH * HA, far]),
                                    -1.0, None, ALU.mult)
            nc.vector.tensor_scalar(line[:, far:LINE], backwards(line[:, 2 * TOK + 1:2 * TOK + 2 * REL], 2 * REL - 1),
                                    -1.0, None, ALU.mult).then_inc(line_made, 1)
            nc.vector.memset(gains[:, DEPTH, :], 0.0)
            for k in range(KD):
                b = 4 + 2 * (k % 2)
                if k == KD // 2:
                    dve.wait_ge(gains_ps, 1)
                    at = 0
                    for dst, n, factor in ((0, KD, 1.0), (KD, KD, 1.0), (2 * KD + 2, WR // P, 1.0),
                                           (2 * KD, 1, -(DA ** -0.5)), (2 * KD + 1, 1, 1.0)):
                        cols = ps[:, 0, at:at + DEPTH * n].rearrange("p (l g) -> p l g", l=DEPTH)
                        last = nc.vector.tensor_scalar(gains[:, 0:DEPTH, dst:dst + n], cols, factor, None, ALU.mult)
                        at += DEPTH * n
                    last.then_inc(gains_set, 1)
                    dve.wait_ge(gains_set, 1)
                    nc.vector.tensor_copy(gain[:], gains[:, 0, :]).then_inc(gain_cur, 1)
                dve.wait_ge(x_ps, k + 1)
                nc.vector.tensor_copy(x[:, k, 0:SEQ], ps[:, b, :]).then_inc(evacuated, 1)
            with dve.Fori(0, DEPTH) as l:
                def unit_lo(n, k=KD):
                    lo(n % 2, U_LAYER * l + n, k)

                dve.wait_ge(gain_cur, l + 1)
                unit_lo(0)
                for k in range(KD):
                    norm_lo(l, 0, mix, k)
                unit_lo(1)
                for k in range(1, KD):
                    add_square(l, 0, mix_sq, k)
                unit_lo(2)
                rms_invert(l, 0)
                unit_lo(3)
                rms_rows(l, 0)
                for n in range(2):
                    scaled(U_LAYER * l + n, n % 2, qk[:, n, :])
                projected(U_LAYER * l + 2)
                nc.vector.tensor_tensor(halves(qk[:, 2, :]), ps[:, 4:6, 0:HALF], halves(row_f[:]), ALU.mult).then_inc(evacuated, 1)
                dve.wait_ge(const_in, 32)
                for dst, table in ((rcos, cos), (rsin, sin)):
                    nc.vector.tensor_tensor(dst[:, 0:SEQ], row_f[:, 0:SEQ], table, ALU.mult)
                    last = nc.vector.tensor_tensor(dst[:, SEQ:TOK], row_f[:, SEQ:TOK], table[:, 0:DEC], ALU.mult)
                last.then_inc(rope_rows, 1)
                def square_lo(j):
                    dve.wait_ge(sq_done, 3 * KD * l + KD + j + 1)
                    dve.wait_ge(qk_sq_hi, 8 * l + j + 1)
                    nc.vector.tensor_tensor(sq_lo[:, j, :], mix_sq[:, j, :], sq_hi[:, j, :].bitcast(F32),
                                            ALU.subtract).then_inc(qk_sq_lo, 1)

                square_lo(0)
                square_lo(1)
                for n in range(3, 12):
                    unit_lo(n + 1)
                    if n <= 8:
                        square_lo(n - 1)
                    if n == 8:
                        dve.wait_ge(qk_stat, l + 1)
                    if n == 10:
                        dve.wait_ge(qk_root, l + 1)
                        nc.vector.reciprocal(qk_col, qk_root_col).then_inc(qk_inv, 1)
                    scaled(U_LAYER * l + n, n % 2, qk[:, n, :] if n < 8 else vt[:, n - 8, :])

                dve.wait_ge(qk_hi, l + 1)
                nc.vector.tensor_tensor(qk_part[:, 1, :], qk_col, qk_part[:, 0, :].bitcast(F32), ALU.subtract).then_inc(qk_lo, 1)

                def half_unit(i):
                    n, half = FIRST_HALF + i // 2, i % 2
                    c = slice(HALF * half, HALF * half + HALF)
                    bank = ps[:, half_bank(i), 0:HALF]
                    if half == 0:
                        dve.wait_ge(half_ps, UNITS_H * l + n - FIRST_HALF + 1)
                    else:
                        projected(U_LAYER * l + n)
                    out = evacuated if half else half_out
                    if n < FIRST_HALF + 8:
                        if i >= 2:
                            dve.wait_ge(ret_ready, 16 * l + i - 1)
                        dst, H = qk_ret[:, n - FIRST_HALF, c], P // 2
                        nc.vector.tensor_tensor(dst, bank, rcos[:, c], ALU.mult)
                        nc.vector.tensor_tensor(vt[0:H, 0, c], bank[H:P, :], rsin[H:P, c], ALU.mult)
                        nc.vector.tensor_tensor(vt[H:P, 0, c], bank[0:H, :], rsin[0:H, c], ALU.mult).then_inc(out, 1)
                        dve.wait_ge(*(out, U_LAYER * l + n + EV + 1) if half else (out, UNITS_H * l + n - FIRST_HALF + 1))
                        nc.vector.tensor_tensor(dst, dst, vt[:, 0, c], ALU.add).then_inc(ret_ready, 1)
                    else:
                        j = n - FIRST_HALF - 8
                        if i == 16 + half:
                            dve.wait_ge(ret_ready, 16 * l + 16)
                        dst = vt[:, j, c] if j < 4 else gate[:, j - 4, c]
                        nc.vector.tensor_tensor(dst, bank, row_f[:, c], ALU.mult).then_inc(out, 1)
                    if half == 0:
                        unit_lo(n + 1)

                def qk_normalise(i):
                    j, b = NORM_ORDER[i], 4 + 2 * (i % 2)
                    dve.wait_ge(qk_bcast, 8 * l + i + 1)
                    g = gain[:, 2 * KD + j // 4:2 * KD + j // 4 + 1]
                    src = (qk[:, j, 0:SEQ], qk[:, j, SEQ:TOK])
                    if j < 4:
                        tiles = q_rev[:, j, 0:SEQ].rearrange("p (t q) -> p t q", t=QT)
                        nc.vector.scalar_tensor_tensor(backwards(tiles, P), src[0].rearrange("p (t q) -> p t q", t=QT), g,
                                                       ps[:, b, :].rearrange("p (t q) -> p t q", t=QT), ALU.mult, ALU.mult)
                        dst = backwards(q_rev[:, j, SEQ:TOK], DEC)
                    else:
                        nc.vector.scalar_tensor_tensor(src[0], src[0], g, ps[:, b, :], ALU.mult, ALU.mult)
                        dst = src[1]
                    nc.vector.scalar_tensor_tensor(dst, src[1], g, ps[:, b + 1, 0:DEC], ALU.mult, ALU.mult).then_inc(qk_normed, 1)

                dve.wait_ge(rope_rows, l + 1)
                for i in range(PRE):
                    if i == 0:
                        dve.wait_ge(tok_ps, 3 * TT * l + TT)
                    half_unit(i)
                    if 1 <= i <= 4:
                        qk_normalise(2 * i - 2)
                        qk_normalise(2 * i - 1)

                def add_bias(k):
                    h, t = ITEMS_A[k]
                    r, w = rows(t), P * (t + 1) if t < QT else TOK
                    waits = [(s_ps, NA * l + k + 1)]
                    if t == 0:
                        waits.append((strip_masked, HA * l + h + 1))
                    if k >= 3:
                        waits.append((pt_ps, NA * l + k - 2))
                    wait_apart(dve, *waits)
                    if t < QT:
                        src, bias = ps[:, 2 + t % 2, 0:w], strip[:, h % RING, STRIP - w:STRIP]
                        dst = work[:, k % 3, 0:w]
                    else:
                        src, bias = ps[0:r, 2:4, 0:HALF], halves(strip[P - DEC:P, h % RING, 0:TOK])
                        dst = halves(work[0:r, k % 3, :])
                    nc.vector.tensor_tensor_reduce(out=dst, in0=src, in1=bias, scale=1.0, scalar=3e38, op0=ALU.add,
                                                   op1=ALU.min, accum_out=least[0:r, k % 4:k % 4 + 1]).then_inc(biased, 1)

                def probs_out(k):
                    h, t = ITEMS_A[k]
                    dve.wait_ge(pt_ps, NA * l + k + 1)
                    if k >= 2:
                        dve.wait_ge(pv_done, NA * l + k - 1)
                    nc.vector.tensor_copy(pt[:, k % 2, 0:P * (t + 1)], ps[:, 4 + k % 2, 0:P * (t + 1)]).then_inc(pt_dve, 1)

                def head_normalise(h):
                    dve.wait_ge(exped, NA * l + TT * (h + 1))
                    nc.vector.reciprocal(rsum[:, h % 2, 0:QT], sums[:, h % 2, 0:QT])
                    nc.vector.reciprocal(rsum[0:DEC, h % 2, QT:TT], sums[0:DEC, h % 2, QT:TT]).then_inc(sums_inv, 1)
                    dve.wait_ge(sums_inv, HA * l + h + 1)
                    dve.wait_ge(pv_done, NA * l + TT * (h + 1))
                    p, c = h // 2, DA * (h % 2)
                    if p >= RING:
                        dve.wait_ge(ot_ps, HA // 2 * l + p - 1)
                    nc.vector.tensor_tensor(o_tok[:, p % 2, 0:QT, c:c + DA],
                                            ps[:, 6 + h % 2, 0:QT * DA].rearrange("p (t d) -> p t d", t=QT),
                                            rsum[:, h % 2, 0:QT].unsqueeze(2).to_broadcast([P, QT, DA]), ALU.mult)
                    nc.vector.tensor_scalar(o_tok[0:DEC, p % 2, QT, c:c + DA], ps[0:DEC, 6 + h % 2, QT * DA:TT * DA],
                                            rsum[0:DEC, h % 2, QT:TT], None, ALU.mult).then_inc(o_normed, 1)

                def attn_lo(p):
                    dve.wait_ge(ot_hi, HA // 2 * l + p + 1)
                    nc.vector.tensor_tensor(mix[:, p, 1, :], q_rev[:, p, :], mix[:, p, 0, :].bitcast(F32), ALU.subtract).then_inc(ot_lo, 1)

                for k in range(STEPS_A):
                    if head_before(k) is not None:
                        head_normalise(head_before(k))
                    if k < NA:
                        add_bias(k)
                    if 0 <= k - 2 < NA and not by_act(k - 2):
                        probs_out(k - 2)
                    if k in AT_A:
                        half_unit(PRE + AT_A.index(k))

                def mask_scores(k):
                    h, t = ITEMS_R[k]
                    r, w = rows(t), P * (t + 1) if t < QT else DEC
                    c = SEQ - w if t < QT else SEQ - P
                    dve.wait_ge(r_ps, NR * l + k + 1)
                    if t == 0:
                        dve.wait_ge(dmask_loaded[h % RING], 16 * HR // RING * l + 16 * (h // RING + 1))
                    if k >= 3:
                        dve.wait_ge(sv_done, NR * l + k - 2)
                    nc.vector.tensor_tensor(work[0:r, k % 3, 0:w], ps[0:r, 2 + k % 2, 0:w], dmask[0:r, h % RING, c:c + w],
                                            ALU.mult).then_inc(decayed, 1)

                def query_decay(h):
                    dve.wait_ge(ret_ready, 16 * l + 16)
                    if h >= RING:
                        dve.wait_ge(sv_done, NR * l + TT * (h - RING + 1))
                    nc.vector.tensor_tensor(qd[:, h % RING, :], qk_ret[:, h, SEQ:TOK],
                                            cst[:, C_QDEC + DEC * h:C_QDEC + DEC * h + DEC], ALU.mult).then_inc(qd_ready, 1)

                def ret_tile(h, t):
                    return ps[:, 4 + h % 2, P * t:P * t + P] if t < QT else ps[0:DEC, 1, 3 * P:4 * P]

                def group_stats(h):
                    dve.wait_ge(sv_done, NR * l + TT * (h + 1))
                    for t in range(TT):
                        last = nc.vector.bn_stats(bn[0:rows(t), t, :], ret_tile(h, t))
                    last.then_inc(bn_parts, 1)
                    wait_apart(dve, (bn_parts, HR * l + h + 1))
                    for t in range(TT):
                        last = nc.vector.bn_aggr(mv[0:rows(t), t, :], bn[0:rows(t), t, :])
                    last.then_inc(bn_done, 1)

                def group_normalise(h):
                    dve.wait_ge(gn_root, HR * l + h + 1)
                    nc.vector.reciprocal(gni[:, 0:QT], gnr[:, 0:QT])
                    nc.vector.reciprocal(gni[0:DEC, QT:TT], gnr[0:DEC, QT:TT]).then_inc(gn_inv, 1)
                    dve.wait_ge(gn_inv, HR * l + h + 1)
                    if h >= RING:
                        dve.wait_ge(or_ps, HR * l + h - 1)
                    for t in range(TT):
                        last = nc.vector.tensor_scalar(o_tok[0:rows(t), h % 2, t, :], ret_tile(h, t), mv[0:rows(t), t, 0:1],
                                                       gni[0:rows(t), t:t + 1], ALU.subtract, ALU.mult)
                    last.then_inc(gn_normed, 1)

                def gated(h):
                    dve.wait_ge(or_ps, HR * l + h + 1)
                    dve.wait_ge(st_ps, HR * l + min(h + 2, HR))
                    dve.wait_ge(g_silu, HR * l + h + 1)
                    g = gain[:, 2 * KD + 2 + h:2 * KD + 3 + h]
                    nc.vector.scalar_tensor_tensor(gate[:, h, 0:SEQ], ps[:, 0, :], g, gate[:, h, 0:SEQ], ALU.mult, ALU.mult)
                    nc.vector.scalar_tensor_tensor(gate[:, h, SEQ:TOK], ps[:, 1, 0:DEC], g, gate[:, h, SEQ:TOK],
                                                   ALU.mult, ALU.mult).then_inc(or_done, 1)

                def gated_lo(h):
                    dve.wait_ge(or_hi, HR * l + h + 1)
                    nc.vector.tensor_tensor(mix[:, 4 + h, 1, :], gate[:, h, :], mix[:, 4 + h, 0, :].bitcast(F32), ALU.subtract).then_inc(or_lo, 1)

                def states(h):
                    H = P // 2
                    dve.wait_ge(st_ps, HR * l + h + 1)
                    nc.vector.tensor_copy(st_tmp[:, 0, :], ps[:, 1, P:2 * P])
                    nc.vector.scalar_tensor_tensor(st_tmp[:, 1, :], s_in[:, h, :], float(gamma(h) ** DEC), ps[:, 1, 2 * P:3 * P],
                                                   ALU.mult, ALU.add).then_inc(st_sum, 1)
                    dve.wait_ge(st_sum, HR * l + h + 1)
                    if h >= RING:
                        dve.wait_ge(st_stored[h % RING], 32 * (HR // RING) * l + 32 * (h // RING))
                    for i in range(2):
                        c = C_ROT + 2 * i + 1
                        nc.vector.tensor_scalar(st_swap[0:H, i, :], st_tmp[H:P, i, :], cst[H:P, c:c + 1], None, ALU.mult)
                        last = nc.vector.tensor_scalar(st_swap[H:P, i, :], st_tmp[0:H, i, :], cst[0:H, c:c + 1], None, ALU.mult)
                    last.then_inc(st_swapped, 1)
                    dve.wait_ge(st_swapped, HR * l + h + 1)
                    for i in range(2):
                        c = C_ROT + 2 * i
                        last = nc.vector.scalar_tensor_tensor(st_out[:, h % RING, i, :], st_tmp[:, i, :], cst[:, c:c + 1],
                                                              st_swap[:, i, :], ALU.mult, ALU.add)
                    last.then_inc(st_done, 1)

                dve.wait_ge(state_loaded, 16 * l + 16)
                dve.wait_ge(pt_ps, NA * l + NA)
                for k in range(NR + 4):
                    h, i = k // TT, k % TT
                    if i == 0 and h >= 2:
                        gated(h - 2)
                    if i == 0 and 1 <= h <= HR:
                        states(h - 1)
                    if k in AT_R:
                        half_unit(FIRST_R + AT_R.index(k))
                    if i == 0 and h < HR:
                        query_decay(h)
                    if k < NR:
                        mask_scores(k)
                    if i == 1 and h == HR:
                        for p in range(HA // 2):
                            attn_lo(p)
                        for j in range(HR - 1):
                            gated_lo(j)
                        unit_lo(FIRST_OUT + 1)
                    if i == 2 and 1 <= h <= HR:
                        group_stats(h - 1)
                    if i == 3 and 1 <= h <= HR:
                        group_normalise(h - 1)
                gated(HR - 1)
                gated_lo(HR - 1)

                def add_to_x(n, s, c):
                    projected(n)
                    xc = x[:, bass.ds(c, 1), :].rearrange("p o (a b) -> p (o a) b", a=2)
                    nc.vector.tensor_tensor(xc, dense(s), xc, ALU.add).then_inc(evacuated, 1)

                for c in range(U_OUT):
                    add_to_x(U_LAYER * l + FIRST_OUT + c, c % 2 if c else 3, c)
                    if c + 1 < U_OUT:
                        unit_lo(FIRST_OUT + c + 2)
                    norm_lo(l, 1, ffn, c)
                    if c:
                        add_square(l, 1, ffn_sq, c)
                dve.wait_ge(h_lo, 2 * KD * l + 2 * KD)
                nc.vector.tensor_copy(gain[:], gains[:, bass.ds(l + 1, 1), :].rearrange("p a b -> p (a b)")).then_inc(gain_cur, 1)
                for g in range(GROUPS):
                    first = FIRST_FFN + U_GROUP * g

                    def group_lo(i, s, k=KD):
                        lo(s, U_LAYER * l + i + first, k)

                    def up_out(f):
                        scaled(U_LAYER * l + 2 * f + (first + 1), 1, work[:, 1, :])

                    def product(f):
                        dve.wait_ge(gate_silu, GROUPS * FT * l + f + (FT * g + 1))
                        dve.wait_ge(evacuated, U_LAYER * l + 2 * f + (first + 1 + EV + 1))
                        nc.vector.tensor_tensor(work[:, 2, :], work[:, 0, :], work[:, 1, :], ALU.mult).then_inc(act_f, 1)

                    def act_low(f):
                        dve.wait_ge(act_hi, GROUPS * FT * l + f + (FT * g + 1))
                        a = act[:, bass.ds(f, 1), :, :]
                        nc.vector.tensor_tensor(a[:, :, 1, :].rearrange("p a b -> p (a b)"), work[:, 2, :],
                                                a[:, :, 0, :].rearrange("p a b -> p (a b)").bitcast(F32), ALU.subtract).then_inc(act_lo, 1)

                    group_lo(1, 1)
                    if g == 0:
                        rms_invert(l, 1)
                        group_lo(2, 0)
                        rms_rows(l, 1)
                    scaled(U_LAYER * l + first, 0, work[:, 0, :])
                    if g:
                        group_lo(2, 0)
                    up_out(0)
                    product(0)
                    with dve.Fori(1, FT - 1) as f:
                        group_lo(2 * f + 1, 1)
                        scaled(U_LAYER * l + 2 * f + first, 0, work[:, 0, :])
                        act_low(f - 1)
                        group_lo(2 * f + 2, 0)
                        up_out(f)
                        product(f)
                    f = FT - 1
                    group_lo(2 * f + 1, 1)
                    scaled(U_LAYER * l + 2 * f + first, 0, work[:, 0, :])
                    act_low(f - 1)
                    group_lo(DOWN, 0, FT)
                    up_out(f)
                    product(f)
                    act_low(f)
                    with dve.Fori(0, (U_OUT - 2) // 2) as c2:
                        c = 2 * c2
                        for s in range(2):
                            group_lo(c + (DOWN + s + 1), 1 - s, FT)
                            add_to_x(U_LAYER * l + c + (first + DOWN + s), s, c + s)
                    group_lo(DOWN + U_OUT - 1, 1, FT)
                    add_to_x(U_LAYER * l + first + DOWN + U_OUT - 2, 0, U_OUT - 2)
                    if g + 1 < GROUPS:
                        group_lo(U_GROUP, 0)
                    add_to_x(U_LAYER * l + first + DOWN + U_OUT - 1, 1, U_OUT - 1)
            for t in range(TT):
                dve.wait_ge(y_ps, t + 1)
                nc.vector.tensor_copy(stage[0:rows(t), t, D // 2:D], ps[0:rows(t), 2 * (t % 2) + 1, :]).then_inc(y_copied[1], 1)

        @block.tensor
        def _(pe):
            PASSES = ((w_hi, 0), (w_hi, 1), (w_lo, 0))

            def passes(bank, slot, k, nk, src):
                for i, (w, part) in enumerate(PASSES):
                    for half in range(2):
                        last = nc.tensor.matmul(ps[:, bank + half, 0:HALF], w[:, slot, k, :],
                                                src[:, k, part, HALF * half:HALF * half + HALF],
                                                start=k == 0 and i == 0, stop=k == nk - 1 and i == 2)
                return last

            def unit(n, slot, nk, src, ready=None, bank=None, midway=None):
                pe.wait_ge(lo_done, n + RING + 1)
                if bank is None:
                    pe.wait_ge(evacuated, n + EV - 1)
                    bank = 2 * slot
                for k in range(nk):
                    if ready:
                        ready(k)
                    if midway and k == nk // 2:
                        midway()
                    last = passes(bank, slot, k, nk, src)
                last.then_inc(w_used, 1)

            def rms_sums(l, which, sq):
                pe.wait_ge(const_in, 32)
                pe.wait_ge(sq_sum, (KD - 1) * (2 * l + which + 1))
                for t in range(TT):
                    last = nc.tensor.matmul(ps[0:rows(t), 6, t:t + 1], sq[:, 0, tok(t)], cst[:, C_ONE:C_ONE + 1],
                                            start=True, stop=True)
                last.then_inc(rms_stat, 1)

            def rms_spread(l, which):
                pe.wait_ge(rms_inv, 2 * l + which + 1)
                for t in range(TT):
                    r = rows(t)
                    dst = ps[:, 7, tok(t)] if t < QT else ps[:, 6, P:P + DEC]
                    last = nc.tensor.transpose(dst, inv[0:r, t:t + 1].to_broadcast([r, P]), ident[0:r, 0:r])
                last.then_inc(rms_bcast, 1)

            def to_tokens(l, group, tiles, some=range(TT)):
                for t in some:
                    before = [u for u in range(t) if tok_bank(group, u) == tok_bank(group, t)]
                    if before:
                        wait_apart(pe, (tok_evac, 3 * TT * l + TT * group + before[-1] + 1))
                    for j in range(4):
                        last = nc.tensor.transpose(ps[0:rows(t), tok_bank(group, t), P * j:P * j + P], tiles[:, j, tok(t)], ident)
                    last.then_inc(tok_ps, 1)

            pe.sem_inc(w_used, RING)
            pe.wait_ge(ident_in, 16)
            for k in range(KD):
                b = 4 + 2 * (k % 2)
                if k == KD // 2:
                    pe.wait_ge(gains_in, 16 * 7)
                    n = DEPTH * GAINS
                    nc.tensor.transpose(ps[:, 0, 0:n], gain_rows, ident[0:n, 0:n]).then_inc(gains_ps, 1)
                if k % (KD // 2) == 0:
                    pe.wait_ge(x_in[k // (KD // 2)], 32)
                if k >= 2:
                    pe.wait_ge(evacuated, RING + k - 1)
                    pe.wait_ge(x_tail, k - 1)
                for t in range(TT):
                    r = rows(t)
                    dst = ps[:, b, tok(t)] if t < QT else ps[:, b + 1, 0:DEC]
                    last = nc.tensor.transpose(dst, stage[0:r, t, P * k:P * k + P], ident[0:r, 0:r])
                last.then_inc(x_ps, 1)
            pe.wait_ge(gains_set, 1)
            pe.wait_ge(evacuated, EV)
            pe.wait_ge(x_tail, KD)
            with pe.Fori(0, DEPTH) as l:
                def in_unit(n, slot, ready=None):
                    unit(U_LAYER * l + n, slot, KD, mix, ready)

                def mix_ready(k):
                    pe.wait_ge(h_lo, 2 * KD * l + k + 1)

                def in_units(a, b):
                    with pe.Fori(a // 2, b // 2) as n2:
                        n = 2 * n2
                        for s in range(2):
                            in_unit(n + s, s)

                in_unit(0, 0, mix_ready)
                in_unit(1, 1)
                rms_sums(l, 0, mix_sq)
                unit(U_LAYER * l + 2, 0, KD, mix, bank=4, midway=lambda: rms_spread(l, 0))
                in_unit(3, 1)
                in_units(4, 8)
                in_unit(8, 0)
                pe.wait_ge(qk_sq_lo, 8 * l + 8)
                for j in range(8):
                    sel = sel_r[:, 16 * j:16 * j + 16]
                    for i, part in enumerate((sq_hi, sq_lo)):
                        ends = dict(start=j + i == 0, stop=j + i == 8)
                        nc.tensor.matmul(ps[0:16, 6, :], sel, part[:, j, 0:SEQ], **ends)
                        last = nc.tensor.matmul(ps[0:16, 7, 0:DEC], sel, part[:, j, SEQ:TOK], **ends)
                last.then_inc(qk_stat, 1)
                in_unit(9, 1)
                in_units(10, 12)

                def half_unit(i):
                    n, half = FIRST_HALF + i // 2, i % 2
                    if half == 0:
                        pe.wait_ge(lo_done, U_LAYER * l + n + RING + 1)
                    if i < 2:
                        pe.wait_ge(evacuated, U_LAYER * l + n - 2 + EV + 1)
                    elif half == 0:
                        pe.wait_ge(half_out, UNITS_H * l + n - FIRST_HALF)
                    else:
                        pe.wait_ge(evacuated, U_LAYER * l + n - 1 + EV + 1)
                    for k in range(KD):
                        for j, (w, part) in enumerate(PASSES):
                            last = nc.tensor.matmul(ps[:, half_bank(i), 0:HALF], w[:, n % 2, k, :],
                                                    mix[:, k, part, HALF * half:HALF * half + HALF],
                                                    start=k == 0 and j == 0, stop=k == KD - 1 and j == 2)
                    last.then_inc(w_used if half else half_ps, 1)

                def spread_roots(i):
                    j, b = NORM_ORDER[i], 4 + 2 * (i % 2)
                    if i >= 2:
                        pe.wait_ge(qk_normed, 8 * l + i - 1)
                    for part in range(2):
                        ends = dict(start=part == 0, stop=part == 1)
                        w = spread_r[:, P * j:P * j + P]
                        nc.tensor.matmul(ps[:, b, :], w, qk_part[:, part, 0:SEQ], **ends)
                        last = nc.tensor.matmul(ps[:, b + 1, 0:DEC], w, qk_part[:, part, SEQ:TOK], **ends)
                    last.then_inc(qk_bcast, 1)

                for i in range(PRE):
                    half_unit(i)
                    if i == 0:
                        pe.wait_ge(evacuated, U_LAYER * l + 11 + EV + 1)
                        pe.wait_ge(qk_root, l + 1)
                        to_tokens(l, 0, vt)
                    elif i <= 4:
                        if i == 1:
                            pe.wait_ge(qk_lo, l + 1)
                            pe.wait_ge(tok_evac, 3 * TT * l + TT)
                        spread_roots(2 * i - 2)
                        spread_roots(2 * i - 1)
                pe.wait_ge(qk_normed, 8 * l + 8)
                to_tokens(l, 1, qk[:, 4:8, :])

                def cache_keys(p):
                    pe.wait_ge(kc_loaded, 16 * (HA // 2) * l + 16 * (p + 1))
                    if p:
                        pe.wait_ge(s_ps, NA * l + 2 * TT * p)
                        pe.wait_ge(o_normed, HA * l + 2 * p - 1)
                    else:
                        pe.wait_ge(tok_evac, 3 * TT * l + 2 * TT)
                    for t in range(QT):
                        last = nc.tensor.transpose(ps[:, 6, P * t:P * t + P], kc_tok[:, t, :], ident)
                    last.then_inc(kct_ps, 1)

                def scores(k):
                    h, t = ITEMS_A[k]
                    hr = head_rows(h)
                    q, keys = q_rev[hr, h // 2, tok(t)], qk[hr, 4 + h // 2, :]
                    waits = []
                    if t in (0, QT) and k:
                        waits.append((biased, NA * l + k))
                    elif k >= 2:
                        waits.append((biased, NA * l + k - 1))
                    if t == QT and h % 2 == 0:
                        waits.append((kct_evac, HA // 2 * l + h // 2 + 1))
                        if h:
                            waits.append((ot_out, HA // 2 * l + h // 2))
                    if t < QT:
                        for semaphore, count in waits:
                            pe.wait_ge(semaphore, count)
                        nc.tensor.matmul(ps[:, 2 + t % 2, 0:P * (t + 1)], q, keys[:, 0:P * (t + 1)],
                                         start=True, stop=True).then_inc(s_ps, 1)
                    else:
                        wait_apart(pe, *waits)
                        cached = kc_t[hr, :]
                        nc.tensor.matmul(ps[0:DEC, 2, 0:HALF], q, cached[:, 0:HALF], start=True, stop=True)
                        nc.tensor.matmul(ps[0:DEC, 3, 0:SEQ - HALF], q, cached[:, HALF:SEQ], start=True, stop=True)
                        nc.tensor.matmul(ps[0:DEC, 3, SEQ - HALF:HALF], q, keys[:, SEQ:TOK],
                                         start=True, stop=True).then_inc(s_ps, 1)

                def probs(k):
                    h, t = ITEMS_A[k]
                    waits = [(exped, NA * l + k + 1)]
                    if k >= 2:
                        waits.append(pt_out(l, k - 2))
                    wait_apart(pe, *waits)
                    b, src = 4 + k % 2, work[:, k % 3, :]
                    if t < QT:
                        for s in range(t + 1):
                            last = nc.tensor.transpose(ps[:, b, P * s:P * s + P], src[:, P * s:P * s + P], ident)
                    else:
                        idr = ident[0:DEC, 0:DEC]
                        for s in range(QT):
                            nc.tensor.transpose(ps[:, b, DEC * s:DEC * s + DEC], src[0:DEC, P * s:P * s + P], idr)
                        last = nc.tensor.transpose(ps[0:DEC, b, QT * DEC:TT * DEC], src[0:DEC, SEQ:TOK], idr)
                    last.then_inc(pt_ps, 1)

                def values(k):
                    h, t = ITEMS_A[k]
                    b, c, src = 6 + h % 2, DA * h, pt[:, k % 2, :]
                    pe.wait_ge(*pt_out(l, k))
                    if t == 0 and h >= 2:
                        pe.wait_ge(o_normed, HA * l + h - 1)
                    if t == 0 and h % 2 == 0:
                        pe.wait_ge(kct_evac, HA // 2 * l + h // 2 + 1)
                    if t == 0 and h % 2 and h > 1:
                        pe.wait_ge(ot_out, HA // 2 * l + h // 2)
                    if t < QT:
                        for s in range(t + 1):
                            last = nc.tensor.matmul(ps[:, b, DA * t:DA * t + DA], src[:, P * s:P * s + P], va[:, s, c:c + DA],
                                                    start=s == 0, stop=s == t)
                    else:
                        p = h // 2
                        pe.wait_ge(vc_loaded[p % RING], 16 * (HA // 2 // RING) * l + 16 * (p // RING + 1))
                        vc = vc_tok[:, p % RING, :, :]
                        out = ps[0:DEC, b, QT * DA:TT * DA]
                        for s in range(QT):
                            nc.tensor.matmul(out, src[:, DEC * s:DEC * s + DEC], vc[:, s, DA * (h % 2):DA * (h % 2) + DA],
                                             start=s == 0, stop=False)
                        last = nc.tensor.matmul(out, src[0:DEC, QT * DEC:TT * DEC], va[0:DEC, QT, c:c + DA],
                                                start=False, stop=True)
                    last.then_inc(pv_done, 1)

                def pair_out(p):
                    pe.wait_ge(o_normed, HA * l + 2 * p + 2)
                    pe.wait_ge(biased, NA * l + min(2 * TT * (p + 1) + QT - 1, NA))
                    for t in range(TT):
                        r = rows(t)
                        dst = ps[:, 7, tok(t)] if t < QT else ps[:, 2, 0:DEC]
                        last = nc.tensor.transpose(dst, o_tok[0:r, p % 2, t, :], ident[0:r, 0:r])
                    last.then_inc(ot_ps, 1)

                pe.wait_ge(evacuated, U_LAYER * l + FIRST_HALF + EV)
                for k in range(STEPS_A):
                    if k in AT_A:
                        half_unit(PRE + AT_A.index(k))
                    if k < NA:
                        scores(k)
                    if k % (2 * TT) == 1 and k < NA:
                        cache_keys(k // (2 * TT))
                    if 0 <= k - 2 < NA:
                        probs(k - 2)
                    if 0 <= k - 3 < NA:
                        values(k - 3)
                    if k < NA and head_before(k) in range(1, HA, 2):
                        pair_out(head_before(k) // 2)
                pe.wait_ge(evacuated, U_LAYER * l + U_IN - HR + EV)
                pe.wait_ge(*pt_out(l, NA - 1))
                pe.wait_ge(o_normed, HA * l + HA - 1)
                to_tokens(l, 2, vt, range(3))
                pair_out(HA // 2 - 1)

                def ret_keys(h):
                    if h >= 2:
                        pe.wait_ge(or_done, HR * l + h - 1)
                    if h:
                        pe.wait_ge(st_sum, HR * l + h)
                    for t in range(TT):
                        dst = ps[:, 0, tok(t)] if t < QT else ps[0:DEC, 1, 0:P]
                        last = nc.tensor.transpose(dst, qk_ret[:, 4 + h, tok(t)], ident)
                    last.then_inc(kd_ps, 1)

                def ret_scores(k):
                    h, t = ITEMS_R[k]
                    if k >= 2:
                        wait_apart(pe, (decayed, NR * l + k - 1))
                    if t < QT:
                        for s in range(t + 1):
                            last = nc.tensor.matmul(ps[:, 2 + k % 2, P * s:P * s + P], qk_ret[:, 4 + h, tok(s)],
                                                    qk_ret[:, h, tok(t)], start=True, stop=True)
                    else:
                        last = nc.tensor.matmul(ps[0:DEC, 2 + k % 2, 0:DEC], qk_ret[:, 4 + h, tok(t)],
                                                qk_ret[:, h, tok(t)], start=True, stop=True)
                    last.then_inc(r_ps, 1)

                def ret_values(k):
                    h, t = ITEMS_R[k]
                    pe.wait_ge(decayed, NR * l + k + 1)
                    if t == 0 and h >= 2:
                        pe.wait_ge(gn_normed, HR * l + h - 1)
                    v = vr[:, :, DR * h:DR * h + DR]
                    if t < QT:
                        for s in range(t + 1):
                            last = nc.tensor.matmul(ps[:, 4 + h % 2, P * t:P * t + P], work[:, k % 3, P * s:P * s + P], v[:, s, :],
                                                    start=s == 0, stop=s == t)
                    else:
                        pe.wait_ge(qd_ready, HR * l + h + 1)
                        if h + 1 < HR:
                            pe.wait_ge(kd_evac, HR * l + h + 2)
                        else:
                            pe.wait_ge(or_done, HR * l + h)
                            pe.wait_ge(st_sum, HR * l + h + 1)
                        out = ps[0:DEC, 1, 3 * P:4 * P]
                        nc.tensor.matmul(out, qd[:, h % RING, :], s_in[:, h, :], start=True, stop=False)
                        last = nc.tensor.matmul(out, work[0:DEC, k % 3, 0:DEC], v[0:DEC, QT, :],
                                                start=False, stop=True)
                    last.then_inc(sv_done, 1)

                def ret_states(h):
                    pe.wait_ge(kd_evac, HR * l + h + 1)
                    if h:
                        pe.wait_ge(gn_normed, HR * l + h)
                    v = vr[:, :, DR * h:DR * h + DR]
                    for t in range(QT):
                        nc.tensor.matmul(ps[:, 1, P:2 * P], kd_tok[:, h % 2, t, :], v[:, t, :], start=t == 0, stop=t == QT - 1)
                    nc.tensor.matmul(ps[:, 1, 2 * P:3 * P], kd_tok[0:DEC, h % 2, QT, :], v[0:DEC, QT, :],
                                     start=True, stop=True).then_inc(st_ps, 1)

                def ret_out(h):
                    pe.wait_ge(gn_normed, HR * l + h + 1)
                    pe.wait_ge(st_sum, HR * l + h + 1)
                    for t in range(TT):
                        r = rows(t)
                        dst = ps[:, 0, tok(t)] if t < QT else ps[:, 1, 0:DEC]
                        last = nc.tensor.transpose(dst, o_tok[0:r, h % 2, t, :], ident[0:r, 0:r])
                    last.then_inc(or_ps, 1)

                pe.wait_ge(ret_ready, 16 * l + 16)
                pe.wait_ge(state_loaded, 16 * l + 16)
                ret_keys(0)
                to_tokens(l, 2, vt, range(3, TT))
                pe.wait_ge(ot_out, HA // 2 * l + HA // 2)
                for k in range(NR + 2):
                    h, i = k // TT, k % TT
                    if k in AT_R:
                        half_unit(FIRST_R + AT_R.index(k))
                    if i == 0 and 1 <= h < HR:
                        ret_keys(h)
                    if k < NR:
                        ret_scores(k)
                    if k == 2:
                        pe.wait_ge(tok_evac, 3 * TT * l + 3 * TT)
                    if 0 <= k - 2 < NR:
                        ret_values(k - 2)
                    if i == TT - 1 and h >= 1:
                        ret_out(h - 1)
                    if i == TT - 1 and h < HR:
                        ret_states(h)

                def mixed(k):
                    if k < 4:
                        pe.wait_ge(ot_lo, HA // 2 * l + k + 1)
                    else:
                        pe.wait_ge(or_lo, HR * l + k - 3)

                pe.wait_ge(evacuated, U_LAYER * l + U_IN + EV)
                pe.wait_ge(lo_done, U_LAYER * l + FIRST_OUT + RING + 1)
                for k in range(KD - 1):
                    mixed(k)
                    passes(6, 0, k, KD, mix)
                pe.wait_ge(lo_done, U_LAYER * l + FIRST_OUT + RING + 2)
                pe.wait_ge(decayed, NR * l + NR)
                for k in range(KD - 2):
                    if k == 3:
                        ret_out(HR - 1)
                    passes(2, 1, k, KD, mix)
                mixed(KD - 1)
                passes(6, 0, KD - 1, KD, mix).then_inc(w_used, 1)
                for k in range(KD - 2, KD):
                    last = passes(2, 1, k, KD, mix)
                last.then_inc(w_used, 1)
                wait_apart(pe, (or_done, HR * l + HR))
                with pe.Fori(1, U_OUT // 2) as c2:
                    c = 2 * c2
                    for s in range(2):
                        unit(U_LAYER * l + c + (FIRST_OUT + s), s, KD, mix)

                def ffn_ready(k):
                    pe.wait_ge(h_lo, 2 * KD * l + KD + k + 1)

                for g in range(GROUPS):
                    first = FIRST_FFN + U_GROUP * g
                    if g == 0:
                        unit(U_LAYER * l + first, 0, KD, ffn, ffn_ready)
                        rms_sums(l, 1, ffn_sq)
                        unit(U_LAYER * l + first + 1, 1, KD, ffn, midway=lambda: rms_spread(l, 1))
                    with pe.Fori(1 if g == 0 else 0, FT) as f:
                        for s in range(2):
                            unit(U_LAYER * l + 2 * f + (first + s), s, KD, ffn)

                    def act_ready(k):
                        pe.wait_ge(act_lo, GROUPS * FT * l + FT * g + k + 1)

                    unit(U_LAYER * l + first + DOWN, 0, FT, act, act_ready)
                    unit(U_LAYER * l + first + DOWN + 1, 1, FT, act)
                    with pe.Fori(1, U_OUT // 2) as c2:
                        c = 2 * c2
                        for s in range(2):
                            unit(U_LAYER * l + c + (first + DOWN + s), s, FT, act)
            pe.wait_ge(evacuated, DEPTH * U_LAYER + EV)
            for t in range(TT):
                if t >= 2:
                    for copied in y_copied:
                        pe.wait_ge(copied, t - 1)
                for k in range(KD):
                    b = 2 * (t % 2) + k // 4
                    last = nc.tensor.transpose(ps[0:rows(t), b, P * (k % 4):P * (k % 4) + P], x[:, k, tok(t)], ident)
                last.then_inc(y_ps, 1)


OUTPUTS = [
    ("y_prompt", (1, SEQ, D)), ("y_sample", (1, DEC, D)),
    ("nk_prompt", (DEPTH, 1, SEQ, HA, DA)), ("nv_prompt", (DEPTH, 1, SEQ, HA, DA)), ("ns_prompt", (DEPTH, 1, HR, DR, DR)),
    ("nk_sample", (DEPTH, 1, DEC, HA, DA)), ("nv_sample", (DEPTH, 1, DEC, HA, DA)), ("ns_sample", (DEPTH, 1, HR, DR, DR)),
]


def tables():
    import numpy as np

    half = DR // 2
    inv = (np.float32(10000.0) ** (-np.arange(half, dtype=np.float32) / np.float32(half))).astype(np.float32)

    def angles(pos):
        return (inv[:, None] * np.asarray(pos, np.float32)[None, :]).astype(np.float32).astype(np.float64)

    c = np.zeros((P, C_ALL))
    c[:, C_ID:C_ID + P] = np.eye(P)
    a = angles(np.arange(SEQ))
    c[:, C_COS:C_COS + SEQ] = np.concatenate([np.cos(a)] * 2)
    c[:, C_SIN:C_SIN + SEQ] = np.concatenate([np.sin(a), -np.sin(a)])
    scale = DR ** -0.5
    decay = np.zeros((HR, P, SEQ))
    for h in range(HR):
        lg = np.log(gamma(h))
        c[:, C_QDEC + DEC * h:C_QDEC + DEC * h + DEC] = np.exp((np.arange(DEC) + 1.0) * lg)
        for t in range(QT):
            c[:, C_KDEC + HR * t + h] = scale * np.exp((SEQ - 1.0 - P * t - np.arange(P)) * lg)
        c[0:DEC, C_KDEC + HR * QT + h] = scale * np.exp((DEC - 1.0 - np.arange(DEC)) * lg)
        for b in range(QT):
            diff = P * (QT - 1 - b) + np.arange(P)[None, :] - np.arange(P)[:, None]
            decay[h, :, P * b:P * b + P] = np.where(diff >= 0, scale * np.exp(np.maximum(diff, 0) * lg), 0.0)
    for i, pos in enumerate((-SEQ, -DEC)):
        a = angles([pos])[:, 0]
        c[:, C_ROT + 2 * i] = np.concatenate([np.cos(a)] * 2)
        c[:, C_ROT + 2 * i + 1] = np.concatenate([np.sin(a), -np.sin(a)])
    for j in range(2 * WA // P):
        c[0:DA, C_SEL + 18 * j] = 1.0
        c[DA:P, C_SEL + 18 * j + 1] = 1.0
    c[:, C_ONE] = 1.0
    c[:, C_EPS] = RMS_EPS
    c[:, C_EPS + 1] = GN_EPS
    return c.astype(np.float32), np.repeat(np.eye(16, dtype=np.float32), DA, axis=1), decay.astype(np.float32)


def kernel(x_prompt, x_sample, cache_a_k, cache_a_v, state_ret, norm_mix, w_in, q_norm, k_norm, rel_table,
           ret_norm, w_out, norm_ffn, w_gate, w_up, w_down):
    import numpy as np
    import concourse.bacc as bacc
    from concourse.bass_utils import run_bass_kernel_spmd

    nc = bacc.Bacc("TRN2", target_bir_lowering=False, num_devices=1)
    const, spread, decay = tables()
    arrays = dict(x_prompt=x_prompt, x_sample=x_sample, cache_k=cache_a_k, cache_v=cache_a_v, state_in=state_ret,
                  norm_mix=norm_mix, w_in=w_in, q_norm=q_norm, k_norm=k_norm, rel_table=rel_table, ret_norm=ret_norm,
                  w_out=w_out, norm_ffn=norm_ffn, w_gate=w_gate, w_up=w_up, w_down=w_down, const=const, spread=spread, decay=decay)
    arrays = {f"in_{name}": np.ascontiguousarray(a) for name, a in arrays.items()}
    aps = [nc.dram_tensor(name, a.shape, mybir.dt.from_np(a.dtype), kind="ExternalInput").ap() for name, a in arrays.items()]
    aps += [nc.dram_tensor(f"out_{name}", shape, F32, kind="ExternalOutput").ap() for name, shape in OUTPUTS]
    lines = nc.dram_tensor("bias_lines", (DEPTH * HA, 6 * P), F32, kind="Internal").ap()
    build(nc, *aps, lines)
    r = run_bass_kernel_spmd(nc, [arrays], core_ids=[0])
    return tuple(r.results[0][f"out_{name}"] for name, _ in OUTPUTS)
```
